# Optimizing a Trainium2 kernel written in Bass

```python
import math
import jax
import jax.numpy as jnp
from jax import lax
import numpy as np
import jax, jax.numpy as jnp

D_MODEL = 1024
BATCH = 1
SEQ = 256
DEPTH = 2

HEAD_DIM = 64
ATTN_SCALE = HEAD_DIM ** -0.5
SWA_HEADS = D_MODEL // 128
SWA_KV_HEADS = SWA_HEADS // 4
SWA_GROUP = SWA_HEADS // SWA_KV_HEADS
SWA_WINDOW = 128
SWA_BLOCK = 128
SC_WIDTH = D_MODEL // 2
SC_KSIZE = 3
MOBA_HEADS = D_MODEL // 128
MOBA_BLOCK = 256
MOBA_TOPK = 3
MOBA_QCHUNK = 32
N_ALIBI_HEADS = SWA_HEADS + MOBA_HEADS
FFN_HIDDEN = -(-8 * D_MODEL // (3 * 256)) * 256
ALPHA = (2 * DEPTH) ** 0.25
BETA = (8 * DEPTH) ** -0.25
LN_EPS = 1e-5

A_Q = SWA_HEADS * HEAD_DIM
A_KV = SWA_KV_HEADS * HEAD_DIM
C_QKV = MOBA_HEADS * HEAD_DIM
PROJ_SIZES = (A_Q, A_KV, A_KV,
              SC_WIDTH, SC_WIDTH, SC_WIDTH,
              C_QKV, C_QKV, C_QKV,
              D_MODEL, D_MODEL, D_MODEL)
PROJ_SPLITS = tuple(int(s) for s in np.cumsum(PROJ_SIZES)[:-1])
PROJ_WIDTH = int(sum(PROJ_SIZES))


def alibi_slopes():
    i = jnp.arange(N_ALIBI_HEADS, dtype=jnp.float32)
    s = jnp.exp2(-8.0 * (i + 1.0) / N_ALIBI_HEADS)
    return s[:SWA_HEADS], s[SWA_HEADS:]

def layer_norm(x, g, b):
    xf = x.astype(jnp.float32)
    mu = jnp.mean(xf, axis=-1, keepdims=True)
    var = jnp.mean(jnp.square(xf - mu), axis=-1, keepdims=True)
    y = (xf - mu) * lax.rsqrt(var + LN_EPS) * g.astype(jnp.float32) + b.astype(jnp.float32)
    return y.astype(x.dtype)

def sliding_window_attention(q, k, v, sinks, slopes):
    B, S = q.shape[0], q.shape[1]
    nb = S // SWA_BLOCK
    qb = q.reshape(B, nb, SWA_BLOCK, SWA_KV_HEADS, SWA_GROUP, HEAD_DIM).astype(jnp.float32)
    kb = k.reshape(B, nb, SWA_BLOCK, SWA_KV_HEADS, HEAD_DIM)
    vb = v.reshape(B, nb, SWA_BLOCK, SWA_KV_HEADS, HEAD_DIM)
    shift = ((0, 0), (1, 0), (0, 0), (0, 0), (0, 0))
    kw = jnp.concatenate([jnp.pad(kb, shift)[:, :-1], kb], axis=2)
    vw = jnp.concatenate([jnp.pad(vb, shift)[:, :-1], vb], axis=2)
    logits = jnp.einsum('bnqhgd,bnkhd->bnhgqk', qb, kw.astype(jnp.float32)) * ATTN_SCALE
    blk = jnp.arange(nb)[:, None] * SWA_BLOCK
    qpos = blk + jnp.arange(SWA_BLOCK)[None, :]
    kpos = blk - SWA_BLOCK + jnp.arange(2 * SWA_BLOCK)[None, :]
    dist = qpos[:, :, None] - kpos[:, None, :]
    allowed = (dist >= 0) & (dist < SWA_WINDOW) & (kpos[:, None, :] >= 0)
    sl = slopes.reshape(SWA_KV_HEADS, SWA_GROUP)[:, :, None, None]
    logits = logits - sl * dist[:, None, None].astype(jnp.float32)
    logits = jnp.where(allowed[:, None, None], logits, -jnp.inf)
    sink = sinks.astype(jnp.float32).reshape(SWA_KV_HEADS, SWA_GROUP)[:, :, None, None]
    m = jnp.maximum(jnp.max(logits, axis=-1, keepdims=True), sink)
    p = jnp.exp(logits - m)
    denom = jnp.sum(p, axis=-1, keepdims=True) + jnp.exp(sink - m)
    out = jnp.einsum('bnhgqk,bnkhd->bnqhgd', p / denom, vw.astype(jnp.float32))
    return out.reshape(B, S, SWA_HEADS * HEAD_DIM).astype(q.dtype)

def gated_short_conv(h, gate_b, gate_c, conv_w):
    u = gate_c * h
    up = jnp.pad(u, ((0, 0), (SC_KSIZE - 1, 0), (0, 0)))
    S = h.shape[1]
    conv = up[:, 0:S] * conv_w[0] + up[:, 1:S + 1] * conv_w[1] + up[:, 2:S + 2] * conv_w[2]
    return gate_b * conv

def moba_attention(q, k, v, slopes):
    B, S = q.shape[0], q.shape[1]
    sp = -(-S // MOBA_BLOCK) * MOBA_BLOCK
    pad = ((0, 0), (0, sp - S), (0, 0), (0, 0))
    q, k, v = [jnp.pad(t, pad).transpose(0, 2, 1, 3) for t in (q, k, v)]
    nblk = sp // MOBA_BLOCK
    top = min(MOBA_TOPK, nblk)
    kbl = k.reshape(B, MOBA_HEADS, nblk, MOBA_BLOCK, HEAD_DIM)
    vbl = v.reshape(B, MOBA_HEADS, nblk, MOBA_BLOCK, HEAD_DIM)
    kmean = jnp.mean(kbl.astype(jnp.float32), axis=3)
    gate = jnp.einsum('bhsd,bhnd->bhsn', q.astype(jnp.float32), kmean)
    cur = jnp.arange(sp) // MOBA_BLOCK
    past = jnp.arange(nblk)[None, :] < cur[:, None]
    gate = jnp.where(past, gate, -jnp.inf)
    _, idx = lax.top_k(gate, top)
    nch = sp // MOBA_QCHUNK
    q_ch = q.reshape(B, MOBA_HEADS, nch, MOBA_QCHUNK, HEAD_DIM).transpose(2, 0, 1, 3, 4)
    idx_ch = idx.reshape(B, MOBA_HEADS, nch, MOBA_QCHUNK, top).transpose(2, 0, 1, 3, 4)
    bi = jnp.arange(B)[:, None, None, None]
    hi = jnp.arange(MOBA_HEADS)[None, :, None, None]
    sl4 = slopes[None, :, None, None]
    sl5 = slopes[None, :, None, None, None]
    koff = jnp.arange(MOBA_BLOCK)

    def chunk(args):
        c, qc, ic = args
        qpos = c * MOBA_QCHUNK + jnp.arange(MOBA_QCHUNK)
        own = (c * MOBA_QCHUNK) // MOBA_BLOCK
        qf = qc.astype(jnp.float32)
        kg = kbl[bi, hi, ic].astype(jnp.float32)
        vg = vbl[bi, hi, ic].astype(jnp.float32)
        ls = jnp.einsum('bhqd,bhqjkd->bhqjk', qf, kg) * ATTN_SCALE
        kpos_sel = ic[..., None] * MOBA_BLOCK + koff
        dist_sel = (qpos[None, None, :, None, None] - kpos_sel).astype(jnp.float32)
        valid = jnp.arange(top)[None, :] < (qpos // MOBA_BLOCK)[:, None]
        ls = jnp.where(valid[None, None, :, :, None], ls - sl5 * dist_sel, -jnp.inf)
        kown = lax.dynamic_index_in_dim(kbl, own, axis=2, keepdims=False).astype(jnp.float32)
        vown = lax.dynamic_index_in_dim(vbl, own, axis=2, keepdims=False).astype(jnp.float32)
        lo = jnp.einsum('bhqd,bhkd->bhqk', qf, kown) * ATTN_SCALE
        dist_own = qpos[:, None] - (own * MOBA_BLOCK + koff)[None, :]
        lo = jnp.where(dist_own >= 0, lo - sl4 * dist_own.astype(jnp.float32), -jnp.inf)
        logits = jnp.concatenate([ls.reshape(B, MOBA_HEADS, MOBA_QCHUNK, top * MOBA_BLOCK), lo], axis=-1)
        p = jax.nn.softmax(logits, axis=-1)
        ps = p[..., :top * MOBA_BLOCK].reshape(B, MOBA_HEADS, MOBA_QCHUNK, top, MOBA_BLOCK)
        po = p[..., top * MOBA_BLOCK:]
        return (jnp.einsum('bhqjk,bhqjkd->bhqd', ps, vg)
                + jnp.einsum('bhqk,bhkd->bhqd', po, vown))

    out = lax.map(chunk, (jnp.arange(nch), q_ch, idx_ch))
    out = out.transpose(1, 0, 3, 2, 4).reshape(B, sp, MOBA_HEADS * HEAD_DIM)[:, :S]
    return out.astype(q.dtype)

def hybrid_mixer(x, w_in, sinks, conv_w, w_br_a, w_br_b, w_br_c, w_out):
    B, S = x.shape[0], x.shape[1]
    proj = jnp.einsum('bsd,de->bse', x, w_in)
    a_q, a_k, a_v, b_h, b_b, b_c, c_q, c_k, c_v, g_a, g_b, g_c = jnp.split(proj, PROJ_SPLITS, axis=-1)
    slopes_a, slopes_c = alibi_slopes()
    y_a = sliding_window_attention(
        a_q.reshape(B, S, SWA_HEADS, HEAD_DIM),
        a_k.reshape(B, S, SWA_KV_HEADS, HEAD_DIM),
        a_v.reshape(B, S, SWA_KV_HEADS, HEAD_DIM), sinks, slopes_a)
    y_b = gated_short_conv(b_h, b_b, b_c, conv_w)
    y_c = moba_attention(
        c_q.reshape(B, S, MOBA_HEADS, HEAD_DIM),
        c_k.reshape(B, S, MOBA_HEADS, HEAD_DIM),
        c_v.reshape(B, S, MOBA_HEADS, HEAD_DIM), slopes_c)
    merged = (jax.nn.sigmoid(g_a) * (y_a @ w_br_a)
              + jax.nn.sigmoid(g_b) * (y_b @ w_br_b)
              + jax.nn.sigmoid(g_c) * (y_c @ w_br_c))
    return merged @ w_out

def swiglu(x, w_gate, w_up, w_down):
    return (jax.nn.silu(x @ w_gate) * (x @ w_up)) @ w_down

def first_inputs(seed: int = 0) -> dict:
    key = jax.random.key(seed)
    ks = jax.random.split(key, 16)
    f32 = jnp.float32
    nrm = lambda k, shape, s: jax.random.normal(k, shape, f32) * s
    L = DEPTH
    br_in = SWA_HEADS * HEAD_DIM
    return {
        'x': jax.random.normal(ks[0], (BATCH, SEQ, D_MODEL), f32),
        'w_in': nrm(ks[1], (L, D_MODEL, PROJ_WIDTH), D_MODEL ** -0.5),
        'attn_sinks': nrm(ks[2], (L, SWA_HEADS), 0.5),
        'conv_w': nrm(ks[3], (L, SC_KSIZE, SC_WIDTH), SC_KSIZE ** -0.5),
        'w_branch_a': nrm(ks[4], (L, br_in, D_MODEL), br_in ** -0.5 * BETA),
        'w_branch_b': nrm(ks[5], (L, SC_WIDTH, D_MODEL), SC_WIDTH ** -0.5 * BETA),
        'w_branch_c': nrm(ks[6], (L, MOBA_HEADS * HEAD_DIM, D_MODEL), (MOBA_HEADS * HEAD_DIM) ** -0.5 * BETA),
        'w_out': nrm(ks[7], (L, D_MODEL, D_MODEL), D_MODEL ** -0.5 * BETA),
        'ln1_g': 1.0 + nrm(ks[8], (L, D_MODEL), 0.02),
        'ln1_b': nrm(ks[9], (L, D_MODEL), 0.02),
        'w_ffn_gate': nrm(ks[10], (L, D_MODEL, FFN_HIDDEN), D_MODEL ** -0.5 * BETA),
        'w_ffn_up': nrm(ks[11], (L, D_MODEL, FFN_HIDDEN), D_MODEL ** -0.5 * BETA),
        'w_ffn_down': nrm(ks[12], (L, FFN_HIDDEN, D_MODEL), FFN_HIDDEN ** -0.5 * BETA),
        'ln2_g': 1.0 + nrm(ks[13], (L, D_MODEL), 0.02),
        'ln2_b': nrm(ks[14], (L, D_MODEL), 0.02),
    }

def first_block(x, w_in, attn_sinks, conv_w, w_branch_a, w_branch_b, w_branch_c, w_out,
              ln1_g, ln1_b, w_ffn_gate, w_ffn_up, w_ffn_down, ln2_g, ln2_b):
    for l in range(DEPTH):
        mix = hybrid_mixer(x, w_in[l], attn_sinks[l], conv_w[l], w_branch_a[l],
                           w_branch_b[l], w_branch_c[l], w_out[l])
        x = layer_norm(ALPHA * x + mix, ln1_g[l], ln1_b[l])
        ffn = swiglu(x, w_ffn_gate[l], w_ffn_up[l], w_ffn_down[l])
        x = layer_norm(ALPHA * x + ffn, ln2_g[l], ln2_b[l])
    return x


CTX_LEN = 256
GRID_W = 64
EPS = 1e-6
HALF = 0.5
D_FF = 2816
N_ADA = 9
CONV_CH = 384
CONV_K = 31
N_HEADS = 8
Q_LORA = 384
KV_LORA = 256
QK_NOPE = 64
QK_ROPE = 32
V_DIM = 64
ROPE_AXIS = QK_ROPE // 2
ROPE_BASE = 10000.0
ATTN_SCALE_2 = (QK_NOPE + QK_ROPE) ** -0.5
Q_BLOCK = 128
FOURIER_GROUPS = 4
FOURIER_GROUP_CH = 128
FOURIER_WIDTH = FOURIER_GROUPS * FOURIER_GROUP_CH
MIX_WIDTH = 2 * CONV_CH + Q_LORA + KV_LORA + QK_ROPE + FOURIER_WIDTH
N_BRANCH = 3


def rms_norm(x, g):
    xf = x.astype(jnp.float32)
    y = xf * lax.rsqrt(jnp.mean(xf * xf, axis=-1, keepdims=True) + EPS)
    return (y * g.astype(jnp.float32)).astype(x.dtype)

def layer_norm_2(x, g, b):
    xf = x.astype(jnp.float32)
    mu = jnp.mean(xf, axis=-1, keepdims=True)
    var = jnp.mean(jnp.square(xf - mu), axis=-1, keepdims=True)
    y = (xf - mu) * lax.rsqrt(var + EPS)
    return (y * g.astype(jnp.float32) + b.astype(jnp.float32)).astype(x.dtype)

def ada_norm(h, g, shift, scale):
    return rms_norm(h, g) * (1 + scale) + shift

def swiglu_2(x, w1, w3, w2):
    return (jax.nn.silu(x @ w1) * (x @ w3)) @ w2

def axial_rope_tables(n_tok, dtype):
    rows = n_tok // GRID_W
    row = jnp.broadcast_to(jnp.arange(rows, dtype=jnp.float32)[:, None], (rows, GRID_W)).reshape(-1)
    col = jnp.broadcast_to(jnp.arange(GRID_W, dtype=jnp.float32)[None, :], (rows, GRID_W)).reshape(-1)
    inv = 1.0 / (ROPE_BASE ** (jnp.arange(ROPE_AXIS // 2, dtype=jnp.float32) * 2.0 / ROPE_AXIS))
    ar = row[:, None] * inv
    ac = col[:, None] * inv
    ang = jnp.concatenate([ar, ar, ac, ac], axis=-1)
    return jnp.cos(ang).astype(dtype), jnp.sin(ang).astype(dtype)

def rotate_half_axial(x):
    xr = x.reshape(x.shape[:-1] + (2, 2, ROPE_AXIS // 2))
    xr = jnp.concatenate([-xr[..., 1:2, :], xr[..., 0:1, :]], axis=-2)
    return xr.reshape(x.shape)

def apply_rope(x, cos, sin):
    return x * cos + rotate_half_axial(x) * sin

def split_mixing(z):
    o1 = 2 * CONV_CH
    o2 = o1 + Q_LORA
    o3 = o2 + KV_LORA
    o4 = o3 + QK_ROPE
    return z[..., :o1], z[..., o1:o2], z[..., o2:o3], z[..., o3:o4], z[..., o4:]

def conv_module(zc, w_dw, b_dw, ln_g, ln_b, w_pw, b_pw):
    a, gt = jnp.split(zc, 2, axis=-1)
    v = a * jax.nn.sigmoid(gt)
    v = lax.conv_general_dilated(v, w_dw[:, None, :].astype(v.dtype), window_strides=(1,),
                                 padding=[(CONV_K // 2, CONV_K // 2)],
                                 dimension_numbers=('NWC', 'WIO', 'NWC'),
                                 feature_group_count=CONV_CH) + b_dw
    v = layer_norm_2(v, ln_g, ln_b)
    return jax.nn.silu(v) @ w_pw + b_pw

def fourier_mix(zf, w, b):
    bsz, t, _ = zf.shape
    g = zf.reshape(bsz, t, FOURIER_GROUPS, FOURIER_GROUP_CH).astype(jnp.float32)
    f = jnp.fft.fftn(g, axes=(1, 3), norm='ortho').real.astype(zf.dtype)
    return f.reshape(bsz, t, FOURIER_WIDTH) @ w + b

def mla_q(cq, g_qn, w_uq, cos, sin):
    bsz, t, _ = cq.shape
    q = (rms_norm(cq, g_qn) @ w_uq).reshape(bsz, t, N_HEADS, QK_NOPE + QK_ROPE)
    if cos is None:
        return q
    q_nope, q_rope = q[..., :QK_NOPE], q[..., QK_NOPE:]
    return jnp.concatenate([q_nope, apply_rope(q_rope, cos[:, None, :], sin[:, None, :])], axis=-1)

def mla_kv(ckv, kr, g_kvn, w_ukv, cos, sin):
    bsz, t, _ = ckv.shape
    kv = (rms_norm(ckv, g_kvn) @ w_ukv).reshape(bsz, t, N_HEADS, QK_NOPE + V_DIM)
    k_nope, v = kv[..., :QK_NOPE], kv[..., QK_NOPE:]
    if cos is not None:
        kr = apply_rope(kr, cos, sin)
    k = jnp.concatenate([k_nope, jnp.broadcast_to(kr[:, :, None, :], (bsz, t, N_HEADS, QK_ROPE))], axis=-1)
    return k, v

def attend_dense(q, k, v):
    s = jnp.einsum('bqhd,bkhd->bhqk', q, k, preferred_element_type=jnp.float32) * ATTN_SCALE_2
    p = jax.nn.softmax(s, axis=-1).astype(v.dtype)
    o = jnp.einsum('bhqk,bkhd->bqhd', p, v)
    return o.reshape(o.shape[0], o.shape[1], N_HEADS * V_DIM)

def attend_blocked(q, k, v):
    bsz, s, _, dk = q.shape
    nb = s // Q_BLOCK
    qb = q.reshape(bsz, nb, Q_BLOCK, N_HEADS, dk).transpose(1, 0, 2, 3, 4)
    o = lax.map(lambda blk: attend_dense(blk, k, v), qb)
    return o.transpose(1, 0, 2, 3).reshape(bsz, s, N_HEADS * V_DIM)

def merge_branches(u, y_conv, y_mla, y_four, w_bg, b_bg, w_out):
    g = jax.nn.sigmoid(u @ w_bg + b_bg)
    g0, g1, g2 = jnp.split(g, N_BRANCH, axis=-1)
    return (g0 * y_conv + g1 * y_mla + g2 * y_four) @ w_out

def second_inputs(seed: int = 0) -> dict:
    key = jax.random.key(seed)
    ks = jax.random.split(key, 40)
    L, D = DEPTH, D_MODEL

    def nrm(k, shape, std):
        return jax.random.normal(k, shape, jnp.float32) * std

    def gain(k, shape):
        return 1.0 + nrm(k, shape, 0.02)

    return {
        'x': nrm(ks[0], (BATCH, SEQ, D), 1.0),
        'c': nrm(ks[1], (BATCH, D), 1.0),
        'ctx': nrm(ks[2], (BATCH, CTX_LEN, D), 1.0),
        'c_ctx': nrm(ks[3], (D,), 1.0),
        'w_ada': nrm(ks[4], (L, D, N_ADA * D), 0.5 * D ** -0.5),
        'b_ada': nrm(ks[5], (L, N_ADA * D), 0.02),
        'g_ffn1': gain(ks[6], (L, D)),
        'w1_ffn1': nrm(ks[7], (L, D, D_FF), D ** -0.5),
        'w3_ffn1': nrm(ks[8], (L, D, D_FF), D ** -0.5),
        'w2_ffn1': nrm(ks[9], (L, D_FF, D), D_FF ** -0.5),
        'g_mix': gain(ks[10], (L, D)),
        'w_in': nrm(ks[11], (L, D, MIX_WIDTH), D ** -0.5),
        'w_dw': nrm(ks[12], (L, CONV_K, CONV_CH), CONV_K ** -0.5),
        'b_dw': nrm(ks[13], (L, CONV_CH), 0.02),
        'ln_g_conv': gain(ks[14], (L, CONV_CH)),
        'ln_b_conv': nrm(ks[15], (L, CONV_CH), 0.02),
        'w_pw_conv': nrm(ks[16], (L, CONV_CH, D), CONV_CH ** -0.5),
        'b_pw_conv': nrm(ks[17], (L, D), 0.02),
        'g_qnorm': gain(ks[18], (L, Q_LORA)),
        'w_uq': nrm(ks[19], (L, Q_LORA, N_HEADS * (QK_NOPE + QK_ROPE)), Q_LORA ** -0.5),
        'g_kvnorm': gain(ks[20], (L, KV_LORA)),
        'w_ukv': nrm(ks[21], (L, KV_LORA, N_HEADS * (QK_NOPE + V_DIM)), KV_LORA ** -0.5),
        'w_o_mla': nrm(ks[22], (L, N_HEADS * V_DIM, D), (N_HEADS * V_DIM) ** -0.5),
        'w_fourier': nrm(ks[23], (L, FOURIER_WIDTH, D), FOURIER_WIDTH ** -0.5),
        'b_fourier': nrm(ks[24], (L, D), 0.02),
        'w_bgate': nrm(ks[25], (L, D, N_BRANCH * D), D ** -0.5),
        'b_bgate': nrm(ks[26], (L, N_BRANCH * D), 0.02),
        'w_out': nrm(ks[27], (L, D, D), D ** -0.5),
        'g_ffn2': gain(ks[28], (L, D)),
        'w1_ffn2': nrm(ks[29], (L, D, D_FF), D ** -0.5),
        'w3_ffn2': nrm(ks[30], (L, D, D_FF), D ** -0.5),
        'w2_ffn2': nrm(ks[31], (L, D_FF, D), D_FF ** -0.5),
        'g_final': gain(ks[32], (D,)),
    }

def second_block(x, c, ctx, c_ctx, w_ada, b_ada, g_ffn1, w1_ffn1, w3_ffn1, w2_ffn1, g_mix, w_in,
              w_dw, b_dw, ln_g_conv, ln_b_conv, w_pw_conv, b_pw_conv, g_qnorm, w_uq, g_kvnorm,
              w_ukv, w_o_mla, w_fourier, b_fourier, w_bgate, b_bgate, w_out, g_ffn2, w1_ffn2,
              w3_ffn2, w2_ffn2, g_final):
    cos, sin = axial_rope_tables(x.shape[1], x.dtype)
    h, hc = x, ctx
    for l in range(DEPTH):
        last = l == DEPTH - 1
        mod = jax.nn.silu(c) @ w_ada[l] + b_ada[l]
        sh1, sc1, gt1, sh2, sc2, gt2, sh3, sc3, gt3 = [m[:, None, :] for m in jnp.split(mod, N_ADA, axis=-1)]
        modc = jax.nn.silu(c_ctx) @ w_ada[l] + b_ada[l]
        csh1, csc1, cgt1, csh2, csc2, cgt2, csh3, csc3, cgt3 = jnp.split(modc, N_ADA, axis=-1)

        h = h + HALF * gt1 * swiglu_2(ada_norm(h, g_ffn1[l], sh1, sc1), w1_ffn1[l], w3_ffn1[l], w2_ffn1[l])
        hc = hc + HALF * cgt1 * swiglu_2(ada_norm(hc, g_ffn1[l], csh1, csc1), w1_ffn1[l], w3_ffn1[l], w2_ffn1[l])

        u = ada_norm(h, g_mix[l], sh2, sc2)
        uc = ada_norm(hc, g_mix[l], csh2, csc2)
        z_conv, z_cq, z_ckv, z_kr, z_four = split_mixing(u @ w_in[l])
        zc_conv, zc_cq, zc_ckv, zc_kr, zc_four = split_mixing(uc @ w_in[l])

        k_lat, v_lat = mla_kv(z_ckv, z_kr, g_kvnorm[l], w_ukv[l], cos, sin)
        k_ctx, v_ctx = mla_kv(zc_ckv, zc_kr, g_kvnorm[l], w_ukv[l], None, None)
        q_lat = mla_q(z_cq, g_qnorm[l], w_uq[l], cos, sin)
        attn = attend_blocked(q_lat, jnp.concatenate([k_ctx, k_lat], axis=1),
                              jnp.concatenate([v_ctx, v_lat], axis=1))
        y = merge_branches(u,
                           conv_module(z_conv, w_dw[l], b_dw[l], ln_g_conv[l], ln_b_conv[l], w_pw_conv[l], b_pw_conv[l]),
                           attn @ w_o_mla[l],
                           fourier_mix(z_four, w_fourier[l], b_fourier[l]),
                           w_bgate[l], b_bgate[l], w_out[l])
        h = h + gt2 * y
        if not last:
            q_ctx = mla_q(zc_cq, g_qnorm[l], w_uq[l], None, None)
            attn_c = attend_dense(q_ctx, k_ctx, v_ctx)
            yc = merge_branches(uc,
                                conv_module(zc_conv, w_dw[l], b_dw[l], ln_g_conv[l], ln_b_conv[l], w_pw_conv[l], b_pw_conv[l]),
                                attn_c @ w_o_mla[l],
                                fourier_mix(zc_four, w_fourier[l], b_fourier[l]),
                                w_bgate[l], b_bgate[l], w_out[l])
            hc = hc + cgt2 * yc

        h = h + HALF * gt3 * swiglu_2(ada_norm(h, g_ffn2[l], sh3, sc3), w1_ffn2[l], w3_ffn2[l], w2_ffn2[l])
        if not last:
            hc = hc + HALF * cgt3 * swiglu_2(ada_norm(hc, g_ffn2[l], csh3, csc3), w1_ffn2[l], w3_ffn2[l], w2_ffn2[l])
    return rms_norm(h, g_final)


def setup_inputs(seed=0):
    out = dict(first_inputs(seed))
    for name, value in second_inputs(seed + 1).items():
        if name != "x":
            out[name + "_2"] = value
    return out


def reference(
    x, w_in, attn_sinks, conv_w, w_branch_a, w_branch_b, w_branch_c, w_out, ln1_g, ln1_b,
    w_ffn_gate, w_ffn_up, w_ffn_down, ln2_g, ln2_b, c_2, ctx_2, c_ctx_2, w_ada_2, b_ada_2,
    g_ffn1_2, w1_ffn1_2, w3_ffn1_2, w2_ffn1_2, g_mix_2, w_in_2, w_dw_2, b_dw_2, ln_g_conv_2,
    ln_b_conv_2, w_pw_conv_2, b_pw_conv_2, g_qnorm_2, w_uq_2, g_kvnorm_2, w_ukv_2, w_o_mla_2,
    w_fourier_2, b_fourier_2, w_bgate_2, b_bgate_2, w_out_2, g_ffn2_2, w1_ffn2_2, w3_ffn2_2,
    w2_ffn2_2, g_final_2,
):
    x = first_block(
        x, w_in, attn_sinks, conv_w, w_branch_a, w_branch_b, w_branch_c, w_out, ln1_g, ln1_b,
        w_ffn_gate, w_ffn_up, w_ffn_down, ln2_g, ln2_b,
    )
    return second_block(
        x, c_2, ctx_2, c_ctx_2, w_ada_2, b_ada_2, g_ffn1_2, w1_ffn1_2, w3_ffn1_2, w2_ffn1_2,
        g_mix_2, w_in_2, w_dw_2, b_dw_2, ln_g_conv_2, ln_b_conv_2, w_pw_conv_2, b_pw_conv_2,
        g_qnorm_2, w_uq_2, g_kvnorm_2, w_ukv_2, w_o_mla_2, w_fourier_2, b_fourier_2, w_bgate_2,
        b_bgate_2, w_out_2, g_ffn2_2, w1_ffn2_2, w3_ffn2_2, w2_ffn2_2, g_final_2,
    )


_drawn_inputs = setup_inputs


def setup_inputs(seed=0):
    import zlib

    import numpy as np

    out = dict(_drawn_inputs(seed))
    spreads = {}
    factors = {'attn_sinks': 8.0,
     'ctx_2': 4.66,
     'g_ffn1_2': 8.0,
     'g_mix_2': 8.0,
     'b_dw_2': 32.433,
     'ln_g_conv_2': 46.503,
     'ln_b_conv_2': 51.507,
     'b_pw_conv_2': 32.049,
     'g_qnorm_2': 8.0,
     'w_uq_2': 2.749,
     'g_kvnorm_2': 8.0,
     'b_fourier_2': 31.445,
     'b_bgate_2': 24.105,
     'g_ffn2_2': 8.0,
     'g_final_2': 7.764}
    for name, (base, spread) in spreads.items():
        noise = np.random.default_rng([zlib.crc32(name.encode()), seed]).standard_normal(out[name].shape)
        drawn = base * np.exp(spread * noise) if base else spread * noise
        out[name] = jnp.asarray(drawn.astype(out[name].dtype))
    for name, factor in factors.items():
        out[name] = (out[name] * factor).astype(out[name].dtype)
    return out
```

```python
from contextlib import ExitStack

import numpy as np

import concourse.bass as bass
from concourse import mybir

ALU = mybir.AluOpType
ACT = mybir.ActivationFunctionType
F32 = mybir.dt.float32
F32R = mybir.dt.float32r
AX_X = mybir.AxisListType.X

P = 128
L = 2
D = 1024
DT = D // P
S = 256
QT = S // P
HD = 64
H = 8
FF = 2816
FT = FF // P
CHUNKS = [8, 8, FT - 16]
ALPHA = (2 * L) ** 0.25
LN_EPS = 1e-5
EPS = 1e-6

SLOTS = 4
SLOT = 8 * P

NADA = 9
ADA_UNIT = 768
ADA_HALF = ADA_UNIT // 2
ADA_N = NADA * D // ADA_HALF
ADA_J = ADA_HALF // P
ADA_WIDE = 4 * (ADA_N - 1) + P
CT = 3
TAPS = 31
PAD = TAPS // 2
ROPE = 32
QK = HD + ROPE
QLT, KVT = 3, 2
FG = 4

SLOPES = [2.0 ** (-8.0 * (i + 1.0) / (2 * H)) for i in range(2 * H)]


def stages():
    out = []
    for l in range(L):
        out.append((f"ada{l}", DT * NADA * D // ADA_UNIT, ADA_UNIT // P))
    for l in range(L):
        out.append((f"qkv{l}", 18, 8))
        out.append((f"bbb{l}", 12, 8))
        out.append((f"gate{l}", 24, 8))
        out.append((f"merge{l}", 24, 4))
        out.append((f"out{l}", 8, 8))
        for c, n in enumerate(CHUNKS):
            out.append((f"up{l}{c}", 2 * n, 8))
            out.append((f"down{l}{c}", 8, n))
    for l in range(L):
        for f in "12":
            if f == "2":
                out.append((f"mix{l}", 16, 8))
                out.append((f"kv{l}", 8, KVT))
                out.append((f"q{l}", H, QLT))
                out += [(f"bm{l}{m}{j}", 1, k) for m in range(DT) for j, k in enumerate((8, CT, 8, 4, 8, 4))]
                out.append((f"bout{l}", 8, 8))
            for c, n in enumerate(CHUNKS):
                out.append((f"fup{f}{l}{c}", 2 * n, 8))
                out.append((f"fdown{f}{l}{c}", 8, n))
    return out


class Plan:

    def __init__(self):
        self.start, self.kt, self.offset, self.evac = {}, [], [], []
        at = 0
        for name, n, kt in stages():
            self.start[name] = len(self.kt)
            for _ in range(n):
                self.kt.append(kt)
                self.offset.append(at)
                self.evac.append(0 if name.startswith("ada") else 1)
                at += P * kt * P
        self.total = at
        self.units = len(self.kt)

    def freed(self, u):
        return sum(self.evac[u % SLOTS:u:SLOTS])

    def slot(self, u):
        return u % SLOTS


class Tally:

    def __init__(self, eng, sem):
        self.eng, self.sem, self.n, self.per, self.it = eng, sem, 0, 0, 0

    def add(self, ins, k=1):
        ins.then_inc(self.sem, k)
        self.n += k
        return ins

    def wait(self, k=0):
        self.n += k
        self.eng.wait_ge(self.sem, self.n + self.per * self.it)

    def enter(self, it, per):
        self.it, self.per, self.at = it, per, self.n

    def leave(self, iters):
        assert self.n - self.at == self.per, (self.sem, self.n - self.at, self.per)
        self.n += self.per * (iters - 1)
        self.it = self.per = 0


def repeat(eng, iters, body, tallies):
    if iters <= 0:
        return
    if iters == 1:
        body(0)
        return
    with eng.Fori(0, iters) as i:
        for t, per in tallies:
            t.enter(i, per)
        body(i)
        for t, _ in tallies:
            t.leave(iters)


def columns(parts):
    out, at = {}, 0
    for name, n in parts:
        out[name] = (at, n)
        at += n
    return out, at


PAR1, NPAR1 = columns([("ln1_g", L * DT), ("ln1_b", L * DT), ("ln2_g", L * DT), ("ln2_b", L * DT),
                       ("conv_w", L * 3 * 4), ("sinks", L * H * QT), ("b_ada", L * NADA * DT), ("c", DT * 2)])
PAR2, NPAR2 = columns([("g_ffn1", L * DT), ("g_mix", L * DT), ("g_ffn2", L * DT), ("w_dw", L * TAPS * CT),
                       ("b_dw", L * CT), ("ln_g", L * CT), ("ln_b", L * CT), ("b_pw", L * DT),
                       ("g_qnorm", L * QLT), ("g_kvnorm", L * KVT), ("b_four", L * DT),
                       ("b_bgate", L * 3 * DT), ("g_final", DT)])
CST0, NCST0 = columns([("ident", P), ("ones", P), ("eps", 2)])
CST1, NCST1 = columns([("dist_a", QT * S), ("dist_c", QT * S), ("pick", 2 * ADA_N)])
CST2, NCST2 = columns([("cos", S), ("sin", S), ("turn", ROPE)])
DFT, NDFT = columns([("chan", 2 * P), ("tok", QT * 2 * S)])


def program(nc, xT, ctxT, w_stream, par1_d, par2_d, cst0_d, cst1_d, cst2_d, dft_d, out):
    plan = Plan()
    U = plan.start
    T2 = 2 * S
    ADA_PER = 2 * NADA * D // ADA_UNIT

    with ExitStack() as ctx:
        def sem(name):
            return ctx.enter_context(nc.semaphore(name))

        def sb(where, name, shape, dt=F32):
            return where.enter_context(nc.sbuf_tensor(name, shape, dt))

        raw = sb(ctx, "raw", [P, SLOTS, SLOT])
        whi = sb(ctx, "whi", [P, SLOTS, SLOT], F32R)
        wlo = sb(ctx, "wlo", [P, SLOTS, SLOT], F32R)
        cst0 = sb(ctx, "cst0", [P, NCST0])
        cst2 = sb(ctx, "cst2", [P, NCST2])
        par2 = sb(ctx, "par2", [P, NPAR2])
        mod = sb(ctx, "mod", [P, L, NADA * DT, 2])
        h = sb(ctx, "h", [P, DT, T2])
        small = sb(ctx, "small", [P, 5, H * QT])
        ident, ones = cst0[:, 0:P], cst0[:, P:2 * P]
        ln_eps, rms_eps = cst0[:, 2 * P:2 * P + 1], cst0[:, 2 * P + 1:2 * P + 2]

        one = ExitStack()
        gates = sb(one, "gates", [P, 24, S])
        qa = sb(one, "qa", [P, 4, S])
        ka = sb(one, "ka", [P, S])
        va = sb(one, "va", [P, QT, P])
        qc = sb(one, "qc", [P, 4, S])
        kc = sb(one, "kc", [P, 4, S])
        vc = sb(one, "vc", [P, QT, 4 * P])
        bbb = sb(one, "bbb", [P, 12, S])
        x1 = sb(one, "x1", [P, DT, S])
        x1hi = sb(one, "x1hi", [P, DT, S], F32R)
        x1lo = sb(one, "x1lo", [P, DT, S], F32R)
        y1hi = sb(one, "y1hi", [P, 12, S], F32R)
        y1lo = sb(one, "y1lo", [P, 12, S], F32R)
        lg = sb(one, "lg", [P, 2 * H, S])
        pt1 = sb(one, "pt1", [P, 2, QT * S])
        par1 = sb(one, "par1", [P, NPAR1])
        cst1 = sb(one, "cst1", [P, NCST1])
        one.close()

        zero = ExitStack()
        cs = sb(zero, "cs", [P, DT, 2])
        wide = sb(zero, "wide", [P, DT, ADA_WIDE], F32R)
        live = sb(zero, "live", [P, 2, ADA_WIDE], F32R)
        rows = sb(zero, "rows", [P, ADA_HALF])
        blank = sb(zero, "blank", [P, ADA_HALF])
        zero.close()

        two = ExitStack()
        uhi = sb(two, "uhi", [P, DT, T2], F32R)
        ulo = sb(two, "ulo", [P, DT, T2], F32R)
        yhi = sb(two, "yhi", [P, 11, T2], F32R)
        ylo = sb(two, "ylo", [P, 11, T2], F32R)
        big1 = sb(two, "big1", [P, DT, T2])
        big2 = sb(two, "big2", [P, DT, T2])
        vt = sb(two, "vt", [P, 4, T2])
        vpad = sb(two, "vpad", [P, CT, 2, S + 2 * PAD])
        acc = sb(two, "acc", [P, CT, T2])
        pp = sb(two, "pp", [P, 4, T2])
        scl = sb(two, "scl", [P, 3, DT, 2])
        hgt = sb(two, "hgt", [P, 2, DT, 2])
        two.close()
        dft = pp[:, 0:3, :].rearrange("p a b -> p (a b)")
        rs1, rs2 = pt1[:, 0, 0:S], pp[:, 3, :]

        banks = [ctx.enter_context(nc.psum_tensor(f"bank{b}", [P, 512], F32)) for b in range(8)]

        def p1(name, l, n):
            at, _ = PAR1[name]
            return par1[:, at + l * n:at + (l + 1) * n]

        def p2(name, l, n):
            at, _ = PAR2[name]
            return par2[:, at + l * n:at + (l + 1) * n]

        def mods(l, n):
            return mod[:, l, n * DT:(n + 1) * DT, :]

        dist = {k: cst1[:, CST1[f"dist_{k}"][0]:CST1[f"dist_{k}"][0] + QT * S] for k in "ac"}
        pick = cst1[0:4 * ADA_N, CST1["pick"][0]:CST1["pick"][0] + 2 * ADA_N]
        cos, sin = cst2[HD:QK, 0:S], cst2[HD:QK, S:2 * S]
        turn = cst2[HD:QK, 2 * S:2 * S + ROPE]

        s_land = [sem(f"unit_landed{s}") for s in range(SLOTS)]
        s_high = sem("unit_high_ready")
        s_low = sem("unit_low_ready")
        s_used = sem("unit_used")
        s_free = [sem(f"bank_read{s}") for s in range(SLOTS)]
        s_const = sem("constants_landed")
        s_dft = sem("dft_landed")
        s_out = sem("out_landed")
        s_dve = sem("dve_step")
        s_val = sem("dve_value_ready")
        s_dop = sem("dve_operand_ready")
        s_split = sem("act_split_ready")
        s_sread = sem("scores_read")
        s_prob = sem("probs_ready")
        s_wide = sem("ada_vector_ready")
        s_outv = sem("out_ready")
        s_aval = sem("act_value_ready")
        s_mid = sem("first_block_out")
        s_ahi = sem("act_high_ready")
        s_sq = sem("squares_ready")
        s_aop = sem("act_operand_ready")
        s_pt = sem("turned_probs_ready")
        s_stat = sem("sum_ready")
        s_mean = sem("mean_ready")
        s_score = sem("scores_ready")
        s_turned = sem("probs_turned")
        s_head = sem("heads_ready")
        s_rot = sem("rotated_ready")
        s_ada = sem("ada_products_ready")
        block = ctx.enter_context(nc.Block())

        def after(u):
            return s_free[u % SLOTS], plan.freed(u) + 1

        def after_at(u0, j, i, per):
            u = u0 + j
            return s_free[u % SLOTS], plan.freed(u) + 1 + per // SLOTS * i

        @block.sync
        def _(sp):
            used = Tally(sp, s_used)

            def load(u, it=0, per=0):
                if u >= SLOTS:
                    sp.wait_ge(s_low, u - SLOTS + 1 + per * it)
                n = plan.kt[u] * P
                if per:
                    src = w_stream[bass.ds((plan.offset[u + per] - plan.offset[u]) * it + plan.offset[u], P * n)]
                else:
                    src = w_stream[plan.offset[u]:plan.offset[u] + P * n]
                sp.dma_start(raw[:, u % SLOTS, 0:n], src.rearrange("(p n) -> p n", p=P)).then_inc(s_land[u % SLOTS], 16)

            def run(u0, n, per):
                iters = n // per
                if iters > 1:
                    with sp.Fori(0, iters - 1) as i:
                        for j in range(per):
                            load(u0 + j, i, per)
                for u in range(u0 + max(iters - 1, 0) * per, u0 + n):
                    load(u)

            for u in range(SLOTS):
                load(u)
            sp.dma_start(par1[:, :], par1_d).then_inc(s_const, 16)
            sp.dma_start(cst0[:, :], cst0_d).then_inc(s_const, 16)
            sp.dma_start(cst1[:, :], cst1_d).then_inc(s_const, 16)
            sp.dma_start(cst2[:, :], cst2_d).then_inc(s_const, 16)
            sp.dma_start(par2[:, :], par2_d).then_inc(s_const, 16)
            sp.dma_start(x1[:, :, :], xT.rearrange("p (t s) -> p t s", t=DT)).then_inc(s_const, 16)
            sp.dma_start(h[:, :, 0:S], ctxT.rearrange("p (t s) -> p t s", t=DT)).then_inc(s_const, 16)
            for l in range(L):
                n = DT * NADA * D // ADA_UNIT
                first = SLOTS if l == 0 else 0
                run(U[f"ada{l}"] + first, n - first, SLOTS)
            for l in range(L):
                for name in ("qkv", "bbb", "gate", "merge", "out"):
                    n = {"qkv": 18, "bbb": 12, "gate": 24, "merge": 24, "out": 8}[name]
                    run(U[f"{name}{l}"], n, SLOTS)
                for c, n in enumerate(CHUNKS):
                    run(U[f"up{l}{c}"], 2 * n, SLOTS)
                    run(U[f"down{l}{c}"], 8, SLOTS)
            for l in range(L):
                for f in "12":
                    if f == "2":
                        run(U[f"mix{l}"], 16, SLOTS)
                        sp.wait_ge(s_used, U[f"mix{l}"] + 1)
                        sp.dma_start(dft[:, 0:NDFT], dft_d).then_inc(s_dft, 16)
                        run(U[f"kv{l}"], 8, SLOTS)
                        run(U[f"q{l}"], H, SLOTS)
                        run(U[f"bm{l}00"], 6 * DT, 12)
                        run(U[f"bout{l}"], 8, SLOTS)
                    for c, n in enumerate(CHUNKS):
                        run(U[f"fup{f}{l}{c}"], 2 * n, SLOTS)
                        run(U[f"fdown{f}{l}{c}"], 8, SLOTS)
            for m in range(DT):
                sp.wait_ge(s_outv, m + 1)
                sp.dma_start(out[:, m * S:(m + 1) * S], big1[:, m, S:T2]).then_inc(s_out, 16)
            sp.wait_ge(s_out, 16 * DT)

        @block.scalar
        def _(act):
            val, stat, turned, head = (Tally(act, s) for s in (s_val, s_stat, s_turned, s_head))
            sc = nc.scalar

            def high(u, it=0, per=0):
                if u >= plan.units:
                    return
                act.wait_ge(s_land[u % SLOTS], 16 * (u // SLOTS + 1) + 16 * (per // SLOTS) * it)
                if u >= SLOTS:
                    act.wait_ge(s_used, u - SLOTS + 1 + per * it)
                n = plan.kt[u] * P
                sc.copy(whi[:, u % SLOTS, 0:n], raw[:, u % SLOTS, 0:n]).then_inc(s_high, 1)

            def stream(u0, n, per, evac, tallies=()):
                iters = n // per
                first = int(u0 == 0)
                for j in range(first * per):
                    high(j + 2)
                    evac(j, 0)

                def body(i):
                    for j in range(per):
                        high(u0 + first * per + j + 2, i, per)
                        evac(j, i + first)

                repeat(act, iters - 1 - first, body, tallies)
                for j in range(per):
                    high(u0 + n - per + j + 2)
                    evac(j, iters - 1)

            def done(u0, j, i, per):
                act.wait_ge(s_used, u0 + j + per * i + 1)

            def bank(u0, j):
                return banks[(u0 + j) % SLOTS]

            def read(u0, j):
                return s_free[(u0 + j) % SLOTS]

            act.wait_ge(s_const, 7 * 16)
            at = PAR1["c"][0]
            high(0)
            high(1)
            sc.activation(cs[:, :, :], par1[:, at:at + 2 * DT].rearrange("p (t s) -> p t s", s=2),
                          ACT.Silu).then_inc(s_aval, 1)
            act.wait_ge(s_aval, 1)
            val.wait(1)
            mid = 4 * (ADA_N - 1)
            sc.copy(wide[:, :, mid:mid + 2], cs[:, :, :]).then_inc(s_ahi, 1)
            for l in range(L):
                stream(U[f"ada{l}"], DT * NADA * D // ADA_UNIT, ADA_PER, lambda j, i: None)

            for m in range(DT):
                sc.copy(x1hi[:, m, :], x1[:, m, :]).then_inc(s_ahi, 1)

            def attention1(kind, y0):
                val.wait(1)
                for n in range(H * QT):
                    sc.activation(lg[:, n, :], lg[:, n, :], ACT.Exp, bias=small[:, 1, n:n + 1],
                                  scale=HD ** -0.5, accum_out=small[:, 2, n:n + 1]).then_inc(s_aval, 1)
                if kind == "a":
                    sc.activation(small[:, 3, :], small[:, 4, :], ACT.Exp).then_inc(s_aval, 1)
                for n in range(H + 1):
                    if n < H:
                        turned.wait(1)
                        b = banks[6 + n % 2]
                        sc.copy(pt1[:, n % 2, 0:S], b[:, 0:S])
                        sc.copy(pt1[:, n % 2, S + P:2 * S], b[:, S + P:2 * S]).then_inc(s_pt, 1)
                    if n >= 1 and n % 2 == 0:
                        head.wait(1)
                        sc.copy(y1hi[:, y0 + n // 2 - 1, :], banks[n // 2 - 1][:, 0:S]).then_inc(s_ahi, 1)

            def hidden(u0, n, c0, c1, sg, hid, ht):
                sc.preload_act_table(ACT.Silu)

                def evac(j, i):
                    if j % 2 == 0:
                        done(u0, j, i, 4)
                        sc.activation(sg(j // 2)[:, c0:c1], bank(u0, j)[:, c0:c1], ACT.Silu).then_inc(read(u0, j), 1)
                    else:
                        act.wait_ge(*after_at(u0, j, i, 4))
                        sc.copy(ht[:, 2 * i + j // 2, c0:c1], hid(j // 2)[:, c0:c1]).then_inc(s_ahi, 1)

                stream(u0, 2 * n, 4, evac)

            def norm1(g, b, last):
                for m in range(0, DT, 2):
                    val.wait(1)
                    sc.activation(lg[:, m:m + 2, :], x1[:, m:m + 2, :], ACT.Square).then_inc(s_sq, 1)
                stat.wait(1)
                sc.activation(rs1, banks[5][:, 0:S], ACT.Sqrt, bias=ln_eps, scale=1.0 / D).then_inc(s_aval, 1)
                for m in range(DT):
                    if m % 2 == 0:
                        val.wait(1)
                    gm, bm = g[:, m:m + 1], b[:, m:m + 1]
                    if last:
                        sc.activation(h[:, m, S:T2], lg[:, m, :], ACT.Identity, bias=bm, scale=gm).then_inc(s_mid, 1)
                    else:
                        sc.activation(x1hi[:, m, :], lg[:, m, :], ACT.Identity, bias=bm, scale=gm)
                        sc.activation(x1[:, m, :], lg[:, m, :], ACT.Identity, bias=bm, scale=gm).then_inc(s_ahi, 1)

            for l in range(L):
                u0 = U[f"qkv{l}"]
                dst = [qa[:, j, :] for j in range(4)] + [ka[:, :], None] + [qc[:, j, :] for j in range(4)] + \
                    [kc[:, j, :] for j in range(4)]
                for j in range(18):
                    high(u0 + j + 2)
                    done(u0, j, 0, 0)
                    if j == 5 or j >= 14:
                        v = va[:, :, :] if j == 5 else vc[:, :, (j - 14) * P:(j - 13) * P]
                        sc.copy(v, bank(u0, j)[:, 0:S].rearrange("p (t c) -> p t c", t=QT)).then_inc(read(u0, j), 1)
                    else:
                        sc.copy(dst[j], bank(u0, j)[:, 0:S]).then_inc(read(u0, j), 1)

                u1 = U[f"bbb{l}"]

                def evac_b(j, i):
                    done(u1, j, i, 4)
                    sc.copy(bbb[:, 4 * i + j, :], bank(u1, j)[:, 0:S]).then_inc(read(u1, j), 1)
                stream(u1, 12, 4, evac_b)

                u2 = U[f"gate{l}"]
                sc.preload_act_table(ACT.Sigmoid)

                def evac_g(j, i):
                    done(u2, j, i, 4)
                    sc.activation(gates[:, 4 * i + j, :], bank(u2, j)[:, 0:S], ACT.Sigmoid).then_inc(read(u2, j), 1)
                stream(u2, 24, 4, evac_g)

                attention1("a", 0)
                val.wait(1)
                sc.copy(y1hi[:, 4:8, :], bbb[:, 8:12, :]).then_inc(s_ahi, 1)
                attention1("c", 8)

                def evac_m(j, i):
                    if j % 3 == 2:
                        val.wait(1)
                        sc.copy(x1hi[:, 4 * i + j // 3, :], lg[:, 3 + (j // 3) % 2, :]).then_inc(s_ahi, 1)
                stream(U[f"merge{l}"], 24, 12, evac_m, [(val, 4)])
                stream(U[f"out{l}"], 8, 4, lambda j, i: None)
                norm1(p1("ln1_g", l, DT), p1("ln1_b", l, DT), False)
                for c, n in enumerate(CHUNKS):
                    hidden(U[f"up{l}{c}"], n, 0, S, lambda k: lg[:, k, :], lambda k: lg[:, 2 + k, :], y1hi)
                    stream(U[f"down{l}{c}"], 8, 4, lambda j, i: None)
                norm1(p1("ln2_g", l, DT), p1("ln2_b", l, DT), l == L - 1)

            act.wait_ge(s_mid, DT)

            def norm2(l, which, c0, ready):
                for m in range(DT):
                    if ready:
                        act.wait_ge(*after(ready + m))
                    sc.activation(big1[:, m, c0:T2], h[:, m, c0:T2], ACT.Square).then_inc(s_sq, 1)
                stat.wait(1)
                sc.activation(rs2[:, c0:T2], banks[4][:, c0:T2], ACT.Sqrt, bias=rms_eps,
                              scale=1.0 / D).then_inc(s_aval, 1)
                if which is None:
                    return
                for m in range(DT):
                    val.wait(1)
                    for s in range(c0 // S, 2):
                        bs = mods(l, 3 * which)[:, m, s:s + 1]
                        gs = scl[:, which, m, s:s + 1]
                        cols = slice(s * S, (s + 1) * S)
                        sc.activation(uhi[:, m, cols], big1[:, m, cols], ACT.Identity, bias=bs, scale=gs)
                        ins = sc.activation(big1[:, m, cols], big1[:, m, cols], ACT.Identity, bias=bs, scale=gs)
                    ins.then_inc(s_ahi, 1)

            def ffn2(l, f, c0):
                for c, n in enumerate(CHUNKS):
                    hidden(U[f"fup{f}{l}{c}"], n, c0, T2, lambda k: pp[:, k, :], lambda k: pp[:, 2 + k, :], yhi)
                    stream(U[f"fdown{f}{l}{c}"], 8, 4, lambda j, i: None)

            def low_norm(src, n, c0, dst, width):
                for m in range(n):
                    sc.activation(big1[:, 4 + m, c0:T2], src[:, m, c0:T2], ACT.Square).then_inc(s_sq, 1)
                stat.wait(1)
                sc.activation(rs2[:, c0:T2], banks[4][:, c0:T2], ACT.Sqrt, bias=rms_eps,
                              scale=1.0 / width).then_inc(s_aval, 1)
                for m in range(n):
                    val.wait(1)
                    sc.copy(yhi[:, dst[m], c0:T2], src[:, m, c0:T2]).then_inc(s_ahi, 1)

            def attention2(s):
                nk = (s + 1) * S
                N = H * QT

                def exp(n):
                    val.wait(1)
                    sc.activation(pp[:, n % 2, 0:nk], banks[4 + n % 2][:, 0:nk], ACT.Exp, bias=small[:, 1, n:n + 1],
                                  scale=QK ** -0.5, accum_out=small[:, 2, n:n + 1]).then_inc(s_aval, 1)
                exp(0)
                for n in range(N + 1):
                    if n + 1 < N:
                        exp(n + 1)
                    if n < N:
                        turned.wait(1)
                        sc.copy(pp[:, 2 + n % 2, 0:nk], banks[6 + n % 2][:, 0:nk]).then_inc(s_pt, 1)
                    if n and n % 4 == 0:
                        head.wait(1)
                        j = n // 4 - 1
                        sc.copy(yhi[:, CT + j, s * S:(s + 1) * S], banks[j][:, 0:S]).then_inc(s_ahi, 1)

            for l in range(L):
                last = l == L - 1
                c0 = S if last else 0
                norm2(l, 0, 0, U[f"fdown2{l - 1}{len(CHUNKS) - 1}"] if l else 0)
                ffn2(l, "1", 0)
                norm2(l, 1, 0, U[f"fdown1{l}{len(CHUNKS) - 1}"])

                u0 = U[f"mix{l}"]
                for j in range(16):
                    high(u0 + j + 2)
                    done(u0, j, 0, 0)
                    cc = 0 if 4 <= j < 7 else c0
                    src = bank(u0, j)[:, cc:T2]
                    if j >= 13:
                        sc.activation(acc[:, j - 13, cc:T2], src, ACT.Sigmoid).then_inc(read(u0, j), 1)
                    else:
                        to = (big2[:, j, cc:T2] if j < 4 else big1[:, j - 4, cc:T2] if j < 6 else
                              vt[:, 3, cc:T2] if j == 6 else vt[:, j - 7, cc:T2] if j < 10 else
                              big2[:, 4 + j - 10, cc:T2])
                        sc.copy(to, src).then_inc(read(u0, j), 1)

                N = FG * (2 - c0 // S)
                for n in range(N + 1):
                    if n < N:
                        stat.wait(1)
                        sc.copy(big1[:, 2 + n % 2, :], banks[4 + n % 2][:, :]).then_inc(s_aop, 1)
                    if n:
                        g, s = (n - 1) % FG, (n - 1) // FG + c0 // S
                        head.wait(1)
                        sc.copy(yhi[:, CT + 4 + g, s * S:(s + 1) * S],
                                banks[6 + (n - 1) % 2][:, 0:S]).then_inc(s_ahi, 1)

                low_norm(big1, KVT, 0, [3, 4], KVT * P)
                low_norm(vt, QLT, c0, [5, 6, 0], QLT * P)
                for s in range(2):
                    if s:
                        val.wait(1)
                    src = big1[HD:QK, 6, 0:S] if s else vt[HD:QK, 3, 0:S]
                    for hh in range(H):
                        ins = sc.copy(big2[HD:QK, hh, s * S:(s + 1) * S], src)
                ins.then_inc(s_aop, 1)

                u0 = U[f"kv{l}"]
                for j in range(8):
                    high(u0 + j + 2)
                    done(u0, j, 0, 0)
                    if j < 4:
                        sc.copy(big2[0:HD, 2 * j, :], bank(u0, j)[0:HD, :])
                        sc.copy(big2[0:HD, 2 * j + 1, :], bank(u0, j)[HD:P, :]).then_inc(read(u0, j), 1)
                    else:
                        sc.copy(vt[:, :, (j - 4) * P:(j - 3) * P],
                                bank(u0, j)[:, :].rearrange("p (t c) -> p t c", t=4)).then_inc(read(u0, j), 1)
                u0 = U[f"q{l}"]
                for j in range(H):
                    high(u0 + j + 2)
                    done(u0, j, 0, 0)
                    sc.copy(big1[0:QK, j, c0:T2], bank(u0, j)[0:QK, c0:T2]).then_inc(read(u0, j), 1)

                for s in range(c0 // S, 2):
                    attention2(s)

                for m in range(CT):
                    val.wait(1)
                    sc.activation(big1[:, m, c0:T2], acc[:, m, c0:T2], ACT.Square).then_inc(s_sq, 1)
                stat.wait(1)
                sc.activation(rs2[:, c0:T2], banks[5][:, c0:T2], ACT.Sqrt, bias=rms_eps,
                              scale=1.0 / (CT * P)).then_inc(s_aval, 1)
                lng, lnb = p2("ln_g", l, CT), p2("ln_b", l, CT)
                for m in range(CT):
                    val.wait(1)
                    sc.activation(yhi[:, m, c0:T2], acc[:, m, c0:T2], ACT.Silu, bias=lnb[:, m:m + 1],
                                  scale=lng[:, m:m + 1])
                    sc.activation(big1[:, m, c0:T2], acc[:, m, c0:T2], ACT.Silu, bias=lnb[:, m:m + 1],
                                  scale=lng[:, m:m + 1]).then_inc(s_ahi, 1)

                u3 = U[f"bm{l}00"]
                bg = p2("b_bgate", l, 3 * DT)
                sc.preload_act_table(ACT.Sigmoid)

                def evac_g2(j, i):
                    if j % 2 == 0:
                        br, m = j % 6 // 2, 2 * i + j // 6
                        done(u3, j, i, 12)
                        sc.activation(pp[:, br, c0:T2], bank(u3, j)[:, c0:T2], ACT.Sigmoid,
                                      bias=bg[:, bass.ds(br * DT + m, 1)]).then_inc(read(u3, j), 1)
                stream(u3, 6 * DT, 12, evac_g2)
                for m in range(DT):
                    val.wait(1)
                    sc.copy(uhi[:, m, c0:T2], big1[:, m, c0:T2]).then_inc(s_ahi, 1)
                stream(U[f"bout{l}"], 8, 4, lambda j, i: None)
                norm2(l, 2, c0, U[f"bout{l}"])
                ffn2(l, "2", c0)
            norm2(L - 1, None, S, U[f"fdown2{L - 1}{len(CHUNKS) - 1}"])

        @block.vector
        def _(dve):
            ve = nc.vector
            step = Tally(dve, s_dve)
            aval, ahi, mean, score, rot, ada = (Tally(dve, s) for s in
                                                        (s_aval, s_ahi, s_mean, s_score, s_rot, s_ada))

            def low(u, it=0, per=0):
                if u >= plan.units:
                    return
                dve.wait_ge(s_high, u + 1 + per * it)
                n = plan.kt[u] * P
                ve.tensor_tensor(wlo[:, u % SLOTS, 0:n], raw[:, u % SLOTS, 0:n],
                                 whi[:, u % SLOTS, 0:n].bitcast(F32), ALU.subtract).then_inc(s_low, 1)

            def stream(u0, n, per, evac, tallies=()):
                iters = n // per
                first = int(u0 == 0)
                for j in range(first * per):
                    low(j + 2)
                    evac(j, 0)

                def body(i):
                    for j in range(per):
                        low(u0 + first * per + j + 2, i, per)
                        evac(j, i + first)

                repeat(dve, iters - 1 - first, body, tallies)
                for j in range(per):
                    low(u0 + n - per + j + 2)
                    evac(j, iters - 1)

            def done(u0, j, i, per):
                dve.wait_ge(s_used, u0 + j + per * i + 1)

            def bank(u0, j):
                return banks[(u0 + j) % SLOTS]

            def read(u0, j):
                return s_free[(u0 + j) % SLOTS]

            def rest(dst, src, hi):
                ve.tensor_tensor(dst, src, hi.bitcast(F32), ALU.subtract).then_inc(s_split, 1)

            def chained(ins):
                step.add(ins)
                step.wait()

            nothing = lambda j, i: None
            mid = 4 * (ADA_N - 1)
            low(0)
            low(1)
            ve.memset(blank[:, :], 0.0).then_inc(s_dop, 1)
            ve.memset(wide[:, :, :].bitcast(F32), 0.0).then_inc(s_val, 1)
            aval.wait(1)
            ahi.wait(1)
            chained(ve.tensor_tensor(wide[:, :, mid + 2:mid + 4], cs[:, :, :], wide[:, :, mid:mid + 2].bitcast(F32),
                                     ALU.subtract))
            for l in range(L):
                u0 = U[f"ada{l}"]

                def window(j, i):
                    if j % (ADA_PER // 2) == 0:
                        b = j // (ADA_PER // 2)
                        ve.tensor_copy(live[:, b, :], wide[:, bass.ds(2 * i + b, 1), :].bitcast(F32)
                                       .rearrange("p a n -> p (a n)")).then_inc(s_wide, 1)

                stream(u0, DT * NADA * D // ADA_UNIT, ADA_PER, window)
                ada.wait(1)
                ve.tensor_copy(rows[0:4 * ADA_N, :], banks[4][0:4 * ADA_N, 0:ADA_HALF]).then_inc(s_dop, 1)
                ada.wait(1)
                for j in range(ADA_J):
                    ve.tensor_tensor(
                        mod[:, l, :, :].rearrange("p (n j) s -> p j n s", j=ADA_J)[:, j],
                        banks[5][:, j * 2 * ADA_N:(j + 1) * 2 * ADA_N].rearrange("p (n s) -> p n s", s=2),
                        p1("b_ada", l, NADA * DT).rearrange("p (n j) -> p j n", j=ADA_J)[:, j].unsqueeze(2)
                        .to_broadcast([P, ADA_N, 2]), ALU.add).then_inc(s_dve, 1)
                    step.n += 1

            for m in range(DT):
                ahi.wait(1)
                rest(x1lo[:, m, :], x1[:, m, :], x1hi[:, m, :])

            def attention1(kind, l, y0):
                for hh in range(H):
                    score.wait(1)
                    slope = SLOPES[hh if kind == "a" else H + hh]
                    step.add(ve.scalar_tensor_tensor(lg[:, 2 * hh:2 * hh + 2, :], dist[kind].rearrange("p (t s) -> p t s", t=2), -slope * HD ** 0.5,
                                                     banks[4 + hh % 2][:, :].rearrange("p (t s) -> p t s", t=2), ALU.mult, ALU.add))
                    ve.memset(small[:, 3, 0:1], 0.0).then_inc(s_sread, 1) if False else None
                    step.wait()
                    ve.tensor_reduce(small[:, 0, 2 * hh:2 * hh + 2], lg[:, 2 * hh:2 * hh + 2, :], AX_X,
                                     ALU.max).then_inc(s_sread, 1)
                dve.wait_ge(s_sread, sread[0] + H)
                sread[0] += H
                if kind == "a":
                    sinks = p1("sinks", l, H * QT)
                    chained(ve.tensor_scalar(small[:, 3, :], sinks, HD ** 0.5, None, ALU.mult))
                    chained(ve.tensor_tensor(small[:, 0, :], small[:, 0, :], small[:, 3, :], ALU.max))
                    chained(ve.tensor_scalar(small[:, 1, :], small[:, 0, :], -HD ** -0.5, None, ALU.mult))
                    ve.tensor_tensor(small[:, 4, :], sinks, small[:, 1, :], ALU.add).then_inc(s_val, 1)
                else:
                    ve.tensor_scalar(small[:, 1, :], small[:, 0, :], -HD ** -0.5, None, ALU.mult).then_inc(s_val, 1)
                if kind == "a":
                    aval.wait(H * QT + 1)
                    chained(ve.tensor_tensor(small[:, 2, :], small[:, 2, :], small[:, 3, :], ALU.add))
                else:
                    aval.wait(H * QT)
                chained(ve.reciprocal(small[:, 2, :], small[:, 2, :]))
                for hh in range(H):
                    for n in (2 * hh, 2 * hh + 1):
                        ins = ve.tensor_scalar(lg[:, n, :], lg[:, n, :], small[:, 2, n:n + 1], None, ALU.mult)
                    ins.then_inc(s_prob, 1)
                for j in range(H // 2):
                    ahi.wait(1)
                    rest(y1lo[:, y0 + j, :], banks[j][:, 0:S], y1hi[:, y0 + j, :])

            sread = [0]

            def short_conv(l):
                chained(ve.tensor_tensor(bbb[:, 0:4, :], bbb[:, 0:4, :], bbb[:, 8:12, :], ALU.mult))
                w = p1("conv_w", l, 12)
                for k in (2, 1, 0):
                    d = 2 - k
                    for j in range(4):
                        wk = w[:, 4 * k + j:4 * k + j + 1]
                        if d == 0:
                            ins = ve.tensor_scalar(bbb[:, 8 + j, :], bbb[:, j, :], wk, None, ALU.mult)
                        else:
                            ins = ve.scalar_tensor_tensor(bbb[:, 8 + j, d:S], bbb[:, j, 0:S - d], wk,
                                                          bbb[:, 8 + j, d:S], ALU.mult, ALU.add)
                        step.add(ins)
                    step.wait()
                ve.tensor_tensor(bbb[:, 8:12, :], bbb[:, 8:12, :], bbb[:, 4:8, :], ALU.mult).then_inc(s_val, 1)
                ahi.wait(1)
                rest(y1lo[:, 4:8, :], bbb[:, 8:12, :], y1hi[:, 4:8, :])

            def hidden(u0, n, c0, c1, sg, hid, hi, lo):
                def evac(j, i):
                    if j % 2:
                        dve.wait_ge(*after_at(u0, j - 1, i, 4))
                        done(u0, j, i, 4)
                        ve.tensor_tensor(hid(j // 2)[:, c0:c1], sg(j // 2)[:, c0:c1], bank(u0, j)[:, c0:c1],
                                         ALU.mult).then_inc(read(u0, j), 1)
                        ahi.wait(1)
                        rest(lo[:, 2 * i + j // 2, c0:c1], hid(j // 2)[:, c0:c1], hi[:, 2 * i + j // 2, c0:c1])
                stream(u0, 2 * n, 4, evac, [(ahi, 2)])

            def norm1(last):
                mean.wait(1)
                for m in range(0, DT, 2):
                    ve.scalar_tensor_tensor(x1[:, m:m + 2, :], banks[4][:, 0:S].unsqueeze(1).to_broadcast([P, 2, S]),
                                            -1.0 / D, x1[:, m:m + 2, :], ALU.mult, ALU.add).then_inc(s_val, 1)
                aval.wait(1)
                chained(ve.reciprocal(rs1, rs1))
                for m in range(0, DT, 2):
                    ve.tensor_tensor(lg[:, m:m + 2, :], x1[:, m:m + 2, :],
                                     rs1.unsqueeze(1).to_broadcast([P, 2, S]), ALU.mult).then_inc(s_val, 1)
                if last:
                    return
                for m in range(DT):
                    ahi.wait(1)
                    rest(x1lo[:, m, :], x1[:, m, :], x1hi[:, m, :])

            def residual1(u0, first):
                def evac(j, i):
                    done(u0, j, i, 4)
                    m = 4 * i + j
                    if first:
                        ins = ve.scalar_tensor_tensor(x1[:, m, :], x1[:, m, :], ALPHA, bank(u0, j)[:, 0:S],
                                                      ALU.mult, ALU.add)
                    else:
                        ins = ve.tensor_tensor(x1[:, m, :], x1[:, m, :], bank(u0, j)[:, 0:S], ALU.add)
                    ins.then_inc(read(u0, j), 1)
                stream(u0, 8, 4, evac)

            for l in range(L):
                for u in range(U[f"qkv{l}"], U[f"qkv{l}"] + 18):
                    low(u + 2)
                stream(U[f"bbb{l}"], 12, 4, nothing)
                stream(U[f"gate{l}"], 24, 4, nothing)
                attention1("a", l, 0)
                short_conv(l)
                attention1("c", l, 8)
                u0 = U[f"merge{l}"]

                def evac_m(j, i):
                    br, m = j % 3, 4 * i + j // 3
                    done(u0, j, i, 12)
                    ve.tensor_tensor(lg[:, br, :], gates[:, br * DT + m, :], bank(u0, j)[:, 0:S],
                                     ALU.mult).then_inc(read(u0, j), 1)
                    if br == 2:
                        dve.wait_ge(*after_at(u0, j, i, 12))
                        mg = lg[:, 3 + (j // 3) % 2, :]
                        chained(ve.tensor_tensor(lg[:, 0, :], lg[:, 0, :], lg[:, 1, :], ALU.add))
                        ve.tensor_tensor(mg, lg[:, 0, :], lg[:, 2, :], ALU.add).then_inc(s_val, 1)
                        ahi.wait(1)
                        rest(x1lo[:, m, :], mg, x1hi[:, m, :])
                stream(u0, 24, 12, evac_m, [(ahi, 4), (step, 4)])
                residual1(U[f"out{l}"], True)
                norm1(False)
                for c, n in enumerate(CHUNKS):
                    hidden(U[f"up{l}{c}"], n, 0, S, lambda k: lg[:, k, :], lambda k: lg[:, 2 + k, :], y1hi, y1lo)
                    residual1(U[f"down{l}{c}"], c == 0)
                norm1(l == L - 1)
            dve.wait_ge(s_mid, DT)

            def norm2(l, which, c0):
                if which is not None:
                    w = 3 * which
                    gn = p2(("g_ffn1", "g_mix", "g_ffn2")[which], l, DT)
                    chained(ve.scalar_tensor_tensor(scl[:, which, :, :], mods(l, w + 1), 1.0,
                                                    gn.unsqueeze(2).to_broadcast([P, DT, 2]), ALU.add, ALU.mult))
                    if which != 1:
                        chained(ve.tensor_scalar(hgt[:, which // 2, :, :], mods(l, w + 2), 0.5, None, ALU.mult))
                aval.wait(1)
                chained(ve.reciprocal(rs2[:, c0:T2], rs2[:, c0:T2]))
                for m in range(DT):
                    if which is None:
                        ve.scalar_tensor_tensor(big1[:, m, c0:T2], h[:, m, c0:T2], p2("g_final", 0, DT)[:, m:m + 1],
                                                rs2[:, c0:T2], ALU.mult, ALU.mult).then_inc(s_outv, 1)
                    else:
                        ve.tensor_tensor(big1[:, m, c0:T2], h[:, m, c0:T2], rs2[:, c0:T2],
                                         ALU.mult).then_inc(s_val, 1)
                if which is None:
                    return
                for m in range(DT):
                    ahi.wait(1)
                    rest(ulo[:, m, c0:T2], big1[:, m, c0:T2], uhi[:, m, c0:T2])

            def update(u0, c0, gate):
                def evac(j, i):
                    done(u0, j, i, 4)
                    m = 4 * i + j
                    for s in range(c0 // S, 2):
                        cols = slice(s * S, (s + 1) * S)
                        ins = ve.scalar_tensor_tensor(h[:, m, cols], bank(u0, j)[:, cols], gate(m, s), h[:, m, cols],
                                                      ALU.mult, ALU.add)
                    ins.then_inc(read(u0, j), 1)
                stream(u0, 8, 4, evac)

            def one_of(ap):
                return ap

            def ffn2(l, f, c0):
                for c, n in enumerate(CHUNKS):
                    hidden(U[f"fup{f}{l}{c}"], n, c0, T2, lambda k: pp[:, k, :], lambda k: pp[:, 2 + k, :], yhi, ylo)
                    update(U[f"fdown{f}{l}{c}"], c0,
                           lambda m, s: hgt[:, int(f) - 1, :, :].rearrange("p t s -> p (t s)")[:, bass.ds(2 * m + s, 1)])

            def low_norm(src, n, c0, dst, g):
                aval.wait(1)
                chained(ve.reciprocal(rs2[:, c0:T2], rs2[:, c0:T2]))
                for m in range(n):
                    ve.scalar_tensor_tensor(src[:, m, c0:T2], src[:, m, c0:T2], g[:, m:m + 1], rs2[:, c0:T2],
                                            ALU.mult, ALU.mult).then_inc(s_val, 1)
                for m in range(n):
                    ahi.wait(1)
                    rest(ylo[:, dst[m], c0:T2], src[:, m, c0:T2], yhi[:, dst[m], c0:T2])

            def attention2(s):
                nk = (s + 1) * S
                N = H * QT

                def bias(n):
                    score.wait(1)
                    chained(ve.tensor_reduce(small[:, 0, n:n + 1], banks[4 + n % 2][:, 0:nk], AX_X, ALU.max))
                    ve.tensor_scalar(small[:, 1, n:n + 1], small[:, 0, n:n + 1], -QK ** -0.5, None,
                                     ALU.mult).then_inc(s_val, 1)
                bias(0)
                bias(1)
                for n in range(N + 1):
                    if n < N:
                        aval.wait(1)
                        chained(ve.reciprocal(small[:, 3, n:n + 1], small[:, 2, n:n + 1]))
                        ve.tensor_scalar(pp[:, n % 2, 0:nk], pp[:, n % 2, 0:nk], small[:, 3, n:n + 1], None,
                                         ALU.mult).then_inc(s_prob, 1)
                    if n + 2 < N:
                        bias(n + 2)
                    if n and n % 4 == 0:
                        ahi.wait(1)
                        j = n // 4 - 1
                        rest(ylo[:, CT + j, s * S:(s + 1) * S], banks[j][:, 0:S], yhi[:, CT + j, s * S:(s + 1) * S])

            for l in range(L):
                last = l == L - 1
                c0 = S if last else 0
                norm2(l, 0, 0)
                ffn2(l, "1", 0)
                norm2(l, 1, 0)
                u0 = U[f"mix{l}"]
                if l == 0:
                    dve.wait_ge(s_used, u0 + 1)
                    step.add(ve.memset(vpad[:, :, :, :], 0.0))
                for j in range(16):
                    low(u0 + j + 2)
                    if j >= 13:
                        dve.wait_ge(*after(u0 + j))
                        s0 = c0 // S
                        step.add(ve.tensor_tensor(
                            vpad[:, j - 13, s0:2, PAD:PAD + S],
                            big2[:, 4 + j - 13, c0:T2].rearrange("p (s t) -> p s t", t=S),
                            acc[:, j - 13, c0:T2].rearrange("p (s t) -> p s t", t=S), ALU.mult))
                for n in range(FG * (2 - c0 // S)):
                    g, s = n % FG, n // FG + c0 // S
                    ahi.wait(1)
                    rest(ylo[:, CT + 4 + g, s * S:(s + 1) * S], banks[6 + n % 2][:, 0:S],
                         yhi[:, CT + 4 + g, s * S:(s + 1) * S])
                low_norm(big1, KVT, 0, [3, 4], p2("g_kvnorm", l, KVT))
                low_norm(vt, QLT, c0, [5, 6, 0], p2("g_qnorm", l, QLT))
                rot.wait(1)
                chained(ve.tensor_tensor(big1[HD:QK, 6, 0:S], vt[HD:QK, 3, S:T2], cos, ALU.mult))
                chained(ve.tensor_tensor(big1[HD:QK, 7, 0:S], banks[5][HD:QK, 0:S], sin, ALU.mult))
                ve.tensor_tensor(big1[HD:QK, 6, 0:S], big1[HD:QK, 6, 0:S], big1[HD:QK, 7, 0:S],
                                 ALU.add).then_inc(s_val, 1)
                for u in range(U[f"kv{l}"], U[f"kv{l}"] + 8 + H):
                    low(u + 2)
                rot.wait(1)
                bcast = lambda t, n: t.unsqueeze(1).to_broadcast([ROPE, n, S])
                for b in range(4):
                    step.add(ve.tensor_tensor(pp[HD:QK, b, :].rearrange("p (a t) -> p a t", a=2),
                                              banks[4 + b][HD:QK, :].rearrange("p (a t) -> p a t", a=2),
                                              bcast(sin, 2), ALU.mult))
                chained(ve.tensor_tensor(big1[HD:QK, :, S:T2], big1[HD:QK, :, S:T2], bcast(cos, H), ALU.mult))
                ve.tensor_tensor(big1[HD:QK, :, S:T2], big1[HD:QK, :, S:T2],
                                 pp[HD:QK, :, :].rearrange("p b (a t) -> p (b a) t", a=2), ALU.add).then_inc(s_dop, 1)
                wd = p2("w_dw", l, TAPS * CT)
                bd = p2("b_dw", l, CT)
                s0 = c0 // S
                for k in range(TAPS):
                    for m in range(CT):
                        a = acc[:, m, c0:T2].rearrange("p (s t) -> p s t", t=S)
                        v = vpad[:, m, s0:2, k:k + S]
                        wk = wd[:, k * CT + m:k * CT + m + 1]
                        dve.wait_ge(s_dve, step.n - (CT - 1) if k else step.n)
                        if k == 0:
                            step.add(ve.tensor_scalar(a, v, wk, bd[:, m:m + 1], ALU.mult, ALU.add))
                        else:
                            step.add(ve.scalar_tensor_tensor(a, v, wk, a, ALU.mult, ALU.add))
                step.wait()
                ve.memset(small[:, 4, :], 0.0).then_inc(s_dop, 1)
                for s in range(c0 // S, 2):
                    attention2(s)
                mean.wait(1)
                for m in range(CT):
                    ve.scalar_tensor_tensor(acc[:, m, c0:T2], banks[4][:, c0:T2], -1.0 / (CT * P), acc[:, m, c0:T2],
                                            ALU.mult, ALU.add).then_inc(s_val, 1)
                aval.wait(1)
                chained(ve.reciprocal(rs2[:, c0:T2], rs2[:, c0:T2]))
                for m in range(CT):
                    ve.tensor_tensor(acc[:, m, c0:T2], acc[:, m, c0:T2], rs2[:, c0:T2], ALU.mult).then_inc(s_val, 1)
                for m in range(CT):
                    ahi.wait(1)
                    rest(ylo[:, m, c0:T2], big1[:, m, c0:T2], yhi[:, m, c0:T2])

                u3 = U[f"bm{l}00"]
                by = {0: p2("b_pw", l, DT), 2: p2("b_four", l, DT)}

                def evac_m2(j, i):
                    if j % 2 == 0:
                        return
                    br, m = j % 6 // 2, 2 * i + j // 6
                    dve.wait_ge(*after_at(u3, j - 1, i, 12))
                    done(u3, j, i, 12)
                    bias = by[br][:, bass.ds(m, 1)] if br in by else 0.0
                    t = 3 * (j // 6)
                    ve.scalar_tensor_tensor(big2[:, t + br, c0:T2], bank(u3, j)[:, c0:T2], bias, pp[:, br, c0:T2],
                                            ALU.add, ALU.mult).then_inc(read(u3, j), 1)
                    if br == 2:
                        dve.wait_ge(*after_at(u3, j, i, 12))
                        chained(ve.tensor_tensor(big2[:, t, c0:T2], big2[:, t, c0:T2], big2[:, t + 1, c0:T2], ALU.add))
                        ve.tensor_tensor(big1[:, m, c0:T2], big2[:, t, c0:T2], big2[:, t + 2, c0:T2],
                                         ALU.add).then_inc(s_val, 1)
                stream(u3, 6 * DT, 12, evac_m2, [(step, 2)])
                for m in range(DT):
                    ahi.wait(1)
                    rest(ulo[:, m, c0:T2], big1[:, m, c0:T2], uhi[:, m, c0:T2])
                update(U[f"bout{l}"], c0,
                       lambda m, s: mod[:, l, :, :].rearrange("p t s -> p (t s)")[:, bass.ds(2 * (5 * DT + m) + s, 1)])
                norm2(l, 2, c0)
                ffn2(l, "2", c0)
            norm2(L - 1, None, S)

        @block.tensor
        def _(pe):
            te = nc.tensor
            split, sq, dop, aop, prob, pt, wd, sread_t = (Tally(pe, s) for s in
                                                          (s_split, s_sq, s_dop, s_aop, s_prob, s_pt, s_wide, s_sread))

            def unit(u0, j, i, per, hi, lo, c0, c1, ready=False):
                u = u0 + j
                pe.wait_ge(s_low, u + 1 + per * i)
                if plan.freed(u):
                    pe.wait_ge(s_free[u % SLOTS], plan.freed(u) + per // SLOTS * i)
                out_ = banks[u % SLOTS][:, c0:c1]
                for k in range(plan.kt[u]):
                    if ready:
                        split.wait(1)
                    w = slice(k * P, (k + 1) * P)
                    te.matmul(out_, whi[:, u % SLOTS, w], hi(k)[:, c0:c1], start=k == 0, stop=False)
                    te.matmul(out_, whi[:, u % SLOTS, w], lo(k)[:, c0:c1], start=False, stop=False)
                    ins = te.matmul(out_, wlo[:, u % SLOTS, w], hi(k)[:, c0:c1], start=False,
                                    stop=k == plan.kt[u] - 1)
                ins.then_inc(s_used, 1)

            def unit_v(u, hi, lo, tt):
                pe.wait_ge(s_low, u + 1)
                pe.wait_ge(s_free[u % SLOTS], plan.freed(u))
                for t in range(tt):
                    out_ = banks[u % SLOTS][:, t * P:(t + 1) * P]
                    rows_ = slice(t * P, (t + 1) * P)
                    for k in range(plan.kt[u]):
                        w = slice(k * P, (k + 1) * P)
                        te.matmul(out_, hi(k)[:, rows_], whi[:, u % SLOTS, w], start=k == 0, stop=False)
                        te.matmul(out_, lo(k)[:, rows_], whi[:, u % SLOTS, w], start=False, stop=False)
                        ins = te.matmul(out_, hi(k)[:, rows_], wlo[:, u % SLOTS, w], start=False,
                                        stop=k == plan.kt[u] - 1)
                ins.then_inc(s_used, 1)

            def stream(u0, n, per, hi, lo, c0, c1, ready=False):
                iters = n // per
                first = 0
                if ready:
                    for j in range(per):
                        unit(u0, j, 0, 0, lambda k: hi(j, k), lambda k: lo(j, k), c0, c1, ready=j == 0)
                    first = 1

                def body(i):
                    for j in range(per):
                        unit(u0 + first * per, j, i, per, lambda k: hi(j, k), lambda k: lo(j, k), c0, c1)
                repeat(pe, iters - first, body, [])

            tile = lambda t: (lambda j, k: t[:, k, :])

            pe.wait_ge(s_const, 7 * 16)
            dop.wait(1)
            for l in range(L):
                u0 = U[f"ada{l}"]
                acc_ = banks[4][:, 0:ADA_HALF]
                te.matmul(acc_, ones, blank[:, :], start=True, stop=False)

                def body(i):
                    for j in range(ADA_PER):
                        b, jj = j // (ADA_PER // 2), j % (ADA_PER // 2)
                        u = u0 + j
                        if jj == 0:
                            wd.wait(1)
                        pe.wait_ge(s_low, u + 1 + ADA_PER * i)
                        for half in range(2):
                            at = 4 * (ADA_N - 1 - 2 * jj - half)
                            cols = slice(half * ADA_HALF, (half + 1) * ADA_HALF)
                            for w in (whi, wlo):
                                ins = te.matmul(acc_, live[:, b, at:at + P], w[:, u % SLOTS, cols],
                                                start=False, stop=False)
                        ins.then_inc(s_used, 1)
                repeat(pe, DT // 2, body, [(wd, 2)])
                te.matmul(acc_, ones, blank[:, :], start=False, stop=True).then_inc(s_ada, 1)
                dop.wait(1)
                for j in range(ADA_J):
                    ins = te.matmul(banks[5][:, j * 2 * ADA_N:(j + 1) * 2 * ADA_N],
                                    rows[0:4 * ADA_N, j * P:(j + 1) * P], pick, start=True, stop=True)
                ins.then_inc(s_ada, 1)

            x1h, x1l = tile(x1hi), tile(x1lo)

            def attention1(kind, v, sr):
                def turn_(hh):
                    prob.wait(1)
                    b = banks[6 + hh % 2]
                    te.transpose(b[:, 0:P], lg[:, 2 * hh, 0:P], ident)
                    te.transpose(b[:, P:S], lg[:, 2 * hh + 1, 0:P], ident)
                    te.transpose(b[:, S + P:2 * S], lg[:, 2 * hh + 1, P:S], ident).then_inc(s_turned, 1)

                def outputs(hh):
                    pt.wait(1)
                    c = hh // 4 if kind == "a" else hh
                    r = slice(HD * (hh % 2), HD * (hh % 2) + HD)
                    b = banks[hh // 2]
                    te.matmul(b[r, 0:S], v[:, 0, c * HD:(c + 1) * HD], pt1[:, hh % 2, 0:S], start=True, stop=False)
                    ins = te.matmul(b[r, P:S], v[:, 1, c * HD:(c + 1) * HD], pt1[:, hh % 2, S + P:2 * S],
                                    start=False, stop=True)
                    if hh % 2:
                        ins.then_inc(s_head, 1)

                for hh in range(H):
                    if hh >= 2:
                        pe.wait_ge(s_sread, sr + hh - 1)
                    g, j = (hh // 4, hh % 4) if kind == "a" else (hh % 2, hh // 2)
                    q, k = (qa, ka[:, :]) if kind == "a" else (qc, kc[:, hh // 2, :])
                    r = slice(HD * g, HD * g + HD)
                    for qt in range(QT):
                        ins = te.matmul(banks[4 + hh % 2][:, qt * S:(qt + 1) * S], q[r, j, qt * P:(qt + 1) * P],
                                        k[r, :], start=True, stop=True)
                    ins.then_inc(s_score, 1)
                for hh in range(H + 1):
                    if hh < H:
                        turn_(hh)
                    if hh:
                        outputs(hh - 1)

            def norm1(u):
                for m in range(DT):
                    pe.wait_ge(*after(u + m))
                    ins = te.matmul(banks[4][:, 0:S], ones, x1[:, m, :], start=m == 0, stop=m == DT - 1)
                ins.then_inc(s_mean, 1)
                for m in range(DT):
                    if m % 2 == 0:
                        sq.wait(1)
                    ins = te.matmul(banks[5][:, 0:S], ones, lg[:, m, :], start=m == 0, stop=m == DT - 1)
                ins.then_inc(s_stat, 1)

            for l in range(L):
                u0 = U[f"qkv{l}"]
                hi_, lo_ = (lambda k: x1hi[:, k, :]), (lambda k: x1lo[:, k, :])
                for j in range(18):
                    if j == 5 or j >= 14:
                        unit_v(u0 + j, hi_, lo_, QT)
                    else:
                        unit(u0, j, 0, 0, hi_, lo_, 0, S, ready=j == 0)
                stream(U[f"bbb{l}"], 12, 4, x1h, x1l, 0, S)
                stream(U[f"gate{l}"], 24, 4, x1h, x1l, 0, S)
                pe.wait_ge(*after(U[f"gate{l}"] + 23))
                attention1("a", va, 2 * H * l)
                split.wait(4)
                attention1("c", vc, 2 * H * l + H)
                split.wait(1 + 4)
                stream(U[f"merge{l}"], 24, 12, lambda j, k: y1hi[:, 4 * (j % 3) + k, :],
                       lambda j, k: y1lo[:, 4 * (j % 3) + k, :], 0, S)
                stream(U[f"out{l}"], 8, 4, x1h, x1l, 0, S, ready=True)
                norm1(U[f"out{l}"])
                for c, n in enumerate(CHUNKS):
                    stream(U[f"up{l}{c}"], 2 * n, 4, x1h, x1l, 0, S, ready=c == 0)
                    stream(U[f"down{l}{c}"], 8, 4, tile(y1hi), tile(y1lo), 0, S, ready=True)
                norm1(U[f"down{l}{len(CHUNKS) - 1}"])

            u2h, u2l = tile(uhi), tile(ulo)

            def sums(bank_, n, c0, src):
                for m in range(n):
                    sq.wait(1)
                    ins = te.matmul(bank_[:, c0:T2], ones, src(m)[:, c0:T2], start=m == 0, stop=m == n - 1)
                ins.then_inc(s_stat, 1)

            def ffn2(l, f, c0):
                for c, n in enumerate(CHUNKS):
                    stream(U[f"fup{f}{l}{c}"], 2 * n, 4, u2h, u2l, c0, T2, ready=c == 0)
                    stream(U[f"fdown{f}{l}{c}"], 8, 4, tile(yhi), tile(ylo), c0, T2, ready=True)

            def attention2(s):
                nk = (s + 1) * S
                N = H * QT

                def scores(n):
                    hh, qt = n // QT, n % QT
                    q0 = s * S + qt * P
                    te.matmul(banks[4 + n % 2][:, 0:nk], big1[0:QK, hh, q0:q0 + P], big2[0:QK, hh, 0:nk],
                              start=True, stop=True).then_inc(s_score, 1)

                def turn_(n):
                    prob.wait(1)
                    for k in range(nk // P):
                        ins = te.transpose(banks[6 + n % 2][:, k * P:(k + 1) * P], pp[:, n % 2, k * P:(k + 1) * P], ident)
                    ins.then_inc(s_turned, 1)

                def outputs(n):
                    pt.wait(1)
                    hh, qt = n // QT, n % QT
                    r = slice(HD * (hh % 2), HD * (hh % 2) + HD)
                    for k in range(nk // P):
                        ins = te.matmul(banks[hh // 2][r, qt * P:(qt + 1) * P], vt[:, k, hh * HD:(hh + 1) * HD],
                                        pp[:, 2 + n % 2, k * P:(k + 1) * P], start=k == 0, stop=k == nk // P - 1)
                    if n % 4 == 3:
                        ins.then_inc(s_head, 1)
                scores(0)
                scores(1)
                for n in range(N + 1):
                    if n < N:
                        turn_(n)
                    if n:
                        outputs(n - 1)
                    if n + 2 < N:
                        scores(n + 2)
                split.wait(4)

            for l in range(L):
                last = l == L - 1
                c0 = S if last else 0
                sums(banks[4], DT, 0, lambda m: big1[:, m, :])
                ffn2(l, "1", 0)
                sums(banks[4], DT, 0, lambda m: big1[:, m, :])
                u0 = U[f"mix{l}"]
                for j in range(16):
                    unit(u0, j, 0, 0, lambda k: uhi[:, k, :], lambda k: ulo[:, k, :], 0 if 4 <= j < 7 or j == 0 else c0, T2,
                         ready=j == 0)
                pe.wait_ge(s_dft, 16 * (l + 1))
                pe.wait_ge(*after(u0 + 15))
                N = FG * (2 - c0 // S)
                for n in range(N + 1):
                    if n < N:
                        g, s = n % FG, n // FG + c0 // S
                        for t in range(QT):
                            q0 = s * S + t * P
                            ins = te.matmul(banks[4 + n % 2][:, t * S:(t + 1) * S], big2[:, g, q0:q0 + P],
                                            dft[:, 0:2 * P], start=True, stop=True)
                        ins.then_inc(s_stat, 1)
                    if n:
                        aop.wait(1)
                        if n > 2:
                            split.wait(1)
                        b = (n - 1) % 2
                        for t in range(QT):
                            for part in range(2):
                                at = 2 * P + (2 * t + part) * S
                                ins = te.matmul(banks[6 + b][:, 0:S],
                                                big1[:, 2 + b, t * S + part * P:t * S + (part + 1) * P],
                                                dft[:, at:at + S], start=t + part == 0, stop=t + part == 2)
                        ins.then_inc(s_head, 1)
                split.wait(2)
                sums(banks[4], KVT, 0, lambda m: big1[:, 4 + m, :])
                sums(banks[4], QLT, c0, lambda m: big1[:, 4 + m, :])
                te.matmul(banks[5][HD:QK, 0:S], turn, vt[HD:QK, 3, S:T2], start=True, stop=True).then_inc(s_rot, 1)
                u0 = U[f"kv{l}"]
                split.wait(KVT)
                kvh, kvl = (lambda k: yhi[:, 3 + k, :]), (lambda k: ylo[:, 3 + k, :])
                for j in range(8):
                    if j < 4:
                        unit(u0, j, 0, 0, kvh, kvl, 0, T2)
                    else:
                        unit_v(u0 + j, kvh, kvl, 4)
                u0 = U[f"q{l}"]
                split.wait(QLT)
                aop.wait(1)
                qt_ = [5, 6, 0]
                for j in range(H):
                    unit(u0, j, 0, 0, lambda k: yhi[:, qt_[k], :], lambda k: ylo[:, qt_[k], :], c0, T2)
                pe.wait_ge(*after(u0 + H - 1))
                for hh in range(H):
                    at = S * (hh % 2)
                    ins = te.matmul(banks[4 + hh // 2][HD:QK, at:at + S], turn, big1[HD:QK, hh, S:T2],
                                    start=True, stop=True)
                ins.then_inc(s_rot, 1)
                dop.wait(1)
                dop.wait(1)
                for s in range(c0 // S, 2):
                    attention2(s)
                for m in range(CT):
                    ins = te.matmul(banks[4][:, c0:T2], ones, acc[:, m, c0:T2], start=m == 0, stop=m == CT - 1)
                ins.then_inc(s_mean, 1)
                sums(banks[5], CT, c0, lambda m: big1[:, m, :])
                split.wait(CT)
                rows_of = ((uhi, ulo, 0), (yhi, ylo, 0), (uhi, ulo, 0), (yhi, ylo, CT), (uhi, ulo, 0), (yhi, ylo, CT + 4))
                stream(U[f"bm{l}00"], 6 * DT, 12, lambda j, k: rows_of[j % 6][0][:, rows_of[j % 6][2] + k, :],
                       lambda j, k: rows_of[j % 6][1][:, rows_of[j % 6][2] + k, :], c0, T2)
                stream(U[f"bout{l}"], 8, 4, u2h, u2l, c0, T2, ready=True)
                sums(banks[4], DT, c0, lambda m: big1[:, m, :])
                ffn2(l, "2", c0)
            sums(banks[4], DT, S, lambda m: big1[:, m, :])


def tiles(w, cols=P):
    k, n = w.shape
    return np.ascontiguousarray(w.reshape(k // P, P, n // cols, cols).transpose(2, 1, 0, 3)).reshape(n // cols, -1)


def by_feature(v):
    return np.moveaxis(v.reshape(v.shape[:-1] + (v.shape[-1] // P, P)), -1, 0).reshape(P, -1)


def weight_stream(a):
    out = []
    for l in range(L):
        w = a["w_ada_2"][l].reshape(DT, P, NADA * D // ADA_UNIT, ADA_UNIT)
        out.append(w.transpose(0, 2, 1, 3).reshape(-1))
    for l in range(L):
        w = a["w_in"][l]
        q = w[:, 0:512].reshape(D, 2, 4, HD).transpose(0, 2, 1, 3).reshape(D, 512)
        out += [tiles(q), tiles(w[:, 512:768]), tiles(w[:, 2304:3840]), tiles(w[:, 768:2304]), tiles(w[:, 3840:])]
        br = [tiles(a[f"w_branch_{x}"][l]) for x in "abc"]
        out += [b[m] for m in range(DT) for b in br]
        out.append(tiles(a["w_out"][l]))
        out += swiglu_units(a["w_ffn_gate"][l], a["w_ffn_up"][l], a["w_ffn_down"][l])
    for l in range(L):
        for f in "12":
            if f == "2":
                w = a["w_in_2"][l]
                kr = w[:, 1408:1440]
                out += [tiles(w[:, 1440:1952]), tiles(w[:, 1152:1408]), tiles(np.concatenate([kr] * 4, 1)),
                        tiles(w[:, 768:1152]), tiles(w[:, 0:768])]
                kv = a["w_ukv_2"][l].reshape(-1, H, 2, HD)
                out += [tiles(kv[:, :, 0].reshape(-1, H * HD)), tiles(kv[:, :, 1].reshape(-1, H * HD))]
                q = a["w_uq_2"][l].reshape(-1, H, QK)
                out.append(tiles(np.concatenate([q, q[:, :, HD:QK]], 2).reshape(-1, H * P)))
                g = tiles(a["w_bgate_2"][l])
                br = [tiles(a[x][l]) for x in ("w_pw_conv_2", "w_o_mla_2", "w_fourier_2")]
                out += [y for m in range(DT) for b in range(3) for y in (g[b * DT + m], br[b][m])]
                out.append(tiles(a["w_out_2"][l]))
            out += swiglu_units(a[f"w1_ffn{f}_2"][l], a[f"w3_ffn{f}_2"][l], a[f"w2_ffn{f}_2"][l])
    return np.concatenate([np.ascontiguousarray(o).reshape(-1) for o in out])


def swiglu_units(gate, up, down):
    g, u = tiles(gate), tiles(up)
    out, t = [], 0
    for n in CHUNKS:
        for m in range(t, t + n):
            out += [g[m], u[m]]
        out.append(tiles(down[t * P:(t + n) * P]))
        t += n
    return out


def constants():
    c0 = np.zeros((P, NCST0), np.float32)
    c0[:, 0:P] = np.eye(P)
    c0[:, P:2 * P] = 1.0
    c0[:, 2 * P], c0[:, 2 * P + 1] = LN_EPS, EPS
    q = (np.arange(QT)[None, :, None] * P + np.arange(P)[:, None, None])
    d = (q - np.arange(S)[None, None, :]).astype(np.float64)
    far = 1e30
    da = np.where((d >= 0) & (d < 128), d, far).reshape(P, -1)
    dc = np.where(d >= 0, d, far).reshape(P, -1)
    pick = np.zeros((P, 2 * ADA_N))
    for n in range(ADA_N):
        for r in range(4):
            pick[4 * n + r, 2 * n + r % 2] = 1.0
    c1 = np.concatenate([da, dc, pick], 1).astype(np.float32)
    ax = ROPE // 2
    t = np.arange(S)
    inv = 1.0 / (10000.0 ** (np.arange(ax // 2) * 2.0 / ax))
    ar, ac = (t // 64)[:, None] * inv, (t % 64)[:, None] * inv
    ang = np.concatenate([ar, ar, ac, ac], 1).T
    turn = np.zeros((ROPE, ROPE))
    for i in range(ROPE):
        first = i % ax < ax // 2
        turn[i + ax // 2 if first else i - ax // 2, i] = -1.0 if first else 1.0
    c2 = np.zeros((P, NCST2), np.float32)
    c2[HD:QK] = np.concatenate([np.cos(ang), np.sin(ang), turn], 1)
    a = 2 * np.pi * np.outer(np.arange(P), np.arange(P)) / P
    b = 2 * np.pi * np.outer(np.arange(S), np.arange(S)) / S
    tok = np.stack([np.cos(b), -np.sin(b)], 1) / np.sqrt(S)
    tok = tok.reshape(QT, P, 2, S).transpose(1, 0, 2, 3).reshape(P, -1)
    dft = np.concatenate([np.cos(a) / np.sqrt(P), np.sin(a) / np.sqrt(P), tok], 1)
    return c0, c1, c2, dft.astype(np.float32)


def layouts(a):
    def tokens(x):
        return np.ascontiguousarray(x.reshape(S, DT, P).transpose(2, 1, 0)).reshape(P, -1)

    c = np.stack([a["c_ctx_2"].reshape(DT, P), a["c_2"].reshape(DT, P)], -1).transpose(1, 0, 2).reshape(P, -1)
    sinks = np.broadcast_to(a["attn_sinks"].reshape(1, L, H, 1), (P, L, H, QT)).reshape(P, -1)
    par1 = np.concatenate([by_feature(a[n]) for n in ("ln1_g", "ln1_b", "ln2_g", "ln2_b", "conv_w")] +
                          [sinks, by_feature(a["b_ada_2"]), c], 1)
    par2 = np.concatenate([by_feature(a[n + "_2"]) for n in
                           ("g_ffn1", "g_mix", "g_ffn2", "w_dw", "b_dw", "ln_g_conv", "ln_b_conv", "b_pw_conv",
                            "g_qnorm", "g_kvnorm", "b_fourier", "b_bgate", "g_final")], 1)
    c0, c1, c2, dft = constants()
    return {"xT": tokens(a["x"]), "ctxT": tokens(a["ctx_2"]), "w_stream": weight_stream(a), "par1": par1,
            "par2": par2, "cst0": c0, "cst1": c1, "cst2": c2, "dft": dft}


def kernel(**inputs):
    import numpy as _np
    import concourse.bacc as _bacc
    from concourse import mybir as _mybir
    from concourse.bass_utils import run_bass_kernel_spmd as _run

    arrays = {k: _np.ascontiguousarray(v) for k, v in layouts({k: _np.asarray(v) for k, v in inputs.items()}).items()}
    nc = _bacc.Bacc("TRN2", target_bir_lowering=False, num_devices=1)
    args = [nc.dram_tensor(f"in_{n}", v.shape, _mybir.dt.from_np(v.dtype), kind="ExternalInput").ap()
            for n, v in arrays.items()]
    args.append(nc.dram_tensor("outT", (P, DT * S), _mybir.dt.float32, kind="ExternalOutput").ap())
    program(nc, *args)
    r = _run(nc, [{f"in_{n}": v for n, v in arrays.items()}], core_ids=[0])
    got = r.results[0]["outT"]
    return _np.ascontiguousarray(got.reshape(P, DT, S).transpose(2, 1, 0)).reshape(1, S, D)
```

```python
from contextlib import ExitStack

import numpy as np

import concourse.bass as bass
from concourse import mybir

ALU = mybir.AluOpType
ACT = mybir.ActivationFunctionType
F32 = mybir.dt.float32
F32R = mybir.dt.float32r
AX_X = mybir.AxisListType.X

P = 128
L = 2
D = 1024
DT = D // P
S = 256
QT = S // P
HD = 64
H = 8
FF = 2816
FT = FF // P
CHUNKS = [8, 8, FT - 16]
ALPHA = (2 * L) ** 0.25
LN_EPS = 1e-5
EPS = 1e-6

SLOTS = 4
SLOT = 8 * P

NADA = 9
CT = 3
TAPS = 31
PAD = TAPS // 2
ROPE = 32
QK = HD + ROPE
QLT, KVT = 3, 2
FG = 4

SLOPES = [2.0 ** (-8.0 * (i + 1.0) / (2 * H)) for i in range(2 * H)]


ADA_TILES = L * NADA * DT
BESIDE = {"up00": 2, "up01": 1, "up02": 1, "up10": 1, "up11": 1, "up12": 1, "fup100": 4, "fup101": 4, "fup102": 4,
          "fup200": 4, "fup201": 4, "fup202": 4, "fup110": 3, "fup111": 3, "fup112": 2}


def stages():
    out = []

    def swiglu(up, down):
        for c, n in enumerate(CHUNKS):
            out.append((f"{up}{c}", [8] * (2 * n)))
            out.append((f"{down}{c}", [n] * 8))

    for l in range(L):
        out.append((f"qkv{l}", [8] * 18))
        out.append((f"bbb{l}", [8] * 12))
        out.append((f"gate{l}", [8] * 24))
        out.append((f"merge{l}", [4] * 24))
        out.append((f"out{l}", [8] * 8))
        swiglu(f"up{l}", f"down{l}")
    for l in range(L):
        swiglu(f"fup1{l}", f"fdown1{l}")
        out.append((f"mix{l}", [8] * 16))
        out.append((f"kv{l}", [KVT] * 8))
        out.append((f"q{l}", [QLT] * H))
        out.append((f"bm{l}", [8, CT, 8, 4, 8, 4] * DT))
        out.append((f"bout{l}", [8] * 8))
        swiglu(f"fup2{l}", f"fdown2{l}")
    return out


class Plan:

    def __init__(self):
        self.start, self.count, self.kt, self.offset = {}, {}, [], []
        at = 0
        for name, units in stages():
            self.start[name], self.count[name] = len(self.kt), len(units)
            for kt in units:
                self.kt.append(kt)
                self.offset.append(at)
                at += P * kt * P
        self.units = len(self.kt)
        self.ada, at, loads = {}, 0, [0] * 4
        self.ada_end = []
        for name, n in BESIDE.items():
            iters = self.count[name] // SLOTS
            self.ada[name] = (at, n, tuple(loads), len(self.ada_end))
            self.ada_end += [at + n * (i + 1) for i in range(iters)]
            at += n * iters
            for s in range(n):
                loads[s] += iters
        assert at == ADA_TILES

    def ada_iterations(self, tiles):
        return sum(e < tiles for e in self.ada_end) + 1

    def freed(self, u):
        return u // SLOTS


class Tally:

    def __init__(self, eng, sem):
        self.eng, self.sem, self.n, self.per, self.it = eng, sem, 0, 0, 0

    def add(self, ins, k=1):
        ins.then_inc(self.sem, k)
        self.n += k
        return ins

    def wait(self, k=0):
        self.n += k
        self.eng.wait_ge(self.sem, self.n + self.per * self.it)

    def enter(self, it, per):
        self.it, self.per, self.at = it, per, self.n

    def leave(self, iters):
        assert self.n - self.at == self.per, (self.sem, self.n - self.at, self.per)
        self.n += self.per * (iters - 1)
        self.it = self.per = 0


def repeat(eng, iters, body, tallies):
    if iters <= 0:
        return
    if iters == 1:
        body(0)
        return
    with eng.Fori(0, iters) as i:
        for t, per in tallies:
            t.enter(i, per)
        body(i)
        for t, _ in tallies:
            t.leave(iters)


def columns(parts):
    out, at = {}, 0
    for name, n in parts:
        out[name] = (at, n)
        at += n
    return out, at


PAR1, NPAR1 = columns([("ln1_g", L * DT), ("ln1_b", L * DT), ("ln2_g", L * DT), ("ln2_b", L * DT),
                       ("conv_w", L * 3 * 4), ("sinks", L * H * QT)])
PAR2, NPAR2 = columns([("g_ffn1", L * DT), ("g_mix", L * DT), ("g_ffn2", L * DT), ("w_dw", L * TAPS * CT),
                       ("b_dw", L * CT), ("ln_g", L * CT), ("ln_b", L * CT), ("b_pw", L * DT),
                       ("g_qnorm", L * QLT), ("g_kvnorm", L * KVT), ("b_four", L * DT),
                       ("b_bgate", L * 3 * DT), ("g_final", DT), ("b_ada", L * NADA * DT)])
CST0, NCST0 = columns([("ident", P), ("ones", P), ("eps", 2)])
CST1, NCST1 = columns([("dist_a", QT * S), ("dist_c", QT * S)])
CST2, NCST2 = columns([("cos", S), ("sin", S), ("turn", ROPE)])
DFT, NDFT = columns([("chan", 2 * P), ("tok", QT * 2 * S)])


def program(nc, xT, ctxT, w_stream, w_ada, c_d, par1_d, par2_d, cst0_d, cst1_d, cst2_d, dft_d, out):
    plan = Plan()
    U = plan.start
    T2 = 2 * S

    with ExitStack() as ctx:
        def sem(name):
            return ctx.enter_context(nc.semaphore(name))

        def sb(where, name, shape, dt=F32):
            return where.enter_context(nc.sbuf_tensor(name, shape, dt))

        raw = sb(ctx, "raw", [P, SLOTS, SLOT])
        whi = sb(ctx, "whi", [P, SLOTS, SLOT], F32R)
        wlo = sb(ctx, "wlo", [P, SLOTS, SLOT], F32R)
        cst0 = sb(ctx, "cst0", [P, NCST0])
        cst2 = sb(ctx, "cst2", [P, NCST2])
        par2 = sb(ctx, "par2", [P, NPAR2])
        mod = sb(ctx, "mod", [P, L, NADA * DT, 2])
        h = sb(ctx, "h", [P, DT, T2])
        cs = sb(ctx, "cs", [P, 2, D])
        sums = sb(ctx, "ada_sums", [P, 8])
        small = sb(ctx, "small", [P, 5, H * QT])
        ident, ones = cst0[:, 0:P], cst0[:, P:2 * P]
        ln_eps, rms_eps = cst0[:, 2 * P:2 * P + 1], cst0[:, 2 * P + 1:2 * P + 2]

        one = ExitStack()
        gates = sb(one, "gates", [P, 24, S])
        qa = sb(one, "qa", [P, 4, S])
        ka = sb(one, "ka", [P, S])
        va = sb(one, "va", [P, QT, P])
        qc = sb(one, "qc", [P, 4, S])
        kc = sb(one, "kc", [P, 4, S])
        vc = sb(one, "vc", [P, QT, 4 * P])
        bbb = sb(one, "bbb", [P, 12, S])
        x1 = sb(one, "x1", [P, DT, S])
        x1hi = sb(one, "x1hi", [P, DT, S], F32R)
        x1lo = sb(one, "x1lo", [P, DT, S], F32R)
        y1hi = sb(one, "y1hi", [P, 12, S], F32R)
        y1lo = sb(one, "y1lo", [P, 12, S], F32R)
        lg = sb(one, "lg", [P, 2 * H, S])
        pt1 = sb(one, "pt1", [P, 2, QT * S])
        par1 = sb(one, "par1", [P, NPAR1])
        cst1 = sb(one, "cst1", [P, NCST1])
        one.close()

        two = ExitStack()
        uhi = sb(two, "uhi", [P, DT, T2], F32R)
        ulo = sb(two, "ulo", [P, DT, T2], F32R)
        yhi = sb(two, "yhi", [P, 9, T2], F32R)
        ylo = sb(two, "ylo", [P, 9, T2], F32R)
        big1 = sb(two, "big1", [P, DT, T2])
        big2 = sb(two, "big2", [P, DT, T2])
        vt = sb(two, "vt", [P, 4, T2])
        vpad = sb(two, "vpad", [P, CT, 2, S + 2 * PAD])
        acc = sb(two, "acc", [P, CT, T2])
        pp = sb(two, "pp", [P, 4, T2])
        scl = sb(two, "scl", [P, 3, DT, 2])
        hgt = sb(two, "hgt", [P, 2, DT, 2])
        two.close()
        three = ExitStack()
        sb(three, "ahead", [P, (2 * DT + 2 * 9 + DT + DT - 2) * T2])
        ychi = sb(three, "ychi", [P, CT, T2], F32R)
        yclo = sb(three, "yclo", [P, CT, T2], F32R)
        three.close()
        dft = pp[:, 0:3, :].rearrange("p a b -> p (a b)")
        rs1, rs2 = pt1[:, 0, 0:S], pp[:, 3, :]

        banks = [ctx.enter_context(nc.psum_tensor(f"bank{b}", [P, 512], F32)) for b in range(8)]

        def p1(name, l, n):
            at, _ = PAR1[name]
            return par1[:, at + l * n:at + (l + 1) * n]

        def p2(name, l, n):
            at, _ = PAR2[name]
            return par2[:, at + l * n:at + (l + 1) * n]

        def mods(l, n):
            return mod[:, l, n * DT:(n + 1) * DT, :]

        dist = {k: cst1[:, CST1[f"dist_{k}"][0]:CST1[f"dist_{k}"][0] + QT * S] for k in "ac"}
        cos, sin = cst2[HD:QK, 0:S], cst2[HD:QK, S:2 * S]
        turn = cst2[HD:QK, 2 * S:2 * S + ROPE]

        s_land = [sem(f"unit_landed{s}") for s in range(SLOTS)]
        s_high = sem("unit_high_ready")
        s_low = sem("unit_low_ready")
        s_used = sem("unit_used")
        s_free = [sem(f"bank_read{s}") for s in range(SLOTS)]
        s_ada_land = [sem(f"ada_landed{s}") for s in range(4)]
        s_ada_sum = sem("ada_sums_ready")
        s_ada_mod = sem("ada_modulation_ready")
        s_x = sem("x_landed")
        s_const = sem("constants_landed")
        s_c = sem("c_landed")
        s_dft = sem("dft_landed")
        s_out = sem("out_landed")
        s_dve = sem("dve_step")
        s_val = sem("dve_value_ready")
        s_dop = sem("dve_operand_ready")
        s_split = sem("act_split_ready")
        s_sread = sem("scores_read")
        s_prob = sem("probs_ready")
        s_outv = sem("out_ready")
        s_aval = sem("act_value_ready")
        s_mid = sem("first_block_out")
        s_ahi = sem("act_high_ready")
        s_sq = sem("squares_ready")
        s_aop = sem("act_operand_ready")
        s_pt = sem("turned_probs_ready")
        s_stat = sem("sum_ready")
        s_mean = sem("mean_ready")
        s_score = sem("scores_ready")
        s_turned = sem("probs_turned")
        s_head = sem("heads_ready")
        s_rot = sem("rotated_ready")
        ring1 = [gates[:, 4 * r:4 * r + 4, :] for r in range(2)]
        ring2 = [big2[:, 4:6, :], big2[:, 6:8, :], vt[:, 0:2, :], vt[:, 2:4, :]]
        waste1, waste2 = gates[:, 8:12, :], acc[:, 0:2, :]
        ring = lambda name: ring2 if name[0] == "f" else ring1
        block = ctx.enter_context(nc.Block())

        def after(u):
            return s_free[u % SLOTS], plan.freed(u) + 1

        def after_at(u0, j, i, per):
            u = u0 + j
            return s_free[u % SLOTS], plan.freed(u) + 1 + per // SLOTS * i

        @block.sync
        def _(sp):
            used = Tally(sp, s_used)

            def load(u, it=0, per=0):
                if u >= SLOTS:
                    sp.wait_ge(s_low, u - SLOTS + 1 + per * it)
                n = plan.kt[u] * P
                if per:
                    src = w_stream[bass.ds((plan.offset[u + per] - plan.offset[u]) * it + plan.offset[u], P * n)]
                else:
                    src = w_stream[plan.offset[u]:plan.offset[u] + P * n]
                sp.dma_start(raw[:, u % SLOTS, 0:n], src.rearrange("(p n) -> p n", p=P)).then_inc(s_land[u % SLOTS], 16)

            def run(u0, n, per):
                iters = n // per
                if iters > 1:
                    with sp.Fori(0, iters - 1) as i:
                        for j in range(per):
                            load(u0 + j, i, per)
                for u in range(u0 + max(iters - 1, 0) * per, u0 + n):
                    load(u)

            sp.dma_start(x1[:, :, :], xT.rearrange("p (t s) -> p t s", t=DT)).then_inc(s_x, 16)
            for u in range(SLOTS):
                load(u)
            sp.dma_start(par1[:, :], par1_d).then_inc(s_const, 16)
            sp.dma_start(cst0[:, :], cst0_d).then_inc(s_const, 16)
            sp.dma_start(cst1[:, :], cst1_d).then_inc(s_const, 16)
            sp.dma_start(cst2[:, :], cst2_d).then_inc(s_const, 16)
            sp.dma_start(par2[:, :], par2_d).then_inc(s_const, 16)
            sp.dma_start(h[:, :, 0:S], ctxT.rearrange("p (t s) -> p t s", t=DT)).then_inc(s_const, 16)
            for name, n in plan.count.items():
                per = 12 if name.startswith("bm") else SLOTS
                first = SLOTS if U[name] == 0 else 0
                run(U[name] + first, n - first, per)
                if name.startswith("mix"):
                    sp.wait_ge(s_used, U[name] + 1)
                    sp.dma_start(dft[:, 0:NDFT], dft_d).then_inc(s_dft, 16)
            for m in range(DT):
                sp.wait_ge(s_outv, m + 1)
                sp.dma_start(out[:, m * S:(m + 1) * S], big1[:, m, S:T2]).then_inc(s_out, 16)
            sp.wait_ge(s_out, 16 * DT)

        @block.gpsimd
        def _(pool):
            free = {"up00": ("merge0", 23), "up10": ("merge1", 23), "fup100": ("down12", 7),
                    "fup200": ("bout0", 0), "fup110": ("fdown202", 7)}
            pool.dma_start(cs[:, :, :], c_d.rearrange("p (s d) -> p s d", s=2)).then_inc(s_c, 16)
            for name, (first, per, _, _) in plan.ada.items():
                if name in free:
                    stage, j = free[name]
                    pool.wait_ge(*after(U[stage] + j))
                if name == "fup100":
                    pool.wait_ge(s_mid, DT)

                def load(r, i):
                    n = P * D
                    at = (first + r) * n
                    src = w_ada[at:at + n] if i is None else w_ada[bass.ds(per * n * i + at, n)]
                    to = ring(name)[r]
                    pool.dma_start(to, src.rearrange("(p a b) -> p a b", p=P,
                                                     a=to.shape[1])).then_inc(s_ada_land[r], 16)

                if first:
                    pool.wait_ge(s_ada_sum, 2 * first)
                for r in range(per):
                    load(r, None)
                with pool.Fori(1, plan.count[name] // SLOTS) as i:
                    for r in range(per):
                        pool.wait_ge(s_ada_sum, 2 * per * i + 2 * (first + r + 1 - per))
                        load(r, i)

        @block.scalar
        def _(act):
            val, stat, turned, head = (Tally(act, s) for s in (s_val, s_stat, s_turned, s_head))
            sc = nc.scalar

            def high(u, it=0, per=0):
                if u >= plan.units:
                    return
                act.wait_ge(s_land[u % SLOTS], 16 * (u // SLOTS + 1) + 16 * (per // SLOTS) * it)
                if u >= SLOTS:
                    act.wait_ge(s_used, u - SLOTS + 1 + per * it)
                n = plan.kt[u] * P
                sc.copy(whi[:, u % SLOTS, 0:n], raw[:, u % SLOTS, 0:n]).then_inc(s_high, 1)

            def stream(u0, n, per, evac, tallies=()):
                iters = n // per

                def body(i):
                    for j in range(per):
                        high(u0 + j + 2, i, per)
                        evac(j, i)

                repeat(act, iters - 1, body, tallies)
                for j in range(per):
                    high(u0 + n - per + j + 2)
                    evac(j, iters - 1)

            def done(u0, j, i, per):
                act.wait_ge(s_used, u0 + j + per * i + 1)

            def bank(u0, j):
                return banks[(u0 + j) % SLOTS]

            def read(u0, j):
                return s_free[(u0 + j) % SLOTS]

            high(0)
            high(1)
            act.wait_ge(s_x, 16)
            for m in range(DT):
                sc.copy(x1hi[:, m, :], x1[:, m, :]).then_inc(s_ahi, 1)
            act.wait_ge(s_const, 6 * 16)
            act.wait_ge(s_c, 16)
            sc.activation(cs[:, :, :], cs[:, :, :], ACT.Silu).then_inc(s_aval, 1)

            def attention1(kind, y0):
                val.wait(1)
                for n in range(H * QT):
                    sc.activation(lg[:, n, :], lg[:, n, :], ACT.Exp, bias=small[:, 1, n:n + 1],
                                  scale=HD ** -0.5, accum_out=small[:, 2, n:n + 1]).then_inc(s_aval, 1)
                if kind == "a":
                    sc.activation(small[:, 3, :], small[:, 4, :], ACT.Exp).then_inc(s_aval, 1)
                for n in range(H + 1):
                    if n < H:
                        turned.wait(1)
                        b = banks[6 + n % 2]
                        sc.copy(pt1[:, n % 2, 0:S], b[:, 0:S])
                        sc.copy(pt1[:, n % 2, S + P:2 * S], b[:, S + P:2 * S]).then_inc(s_pt, 1)
                    if n >= 1 and n % 2 == 0:
                        head.wait(1)
                        sc.copy(y1hi[:, y0 + n // 2 - 1, :], banks[n // 2 - 1][:, 0:S]).then_inc(s_ahi, 1)

            def hidden(stage, c, c0, c1, sg, hid, ht):
                u0 = U[f"{stage}{c}"]
                sc.preload_act_table(ACT.Silu)

                def evac(j, i):
                    k = j // 2
                    if j % 2 == 0:
                        done(u0, j, i, 4)
                        sc.activation(sg(k)[:, c0:c1], bank(u0, j)[:, c0:c1], ACT.Silu).then_inc(read(u0, j), 1)
                    else:
                        act.wait_ge(*after_at(u0, j, i, 4))
                        sc.copy(ht[:, 2 * i + k, c0:c1], hid(k)[:, c0:c1]).then_inc(s_ahi, 1)

                stream(u0, plan.count[f"{stage}{c}"], 4, evac)

            def norm1(g, b, last):
                for m in range(0, DT, 2):
                    val.wait(1)
                    sc.activation(lg[:, m:m + 2, :], x1[:, m:m + 2, :], ACT.Square).then_inc(s_sq, 1)
                stat.wait(1)
                sc.activation(rs1, banks[5][:, 0:S], ACT.Sqrt, bias=ln_eps, scale=1.0 / D).then_inc(s_aval, 1)
                for m in range(DT):
                    if m % 2 == 0:
                        val.wait(1)
                    gm, bm = g[:, m:m + 1], b[:, m:m + 1]
                    if last:
                        sc.activation(h[:, m, S:T2], lg[:, m, :], ACT.Identity, bias=bm, scale=gm).then_inc(s_mid, 1)
                    else:
                        sc.activation(x1hi[:, m, :], lg[:, m, :], ACT.Identity, bias=bm, scale=gm)
                        sc.activation(x1[:, m, :], lg[:, m, :], ACT.Identity, bias=bm, scale=gm).then_inc(s_ahi, 1)

            for l in range(L):
                u0 = U[f"qkv{l}"]
                dst = [qa[:, j, :] for j in range(4)] + [ka[:, :], None] + [qc[:, j, :] for j in range(4)] + \
                    [kc[:, j, :] for j in range(4)]
                for j in range(18):
                    high(u0 + j + 2)
                    done(u0, j, 0, 0)
                    if j == 5 or j >= 14:
                        v = va[:, :, :] if j == 5 else vc[:, :, (j - 14) * P:(j - 13) * P]
                        sc.copy(v, bank(u0, j)[:, 0:S].rearrange("p (t c) -> p t c", t=QT)).then_inc(read(u0, j), 1)
                    else:
                        sc.copy(dst[j], bank(u0, j)[:, 0:S]).then_inc(read(u0, j), 1)

                u1 = U[f"bbb{l}"]

                def evac_b(j, i):
                    done(u1, j, i, 4)
                    sc.copy(bbb[:, 4 * i + j, :], bank(u1, j)[:, 0:S]).then_inc(read(u1, j), 1)
                stream(u1, 12, 4, evac_b)

                u2 = U[f"gate{l}"]
                sc.preload_act_table(ACT.Sigmoid)

                def evac_g(j, i):
                    done(u2, j, i, 4)
                    sc.activation(gates[:, 4 * i + j, :], bank(u2, j)[:, 0:S], ACT.Sigmoid).then_inc(read(u2, j), 1)
                stream(u2, 24, 4, evac_g)

                attention1("a", 0)
                val.wait(1)
                sc.copy(y1hi[:, 4:8, :], bbb[:, 8:12, :]).then_inc(s_ahi, 1)
                attention1("c", 8)

                def evac_m(j, i):
                    if j % 3 == 2:
                        val.wait(1)
                        sc.copy(x1hi[:, 4 * i + j // 3, :], lg[:, 3 + (j // 3) % 2, :]).then_inc(s_ahi, 1)
                stream(U[f"merge{l}"], 24, 12, evac_m, [(val, 4)])
                stream(U[f"out{l}"], 8, 4, lambda j, i: None)
                norm1(p1("ln1_g", l, DT), p1("ln1_b", l, DT), False)
                for c, n in enumerate(CHUNKS):
                    hidden(f"up{l}", c, 0, S, lambda k: lg[:, k, :], lambda k: lg[:, 2 + k, :], y1hi)
                    stream(U[f"down{l}{c}"], 8, 4, lambda j, i: None)
                norm1(p1("ln2_g", l, DT), p1("ln2_b", l, DT), l == L - 1)

            act.wait_ge(s_mid, DT)

            def norm2(l, which, c0, ready):
                for m in range(DT):
                    if ready:
                        act.wait_ge(*after(ready + m))
                    sc.activation(big1[:, m, c0:T2], h[:, m, c0:T2], ACT.Square).then_inc(s_sq, 1)
                stat.wait(1)
                sc.activation(rs2[:, c0:T2], banks[4][:, c0:T2], ACT.Sqrt, bias=rms_eps,
                              scale=1.0 / D).then_inc(s_aval, 1)
                if which is None:
                    return
                for m in range(DT):
                    val.wait(1)
                    for s in range(c0 // S, 2):
                        bs = mods(l, 3 * which)[:, m, s:s + 1]
                        gs = scl[:, which, m, s:s + 1]
                        cols = slice(s * S, (s + 1) * S)
                        sc.activation(uhi[:, m, cols], big1[:, m, cols], ACT.Identity, bias=bs, scale=gs)
                        ins = sc.activation(big1[:, m, cols], big1[:, m, cols], ACT.Identity, bias=bs, scale=gs)
                    ins.then_inc(s_ahi, 1)

            def ffn2(l, f, c0):
                for c, n in enumerate(CHUNKS):
                    hidden(f"fup{f}{l}", c, c0, T2, lambda k: pp[:, k, :], lambda k: pp[:, 2 + k, :], yhi)
                    stream(U[f"fdown{f}{l}{c}"], 8, 4, lambda j, i: None)

            def low_norm(src, n, c0, dst, width):
                for m in range(n):
                    sc.activation(big1[:, 4 + m, c0:T2], src[:, m, c0:T2], ACT.Square).then_inc(s_sq, 1)
                stat.wait(1)
                sc.activation(rs2[:, c0:T2], banks[4][:, c0:T2], ACT.Sqrt, bias=rms_eps,
                              scale=1.0 / width).then_inc(s_aval, 1)
                for m in range(n):
                    val.wait(1)
                    sc.copy(yhi[:, dst[m], c0:T2], src[:, m, c0:T2]).then_inc(s_ahi, 1)

            def attention2(s):
                nk = (s + 1) * S
                N = H * QT

                def exp(n):
                    val.wait(1)
                    sc.activation(pp[:, n % 2, 0:nk], banks[4 + n % 2][:, 0:nk], ACT.Exp, bias=small[:, 1, n:n + 1],
                                  scale=QK ** -0.5, accum_out=small[:, 2, n:n + 1]).then_inc(s_aval, 1)
                exp(0)
                for n in range(N + 1):
                    if n + 1 < N:
                        exp(n + 1)
                    if n < N:
                        turned.wait(1)
                        sc.copy(pp[:, 2 + n % 2, 0:nk], banks[6 + n % 2][:, 0:nk]).then_inc(s_pt, 1)
                    if n and n % 4 == 0:
                        head.wait(1)
                        j = n // 4 - 1
                        sc.copy(yhi[:, j, s * S:(s + 1) * S], banks[j][:, 0:S]).then_inc(s_ahi, 1)

            for l in range(L):
                last = l == L - 1
                c0 = S if last else 0
                norm2(l, 0, 0, U[f"fdown2{l - 1}{len(CHUNKS) - 1}"] if l else 0)
                ffn2(l, "1", 0)
                norm2(l, 1, 0, U[f"fdown1{l}{len(CHUNKS) - 1}"])

                u0 = U[f"mix{l}"]
                for j in range(16):
                    high(u0 + j + 2)
                    done(u0, j, 0, 0)
                    cc = 0 if 4 <= j < 7 else c0
                    src = bank(u0, j)[:, cc:T2]
                    if j >= 13:
                        sc.activation(acc[:, j - 13, cc:T2], src, ACT.Sigmoid).then_inc(read(u0, j), 1)
                    else:
                        to = (big2[:, j, cc:T2] if j < 4 else big1[:, j - 4, cc:T2] if j < 6 else
                              vt[:, 3, cc:T2] if j == 6 else vt[:, j - 7, cc:T2] if j < 10 else
                              big2[:, 4 + j - 10, cc:T2])
                        sc.copy(to, src).then_inc(read(u0, j), 1)

                N = FG * (2 - c0 // S)
                for n in range(N + 1):
                    if n < N:
                        stat.wait(1)
                        sc.copy(big1[:, 2 + n % 2, :], banks[4 + n % 2][:, :]).then_inc(s_aop, 1)
                    if n:
                        g, s = (n - 1) % FG, (n - 1) // FG + c0 // S
                        head.wait(1)
                        sc.copy(yhi[:, 4 + g, s * S:(s + 1) * S],
                                banks[6 + (n - 1) % 2][:, 0:S]).then_inc(s_ahi, 1)

                low_norm(big1, KVT, 0, [0, 1], KVT * P)
                low_norm(vt, QLT, c0, [2, 3, 8], QLT * P)
                for s in range(2):
                    if s:
                        val.wait(1)
                    src = big1[HD:QK, 6, 0:S] if s else vt[HD:QK, 3, 0:S]
                    for hh in range(H):
                        ins = sc.copy(big2[HD:QK, hh, s * S:(s + 1) * S], src)
                ins.then_inc(s_aop, 1)

                u0 = U[f"kv{l}"]
                for j in range(8):
                    high(u0 + j + 2)
                    done(u0, j, 0, 0)
                    if j < 4:
                        sc.copy(big2[0:HD, 2 * j, :], bank(u0, j)[0:HD, :])
                        sc.copy(big2[0:HD, 2 * j + 1, :], bank(u0, j)[HD:P, :]).then_inc(read(u0, j), 1)
                    else:
                        sc.copy(vt[:, :, (j - 4) * P:(j - 3) * P],
                                bank(u0, j)[:, :].rearrange("p (t c) -> p t c", t=4)).then_inc(read(u0, j), 1)
                u0 = U[f"q{l}"]
                for j in range(H):
                    high(u0 + j + 2)
                    done(u0, j, 0, 0)
                    sc.copy(big1[0:QK, j, c0:T2], bank(u0, j)[0:QK, c0:T2]).then_inc(read(u0, j), 1)

                for s in range(c0 // S, 2):
                    attention2(s)

                for m in range(CT):
                    val.wait(1)
                    sc.activation(big1[:, m, c0:T2], acc[:, m, c0:T2], ACT.Square).then_inc(s_sq, 1)
                stat.wait(1)
                sc.activation(rs2[:, c0:T2], banks[5][:, c0:T2], ACT.Sqrt, bias=rms_eps,
                              scale=1.0 / (CT * P)).then_inc(s_aval, 1)
                lng, lnb = p2("ln_g", l, CT), p2("ln_b", l, CT)
                for m in range(CT):
                    val.wait(1)
                    sc.activation(ychi[:, m, c0:T2], acc[:, m, c0:T2], ACT.Silu, bias=lnb[:, m:m + 1],
                                  scale=lng[:, m:m + 1])
                    sc.activation(big1[:, m, c0:T2], acc[:, m, c0:T2], ACT.Silu, bias=lnb[:, m:m + 1],
                                  scale=lng[:, m:m + 1]).then_inc(s_ahi, 1)

                u3 = U[f"bm{l}"]
                bg = p2("b_bgate", l, 3 * DT)
                sc.preload_act_table(ACT.Sigmoid)

                def evac_g2(j, i):
                    if j % 2 == 0:
                        br, m = j % 6 // 2, 2 * i + j // 6
                        done(u3, j, i, 12)
                        sc.activation(pp[:, br, c0:T2], bank(u3, j)[:, c0:T2], ACT.Sigmoid,
                                      bias=bg[:, bass.ds(br * DT + m, 1)]).then_inc(read(u3, j), 1)
                stream(u3, 6 * DT, 12, evac_g2)
                for m in range(DT):
                    val.wait(1)
                    sc.copy(uhi[:, m, c0:T2], big1[:, m, c0:T2]).then_inc(s_ahi, 1)
                stream(U[f"bout{l}"], 8, 4, lambda j, i: None)
                norm2(l, 2, c0, U[f"bout{l}"])
                ffn2(l, "2", c0)
            norm2(L - 1, None, S, U[f"fdown2{L - 1}{len(CHUNKS) - 1}"])

        @block.vector
        def _(dve):
            ve = nc.vector
            step = Tally(dve, s_dve)
            aval, ahi, mean, score, rot = (Tally(dve, s) for s in (s_aval, s_ahi, s_mean, s_score, s_rot))

            def low(u, it=0, per=0):
                if u >= plan.units:
                    return
                dve.wait_ge(s_high, u + 1 + per * it)
                n = plan.kt[u] * P
                ve.tensor_tensor(wlo[:, u % SLOTS, 0:n], raw[:, u % SLOTS, 0:n],
                                 whi[:, u % SLOTS, 0:n].bitcast(F32), ALU.subtract).then_inc(s_low, 1)

            def stream(u0, n, per, evac, tallies=()):
                iters = n // per

                def body(i):
                    for j in range(per):
                        low(u0 + j + 2, i, per)
                        evac(j, i)

                repeat(dve, iters - 1, body, tallies)
                for j in range(per):
                    low(u0 + n - per + j + 2)
                    evac(j, iters - 1)

            def done(u0, j, i, per):
                dve.wait_ge(s_used, u0 + j + per * i + 1)

            def bank(u0, j):
                return banks[(u0 + j) % SLOTS]

            def read(u0, j):
                return s_free[(u0 + j) % SLOTS]

            def rest(dst, src, hi):
                ve.tensor_tensor(dst, src, hi.bitcast(F32), ALU.subtract).then_inc(s_split, 1)

            def chained(ins):
                step.add(ins)
                step.wait()

            nothing = lambda j, i: None
            low(0)
            low(1)
            for m in range(DT):
                ahi.wait(1)
                rest(x1lo[:, m, :], x1[:, m, :], x1hi[:, m, :])
            aval.wait(1)

            def ada(name, j, i):
                first, per, loads, before = plan.ada[name]
                for o in range(2 * per):
                    if o * 4 // (2 * per) != j:
                        continue
                    r, s = o // 2, o % 2
                    if s == 0:
                        dve.wait_ge(s_ada_land[r], 16 * i + 16 * (loads[r] + 1))
                    if o == 0 and not (isinstance(i, int) and before + i == 0):
                        dve.wait_ge(s_ada_mod, i + before)
                    if not (isinstance(i, int) and first + o + i == 0):
                        dve.wait_ge(s_ada_sum, 2 * per * i + (2 * first + o))
                    out_ = waste2 if name[0] == "f" else waste1
                    ve.tensor_tensor_reduce(out_, ring(name)[r],
                                            cs[:, s, :].rearrange("p (a b) -> p a b", a=out_.shape[1]), 1.0, 0.0,
                                            ALU.mult, ALU.add, sums[:, o:o + 1]).then_inc(s_ada_sum, 1)
                if j == 3:
                    dve.wait_ge(s_ada_sum, 2 * per * i + 2 * (first + per))
                    ve.tensor_tensor(
                        mod[:, :, :, :].rearrange("p l t s -> p (l t) s")[:, bass.ds(per * i + first, per), :],
                        sums[:, 0:2 * per].rearrange("p (t s) -> p t s", s=2),
                        par2[:, bass.ds(per * i + (first + PAR2["b_ada"][0]), per)].unsqueeze(2)
                        .to_broadcast([P, per, 2]), ALU.add).then_inc(s_ada_mod, 1)

            def attention1(kind, l, y0):
                for hh in range(H):
                    score.wait(1)
                    slope = SLOPES[hh if kind == "a" else H + hh]
                    step.add(ve.scalar_tensor_tensor(lg[:, 2 * hh:2 * hh + 2, :], dist[kind].rearrange("p (t s) -> p t s", t=2), -slope * HD ** 0.5,
                                                     banks[4 + hh % 2][:, :].rearrange("p (t s) -> p t s", t=2), ALU.mult, ALU.add))
                    step.wait()
                    ve.tensor_reduce(small[:, 0, 2 * hh:2 * hh + 2], lg[:, 2 * hh:2 * hh + 2, :], AX_X,
                                     ALU.max).then_inc(s_sread, 1)
                dve.wait_ge(s_sread, sread[0] + H)
                sread[0] += H
                if kind == "a":
                    sinks = p1("sinks", l, H * QT)
                    chained(ve.tensor_scalar(small[:, 3, :], sinks, HD ** 0.5, None, ALU.mult))
                    chained(ve.tensor_tensor(small[:, 0, :], small[:, 0, :], small[:, 3, :], ALU.max))
                    chained(ve.tensor_scalar(small[:, 1, :], small[:, 0, :], -HD ** -0.5, None, ALU.mult))
                    ve.tensor_tensor(small[:, 4, :], sinks, small[:, 1, :], ALU.add).then_inc(s_val, 1)
                else:
                    ve.tensor_scalar(small[:, 1, :], small[:, 0, :], -HD ** -0.5, None, ALU.mult).then_inc(s_val, 1)
                if kind == "a":
                    aval.wait(H * QT + 1)
                    chained(ve.tensor_tensor(small[:, 2, :], small[:, 2, :], small[:, 3, :], ALU.add))
                else:
                    aval.wait(H * QT)
                chained(ve.reciprocal(small[:, 2, :], small[:, 2, :]))
                for hh in range(H):
                    for n in (2 * hh, 2 * hh + 1):
                        ins = ve.tensor_scalar(lg[:, n, :], lg[:, n, :], small[:, 2, n:n + 1], None, ALU.mult)
                    ins.then_inc(s_prob, 1)
                for j in range(H // 2):
                    ahi.wait(1)
                    rest(y1lo[:, y0 + j, :], banks[j][:, 0:S], y1hi[:, y0 + j, :])

            sread = [0]

            def short_conv(l):
                chained(ve.tensor_tensor(bbb[:, 0:4, :], bbb[:, 0:4, :], bbb[:, 8:12, :], ALU.mult))
                w = p1("conv_w", l, 12)
                for k in (2, 1, 0):
                    d = 2 - k
                    for j in range(4):
                        wk = w[:, 4 * k + j:4 * k + j + 1]
                        if d == 0:
                            ins = ve.tensor_scalar(bbb[:, 8 + j, :], bbb[:, j, :], wk, None, ALU.mult)
                        else:
                            ins = ve.scalar_tensor_tensor(bbb[:, 8 + j, d:S], bbb[:, j, 0:S - d], wk,
                                                          bbb[:, 8 + j, d:S], ALU.mult, ALU.add)
                        step.add(ins)
                    step.wait()
                ve.tensor_tensor(bbb[:, 8:12, :], bbb[:, 8:12, :], bbb[:, 4:8, :], ALU.mult).then_inc(s_val, 1)
                ahi.wait(1)
                rest(y1lo[:, 4:8, :], bbb[:, 8:12, :], y1hi[:, 4:8, :])

            def hidden(stage, c, c0, c1, sg, hid, hi, lo):
                name = f"{stage}{c}"
                u0 = U[name]

                def evac(j, i):
                    k = j // 2
                    if j % 2:
                        dve.wait_ge(*after_at(u0, j - 1, i, 4))
                        done(u0, j, i, 4)
                        ve.tensor_tensor(hid(k)[:, c0:c1], sg(k)[:, c0:c1], bank(u0, j)[:, c0:c1],
                                         ALU.mult).then_inc(read(u0, j), 1)
                        ahi.wait(1)
                        rest(lo[:, 2 * i + k, c0:c1], hid(k)[:, c0:c1], hi[:, 2 * i + k, c0:c1])
                    if name in plan.ada:
                        ada(name, j, i)
                stream(u0, plan.count[name], 4, evac, [(ahi, 2)])

            def norm1(last):
                mean.wait(1)
                for m in range(0, DT, 2):
                    ve.scalar_tensor_tensor(x1[:, m:m + 2, :], banks[4][:, 0:S].unsqueeze(1).to_broadcast([P, 2, S]),
                                            -1.0 / D, x1[:, m:m + 2, :], ALU.mult, ALU.add).then_inc(s_val, 1)
                aval.wait(1)
                chained(ve.reciprocal(rs1, rs1))
                for m in range(0, DT, 2):
                    ve.tensor_tensor(lg[:, m:m + 2, :], x1[:, m:m + 2, :],
                                     rs1.unsqueeze(1).to_broadcast([P, 2, S]), ALU.mult).then_inc(s_val, 1)
                if last:
                    return
                for m in range(DT):
                    ahi.wait(1)
                    rest(x1lo[:, m, :], x1[:, m, :], x1hi[:, m, :])

            def residual1(u0, first):
                def evac(j, i):
                    done(u0, j, i, 4)
                    m = 4 * i + j
                    if first:
                        ins = ve.scalar_tensor_tensor(x1[:, m, :], x1[:, m, :], ALPHA, bank(u0, j)[:, 0:S],
                                                      ALU.mult, ALU.add)
                    else:
                        ins = ve.tensor_tensor(x1[:, m, :], x1[:, m, :], bank(u0, j)[:, 0:S], ALU.add)
                    ins.then_inc(read(u0, j), 1)
                stream(u0, 8, 4, evac)

            for l in range(L):
                for u in range(U[f"qkv{l}"], U[f"qkv{l}"] + 18):
                    low(u + 2)
                stream(U[f"bbb{l}"], 12, 4, nothing)
                stream(U[f"gate{l}"], 24, 4, nothing)
                attention1("a", l, 0)
                short_conv(l)
                attention1("c", l, 8)
                u0 = U[f"merge{l}"]

                def evac_m(j, i):
                    br, m = j % 3, 4 * i + j // 3
                    done(u0, j, i, 12)
                    ve.tensor_tensor(lg[:, br, :], gates[:, br * DT + m, :], bank(u0, j)[:, 0:S],
                                     ALU.mult).then_inc(read(u0, j), 1)
                    if br == 2:
                        dve.wait_ge(*after_at(u0, j, i, 12))
                        mg = lg[:, 3 + (j // 3) % 2, :]
                        chained(ve.tensor_tensor(lg[:, 0, :], lg[:, 0, :], lg[:, 1, :], ALU.add))
                        ve.tensor_tensor(mg, lg[:, 0, :], lg[:, 2, :], ALU.add).then_inc(s_val, 1)
                        ahi.wait(1)
                        rest(x1lo[:, m, :], mg, x1hi[:, m, :])
                stream(u0, 24, 12, evac_m, [(ahi, 4), (step, 4)])
                residual1(U[f"out{l}"], True)
                norm1(False)
                for c, n in enumerate(CHUNKS):
                    hidden(f"up{l}", c, 0, S, lambda k: lg[:, k, :], lambda k: lg[:, 2 + k, :], y1hi, y1lo)
                    residual1(U[f"down{l}{c}"], c == 0)
                norm1(l == L - 1)
            dve.wait_ge(s_mid, DT)

            def norm2(l, which, c0):
                if which is not None:
                    w = 3 * which
                    dve.wait_ge(s_ada_mod, plan.ada_iterations(DT * (NADA * l + w + 2)))
                    gn = p2(("g_ffn1", "g_mix", "g_ffn2")[which], l, DT)
                    chained(ve.scalar_tensor_tensor(scl[:, which, :, :], mods(l, w + 1), 1.0,
                                                    gn.unsqueeze(2).to_broadcast([P, DT, 2]), ALU.add, ALU.mult))
                aval.wait(1)
                chained(ve.reciprocal(rs2[:, c0:T2], rs2[:, c0:T2]))
                for m in range(DT):
                    if which is None:
                        ve.scalar_tensor_tensor(big1[:, m, c0:T2], h[:, m, c0:T2], p2("g_final", 0, DT)[:, m:m + 1],
                                                rs2[:, c0:T2], ALU.mult, ALU.mult).then_inc(s_outv, 1)
                    else:
                        ve.tensor_tensor(big1[:, m, c0:T2], h[:, m, c0:T2], rs2[:, c0:T2],
                                         ALU.mult).then_inc(s_val, 1)
                if which is None:
                    return
                for m in range(DT):
                    ahi.wait(1)
                    rest(ulo[:, m, c0:T2], big1[:, m, c0:T2], uhi[:, m, c0:T2])

            def update(u0, c0, gate):
                def evac(j, i):
                    done(u0, j, i, 4)
                    m = 4 * i + j
                    for s in range(c0 // S, 2):
                        cols = slice(s * S, (s + 1) * S)
                        ins = ve.scalar_tensor_tensor(h[:, m, cols], bank(u0, j)[:, cols], gate(m, s), h[:, m, cols],
                                                      ALU.mult, ALU.add)
                    ins.then_inc(read(u0, j), 1)
                stream(u0, 8, 4, evac)

            def ffn2(l, f, c0):
                for c, n in enumerate(CHUNKS):
                    hidden(f"fup{f}{l}", c, c0, T2, lambda k: pp[:, k, :], lambda k: pp[:, 2 + k, :], yhi, ylo)
                    if c == 0:
                        part = {"1": 2, "2": 8}[f]
                        dve.wait_ge(s_ada_mod, plan.ada_iterations(DT * (NADA * l + part + 1)))
                        chained(ve.tensor_scalar(hgt[:, int(f) - 1, :, :], mods(l, part), 0.5, None, ALU.mult))
                    update(U[f"fdown{f}{l}{c}"], c0,
                           lambda m, s: hgt[:, int(f) - 1, :, :].rearrange("p t s -> p (t s)")[:, bass.ds(2 * m + s, 1)])

            def low_norm(src, n, c0, dst, g):
                aval.wait(1)
                chained(ve.reciprocal(rs2[:, c0:T2], rs2[:, c0:T2]))
                for m in range(n):
                    ve.scalar_tensor_tensor(src[:, m, c0:T2], src[:, m, c0:T2], g[:, m:m + 1], rs2[:, c0:T2],
                                            ALU.mult, ALU.mult).then_inc(s_val, 1)
                for m in range(n):
                    ahi.wait(1)
                    rest(ylo[:, dst[m], c0:T2], src[:, m, c0:T2], yhi[:, dst[m], c0:T2])

            def attention2(s):
                nk = (s + 1) * S
                N = H * QT

                def bias(n):
                    score.wait(1)
                    chained(ve.tensor_reduce(small[:, 0, n:n + 1], banks[4 + n % 2][:, 0:nk], AX_X, ALU.max))
                    ve.tensor_scalar(small[:, 1, n:n + 1], small[:, 0, n:n + 1], -QK ** -0.5, None,
                                     ALU.mult).then_inc(s_val, 1)
                bias(0)
                bias(1)
                for n in range(N + 1):
                    if n < N:
                        aval.wait(1)
                        chained(ve.reciprocal(small[:, 3, n:n + 1], small[:, 2, n:n + 1]))
                        ve.tensor_scalar(pp[:, n % 2, 0:nk], pp[:, n % 2, 0:nk], small[:, 3, n:n + 1], None,
                                         ALU.mult).then_inc(s_prob, 1)
                    if n + 2 < N:
                        bias(n + 2)
                    if n and n % 4 == 0:
                        ahi.wait(1)
                        j = n // 4 - 1
                        rest(ylo[:, j, s * S:(s + 1) * S], banks[j][:, 0:S], yhi[:, j, s * S:(s + 1) * S])

            for l in range(L):
                last = l == L - 1
                c0 = S if last else 0
                norm2(l, 0, 0)
                ffn2(l, "1", 0)
                norm2(l, 1, 0)
                u0 = U[f"mix{l}"]
                if l == 0:
                    dve.wait_ge(s_used, u0 + 1)
                    step.add(ve.memset(vpad[:, :, :, :], 0.0))
                for j in range(16):
                    low(u0 + j + 2)
                    if j >= 13:
                        dve.wait_ge(*after(u0 + j))
                        s0 = c0 // S
                        step.add(ve.tensor_tensor(
                            vpad[:, j - 13, s0:2, PAD:PAD + S],
                            big2[:, 4 + j - 13, c0:T2].rearrange("p (s t) -> p s t", t=S),
                            acc[:, j - 13, c0:T2].rearrange("p (s t) -> p s t", t=S), ALU.mult))
                for n in range(FG * (2 - c0 // S)):
                    g, s = n % FG, n // FG + c0 // S
                    ahi.wait(1)
                    rest(ylo[:, 4 + g, s * S:(s + 1) * S], banks[6 + n % 2][:, 0:S],
                         yhi[:, 4 + g, s * S:(s + 1) * S])
                low_norm(big1, KVT, 0, [0, 1], p2("g_kvnorm", l, KVT))
                low_norm(vt, QLT, c0, [2, 3, 8], p2("g_qnorm", l, QLT))
                rot.wait(1)
                chained(ve.tensor_tensor(big1[HD:QK, 6, 0:S], vt[HD:QK, 3, S:T2], cos, ALU.mult))
                chained(ve.tensor_tensor(big1[HD:QK, 7, 0:S], banks[5][HD:QK, 0:S], sin, ALU.mult))
                ve.tensor_tensor(big1[HD:QK, 6, 0:S], big1[HD:QK, 6, 0:S], big1[HD:QK, 7, 0:S],
                                 ALU.add).then_inc(s_val, 1)
                for u in range(U[f"kv{l}"], U[f"kv{l}"] + 8 + H):
                    low(u + 2)
                rot.wait(1)
                bcast = lambda t, n: t.unsqueeze(1).to_broadcast([ROPE, n, S])
                for b in range(4):
                    step.add(ve.tensor_tensor(pp[HD:QK, b, :].rearrange("p (a t) -> p a t", a=2),
                                              banks[4 + b][HD:QK, :].rearrange("p (a t) -> p a t", a=2),
                                              bcast(sin, 2), ALU.mult))
                chained(ve.tensor_tensor(big1[HD:QK, :, S:T2], big1[HD:QK, :, S:T2], bcast(cos, H), ALU.mult))
                ve.tensor_tensor(big1[HD:QK, :, S:T2], big1[HD:QK, :, S:T2],
                                 pp[HD:QK, :, :].rearrange("p b (a t) -> p (b a) t", a=2), ALU.add).then_inc(s_dop, 1)
                wd = p2("w_dw", l, TAPS * CT)
                bd = p2("b_dw", l, CT)
                s0 = c0 // S
                for k in range(TAPS):
                    for m in range(CT):
                        a = acc[:, m, c0:T2].rearrange("p (s t) -> p s t", t=S)
                        v = vpad[:, m, s0:2, k:k + S]
                        wk = wd[:, k * CT + m:k * CT + m + 1]
                        dve.wait_ge(s_dve, step.n - (CT - 1) if k else step.n)
                        if k == 0:
                            step.add(ve.tensor_scalar(a, v, wk, bd[:, m:m + 1], ALU.mult, ALU.add))
                        else:
                            step.add(ve.scalar_tensor_tensor(a, v, wk, a, ALU.mult, ALU.add))
                step.wait()
                ve.memset(small[:, 4, :], 0.0).then_inc(s_dop, 1)
                for s in range(c0 // S, 2):
                    attention2(s)
                mean.wait(1)
                for m in range(CT):
                    ve.scalar_tensor_tensor(acc[:, m, c0:T2], banks[4][:, c0:T2], -1.0 / (CT * P), acc[:, m, c0:T2],
                                            ALU.mult, ALU.add).then_inc(s_val, 1)
                aval.wait(1)
                chained(ve.reciprocal(rs2[:, c0:T2], rs2[:, c0:T2]))
                for m in range(CT):
                    ve.tensor_tensor(acc[:, m, c0:T2], acc[:, m, c0:T2], rs2[:, c0:T2], ALU.mult).then_inc(s_val, 1)
                for m in range(CT):
                    ahi.wait(1)
                    rest(yclo[:, m, c0:T2], big1[:, m, c0:T2], ychi[:, m, c0:T2])

                u3 = U[f"bm{l}"]
                by = {0: p2("b_pw", l, DT), 2: p2("b_four", l, DT)}

                def evac_m2(j, i):
                    if j % 2 == 0:
                        return
                    br, m = j % 6 // 2, 2 * i + j // 6
                    dve.wait_ge(*after_at(u3, j - 1, i, 12))
                    done(u3, j, i, 12)
                    bias = by[br][:, bass.ds(m, 1)] if br in by else 0.0
                    t = 3 * (j // 6)
                    ve.scalar_tensor_tensor(big2[:, t + br, c0:T2], bank(u3, j)[:, c0:T2], bias, pp[:, br, c0:T2],
                                            ALU.add, ALU.mult).then_inc(read(u3, j), 1)
                    if br == 2:
                        dve.wait_ge(*after_at(u3, j, i, 12))
                        chained(ve.tensor_tensor(big2[:, t, c0:T2], big2[:, t, c0:T2], big2[:, t + 1, c0:T2], ALU.add))
                        ve.tensor_tensor(big1[:, m, c0:T2], big2[:, t, c0:T2], big2[:, t + 2, c0:T2],
                                         ALU.add).then_inc(s_val, 1)
                stream(u3, 6 * DT, 12, evac_m2, [(step, 2)])
                for m in range(DT):
                    ahi.wait(1)
                    rest(ulo[:, m, c0:T2], big1[:, m, c0:T2], uhi[:, m, c0:T2])
                update(U[f"bout{l}"], c0,
                       lambda m, s: mod[:, l, :, :].rearrange("p t s -> p (t s)")[:, bass.ds(2 * (5 * DT + m) + s, 1)])
                norm2(l, 2, c0)
                ffn2(l, "2", c0)
            norm2(L - 1, None, S)

        @block.tensor
        def _(pe):
            te = nc.tensor
            split, sq, dop, aop, prob, pt = (Tally(pe, s) for s in (s_split, s_sq, s_dop, s_aop, s_prob, s_pt))

            def unit(u0, j, i, per, hi, lo, c0, c1, ready=False):
                u = u0 + j
                pe.wait_ge(s_low, u + 1 + per * i)
                if plan.freed(u):
                    pe.wait_ge(s_free[u % SLOTS], plan.freed(u) + per // SLOTS * i)
                out_ = banks[u % SLOTS][:, c0:c1]
                for k in range(plan.kt[u]):
                    if ready:
                        split.wait(1)
                    w = slice(k * P, (k + 1) * P)
                    te.matmul(out_, whi[:, u % SLOTS, w], hi(k)[:, c0:c1], start=k == 0, stop=False)
                    te.matmul(out_, whi[:, u % SLOTS, w], lo(k)[:, c0:c1], start=False, stop=False)
                    ins = te.matmul(out_, wlo[:, u % SLOTS, w], hi(k)[:, c0:c1], start=False,
                                    stop=k == plan.kt[u] - 1)
                ins.then_inc(s_used, 1)

            def unit_v(u, hi, lo, tt):
                pe.wait_ge(s_low, u + 1)
                pe.wait_ge(s_free[u % SLOTS], plan.freed(u))
                for t in range(tt):
                    out_ = banks[u % SLOTS][:, t * P:(t + 1) * P]
                    rows_ = slice(t * P, (t + 1) * P)
                    for k in range(plan.kt[u]):
                        w = slice(k * P, (k + 1) * P)
                        te.matmul(out_, hi(k)[:, rows_], whi[:, u % SLOTS, w], start=k == 0, stop=False)
                        te.matmul(out_, lo(k)[:, rows_], whi[:, u % SLOTS, w], start=False, stop=False)
                        ins = te.matmul(out_, hi(k)[:, rows_], wlo[:, u % SLOTS, w], start=False,
                                        stop=k == plan.kt[u] - 1)
                ins.then_inc(s_used, 1)

            def stream(u0, n, per, hi, lo, c0, c1, ready=False):
                iters = n // per
                first = 0
                if ready:
                    for j in range(per):
                        unit(u0, j, 0, 0, lambda k: hi(j, k), lambda k: lo(j, k), c0, c1, ready=j == 0)
                    first = 1

                def body(i):
                    for j in range(per):
                        unit(u0 + first * per, j, i, per, lambda k: hi(j, k), lambda k: lo(j, k), c0, c1)
                repeat(pe, iters - first, body, [])

            tile = lambda t: (lambda j, k: t[:, k, :])

            pe.wait_ge(s_const, 6 * 16)
            x1h, x1l = tile(x1hi), tile(x1lo)

            def attention1(kind, v, sr):
                def turn_(hh):
                    prob.wait(1)
                    b = banks[6 + hh % 2]
                    te.transpose(b[:, 0:P], lg[:, 2 * hh, 0:P], ident)
                    te.transpose(b[:, P:S], lg[:, 2 * hh + 1, 0:P], ident)
                    te.transpose(b[:, S + P:2 * S], lg[:, 2 * hh + 1, P:S], ident).then_inc(s_turned, 1)

                def outputs(hh):
                    pt.wait(1)
                    c = hh // 4 if kind == "a" else hh
                    r = slice(HD * (hh % 2), HD * (hh % 2) + HD)
                    b = banks[hh // 2]
                    te.matmul(b[r, 0:S], v[:, 0, c * HD:(c + 1) * HD], pt1[:, hh % 2, 0:S], start=True, stop=False)
                    ins = te.matmul(b[r, P:S], v[:, 1, c * HD:(c + 1) * HD], pt1[:, hh % 2, S + P:2 * S],
                                    start=False, stop=True)
                    if hh % 2:
                        ins.then_inc(s_head, 1)

                for hh in range(H):
                    if hh >= 2:
                        pe.wait_ge(s_sread, sr + hh - 1)
                    g, j = (hh // 4, hh % 4) if kind == "a" else (hh % 2, hh // 2)
                    q, k = (qa, ka[:, :]) if kind == "a" else (qc, kc[:, hh // 2, :])
                    r = slice(HD * g, HD * g + HD)
                    for qt in range(QT):
                        ins = te.matmul(banks[4 + hh % 2][:, qt * S:(qt + 1) * S], q[r, j, qt * P:(qt + 1) * P],
                                        k[r, :], start=True, stop=True)
                    ins.then_inc(s_score, 1)
                for hh in range(H + 1):
                    if hh < H:
                        turn_(hh)
                    if hh:
                        outputs(hh - 1)

            def norm1(u):
                for m in range(DT):
                    pe.wait_ge(*after(u + m))
                    ins = te.matmul(banks[4][:, 0:S], ones, x1[:, m, :], start=m == 0, stop=m == DT - 1)
                ins.then_inc(s_mean, 1)
                for m in range(DT):
                    if m % 2 == 0:
                        sq.wait(1)
                    ins = te.matmul(banks[5][:, 0:S], ones, lg[:, m, :], start=m == 0, stop=m == DT - 1)
                ins.then_inc(s_stat, 1)

            for l in range(L):
                u0 = U[f"qkv{l}"]
                hi_, lo_ = (lambda k: x1hi[:, k, :]), (lambda k: x1lo[:, k, :])
                for j in range(18):
                    if j == 5 or j >= 14:
                        unit_v(u0 + j, hi_, lo_, QT)
                    else:
                        unit(u0, j, 0, 0, hi_, lo_, 0, S, ready=j == 0)
                stream(U[f"bbb{l}"], 12, 4, x1h, x1l, 0, S)
                stream(U[f"gate{l}"], 24, 4, x1h, x1l, 0, S)
                pe.wait_ge(*after(U[f"gate{l}"] + 23))
                attention1("a", va, 2 * H * l)
                split.wait(4)
                attention1("c", vc, 2 * H * l + H)
                split.wait(1 + 4)
                stream(U[f"merge{l}"], 24, 12, lambda j, k: y1hi[:, 4 * (j % 3) + k, :],
                       lambda j, k: y1lo[:, 4 * (j % 3) + k, :], 0, S)
                stream(U[f"out{l}"], 8, 4, x1h, x1l, 0, S, ready=True)
                norm1(U[f"out{l}"])
                for c, n in enumerate(CHUNKS):
                    stream(U[f"up{l}{c}"], 2 * n, 4, x1h, x1l, 0, S, ready=c == 0)
                    stream(U[f"down{l}{c}"], 8, 4, tile(y1hi), tile(y1lo), 0, S, ready=True)
                norm1(U[f"down{l}{len(CHUNKS) - 1}"])

            u2h, u2l = tile(uhi), tile(ulo)

            def add_up(bank_, n, c0, src):
                for m in range(n):
                    sq.wait(1)
                    ins = te.matmul(bank_[:, c0:T2], ones, src(m)[:, c0:T2], start=m == 0, stop=m == n - 1)
                ins.then_inc(s_stat, 1)

            def ffn2(l, f, c0):
                for c, n in enumerate(CHUNKS):
                    stream(U[f"fup{f}{l}{c}"], 2 * n, 4, u2h, u2l, c0, T2, ready=c == 0)
                    stream(U[f"fdown{f}{l}{c}"], 8, 4, tile(yhi), tile(ylo), c0, T2, ready=True)

            def attention2(s):
                nk = (s + 1) * S
                N = H * QT

                def scores(n):
                    hh, qt = n // QT, n % QT
                    q0 = s * S + qt * P
                    te.matmul(banks[4 + n % 2][:, 0:nk], big1[0:QK, hh, q0:q0 + P], big2[0:QK, hh, 0:nk],
                              start=True, stop=True).then_inc(s_score, 1)

                def turn_(n):
                    prob.wait(1)
                    for k in range(nk // P):
                        ins = te.transpose(banks[6 + n % 2][:, k * P:(k + 1) * P], pp[:, n % 2, k * P:(k + 1) * P], ident)
                    ins.then_inc(s_turned, 1)

                def outputs(n):
                    pt.wait(1)
                    hh, qt = n // QT, n % QT
                    r = slice(HD * (hh % 2), HD * (hh % 2) + HD)
                    for k in range(nk // P):
                        ins = te.matmul(banks[hh // 2][r, qt * P:(qt + 1) * P], vt[:, k, hh * HD:(hh + 1) * HD],
                                        pp[:, 2 + n % 2, k * P:(k + 1) * P], start=k == 0, stop=k == nk // P - 1)
                    if n % 4 == 3:
                        ins.then_inc(s_head, 1)
                scores(0)
                scores(1)
                for n in range(N + 1):
                    if n < N:
                        turn_(n)
                    if n:
                        outputs(n - 1)
                    if n + 2 < N:
                        scores(n + 2)
                split.wait(4)

            for l in range(L):
                last = l == L - 1
                c0 = S if last else 0
                add_up(banks[4], DT, 0, lambda m: big1[:, m, :])
                ffn2(l, "1", 0)
                add_up(banks[4], DT, 0, lambda m: big1[:, m, :])
                u0 = U[f"mix{l}"]
                for j in range(16):
                    unit(u0, j, 0, 0, lambda k: uhi[:, k, :], lambda k: ulo[:, k, :], 0 if 4 <= j < 7 or j == 0 else c0, T2,
                         ready=j == 0)
                pe.wait_ge(s_dft, 16 * (l + 1))
                pe.wait_ge(*after(u0 + 15))
                N = FG * (2 - c0 // S)
                for n in range(N + 1):
                    if n < N:
                        g, s = n % FG, n // FG + c0 // S
                        for t in range(QT):
                            q0 = s * S + t * P
                            ins = te.matmul(banks[4 + n % 2][:, t * S:(t + 1) * S], big2[:, g, q0:q0 + P],
                                            dft[:, 0:2 * P], start=True, stop=True)
                        ins.then_inc(s_stat, 1)
                    if n:
                        aop.wait(1)
                        if n > 2:
                            split.wait(1)
                        b = (n - 1) % 2
                        for t in range(QT):
                            for part in range(2):
                                at = 2 * P + (2 * t + part) * S
                                ins = te.matmul(banks[6 + b][:, 0:S],
                                                big1[:, 2 + b, t * S + part * P:t * S + (part + 1) * P],
                                                dft[:, at:at + S], start=t + part == 0, stop=t + part == 2)
                        ins.then_inc(s_head, 1)
                split.wait(2)
                add_up(banks[4], KVT, 0, lambda m: big1[:, 4 + m, :])
                add_up(banks[4], QLT, c0, lambda m: big1[:, 4 + m, :])
                te.matmul(banks[5][HD:QK, 0:S], turn, vt[HD:QK, 3, S:T2], start=True, stop=True).then_inc(s_rot, 1)
                u0 = U[f"kv{l}"]
                split.wait(KVT)
                kvh, kvl = (lambda k: yhi[:, k, :]), (lambda k: ylo[:, k, :])
                for j in range(8):
                    if j < 4:
                        unit(u0, j, 0, 0, kvh, kvl, 0, T2)
                    else:
                        unit_v(u0 + j, kvh, kvl, 4)
                u0 = U[f"q{l}"]
                split.wait(QLT)
                aop.wait(1)
                qt_ = [2, 3, 8]
                for j in range(H):
                    unit(u0, j, 0, 0, lambda k: yhi[:, qt_[k], :], lambda k: ylo[:, qt_[k], :], c0, T2)
                pe.wait_ge(*after(u0 + H - 1))
                for hh in range(H):
                    at = S * (hh % 2)
                    ins = te.matmul(banks[4 + hh // 2][HD:QK, at:at + S], turn, big1[HD:QK, hh, S:T2],
                                    start=True, stop=True)
                ins.then_inc(s_rot, 1)
                dop.wait(1)
                dop.wait(1)
                for s in range(c0 // S, 2):
                    attention2(s)
                for m in range(CT):
                    ins = te.matmul(banks[4][:, c0:T2], ones, acc[:, m, c0:T2], start=m == 0, stop=m == CT - 1)
                ins.then_inc(s_mean, 1)
                add_up(banks[5], CT, c0, lambda m: big1[:, m, :])
                split.wait(CT)
                rows_of = ((uhi, ulo, 0), (ychi, yclo, 0), (uhi, ulo, 0), (yhi, ylo, 0), (uhi, ulo, 0), (yhi, ylo, 4))
                stream(U[f"bm{l}"], 6 * DT, 12, lambda j, k: rows_of[j % 6][0][:, rows_of[j % 6][2] + k, :],
                       lambda j, k: rows_of[j % 6][1][:, rows_of[j % 6][2] + k, :], c0, T2)
                stream(U[f"bout{l}"], 8, 4, u2h, u2l, c0, T2, ready=True)
                add_up(banks[4], DT, c0, lambda m: big1[:, m, :])
                ffn2(l, "2", c0)
            add_up(banks[4], DT, S, lambda m: big1[:, m, :])


def tiles(w, cols=P):
    k, n = w.shape
    return np.ascontiguousarray(w.reshape(k // P, P, n // cols, cols).transpose(2, 1, 0, 3)).reshape(n // cols, -1)


def by_feature(v):
    return np.moveaxis(v.reshape(v.shape[:-1] + (v.shape[-1] // P, P)), -1, 0).reshape(P, -1)


def weight_stream(a):
    out = []
    for l in range(L):
        w = a["w_in"][l]
        q = w[:, 0:512].reshape(D, 2, 4, HD).transpose(0, 2, 1, 3).reshape(D, 512)
        out += [tiles(q), tiles(w[:, 512:768]), tiles(w[:, 2304:3840]), tiles(w[:, 768:2304]), tiles(w[:, 3840:])]
        br = [tiles(a[f"w_branch_{x}"][l]) for x in "abc"]
        out += [b[m] for m in range(DT) for b in br]
        out.append(tiles(a["w_out"][l]))
        out += swiglu_units(a["w_ffn_gate"][l], a["w_ffn_up"][l], a["w_ffn_down"][l])
    for l in range(L):
        for f in "12":
            if f == "2":
                w = a["w_in_2"][l]
                kr = w[:, 1408:1440]
                out += [tiles(w[:, 1440:1952]), tiles(w[:, 1152:1408]), tiles(np.concatenate([kr] * 4, 1)),
                        tiles(w[:, 768:1152]), tiles(w[:, 0:768])]
                kv = a["w_ukv_2"][l].reshape(-1, H, 2, HD)
                out += [tiles(kv[:, :, 0].reshape(-1, H * HD)), tiles(kv[:, :, 1].reshape(-1, H * HD))]
                q = a["w_uq_2"][l].reshape(-1, H, QK)
                out.append(tiles(np.concatenate([q, q[:, :, HD:QK]], 2).reshape(-1, H * P)))
                g = tiles(a["w_bgate_2"][l])
                br = [tiles(a[x][l]) for x in ("w_pw_conv_2", "w_o_mla_2", "w_fourier_2")]
                out += [y for m in range(DT) for b in range(3) for y in (g[b * DT + m], br[b][m])]
                out.append(tiles(a["w_out_2"][l]))
            out += swiglu_units(a[f"w1_ffn{f}_2"][l], a[f"w3_ffn{f}_2"][l], a[f"w2_ffn{f}_2"][l])
    return np.concatenate([np.ascontiguousarray(o).reshape(-1) for o in out])


def swiglu_units(gate, up, down):
    own = np.stack([tiles(gate), tiles(up)], 1).reshape(2 * FT, -1)
    out, t = [], 0
    for n in CHUNKS:
        out += [own[2 * t:2 * (t + n)], tiles(down[t * P:(t + n) * P])]
        t += n
    return out


def constants():
    c0 = np.zeros((P, NCST0), np.float32)
    c0[:, 0:P] = np.eye(P)
    c0[:, P:2 * P] = 1.0
    c0[:, 2 * P], c0[:, 2 * P + 1] = LN_EPS, EPS
    q = (np.arange(QT)[None, :, None] * P + np.arange(P)[:, None, None])
    d = (q - np.arange(S)[None, None, :]).astype(np.float64)
    far = 1e30
    da = np.where((d >= 0) & (d < 128), d, far).reshape(P, -1)
    dc = np.where(d >= 0, d, far).reshape(P, -1)
    c1 = np.concatenate([da, dc], 1).astype(np.float32)
    ax = ROPE // 2
    t = np.arange(S)
    inv = 1.0 / (10000.0 ** (np.arange(ax // 2) * 2.0 / ax))
    ar, ac = (t // 64)[:, None] * inv, (t % 64)[:, None] * inv
    ang = np.concatenate([ar, ar, ac, ac], 1).T
    turn = np.zeros((ROPE, ROPE))
    for i in range(ROPE):
        first = i % ax < ax // 2
        turn[i + ax // 2 if first else i - ax // 2, i] = -1.0 if first else 1.0
    c2 = np.zeros((P, NCST2), np.float32)
    c2[HD:QK, :] = np.concatenate([np.cos(ang), np.sin(ang), turn], 1)
    a = 2 * np.pi * np.outer(np.arange(P), np.arange(P)) / P
    b = 2 * np.pi * np.outer(np.arange(S), np.arange(S)) / S
    tok = np.stack([np.cos(b), -np.sin(b)], 1) / np.sqrt(S)
    tok = tok.reshape(QT, P, 2, S).transpose(1, 0, 2, 3).reshape(P, -1)
    dft = np.concatenate([np.cos(a) / np.sqrt(P), np.sin(a) / np.sqrt(P), tok], 1)
    return c0, c1, c2, dft.astype(np.float32)


def layouts(a):
    def tokens(x):
        return np.ascontiguousarray(x.reshape(S, DT, P).transpose(2, 1, 0)).reshape(P, -1)

    c = np.broadcast_to(np.concatenate([a["c_ctx_2"].reshape(-1), a["c_2"].reshape(-1)]), (P, 2 * D))
    sinks = np.broadcast_to(a["attn_sinks"].reshape(1, L, H, 1), (P, L, H, QT)).reshape(P, -1)
    par1 = np.concatenate([by_feature(a[n]) for n in ("ln1_g", "ln1_b", "ln2_g", "ln2_b", "conv_w")] +
                          [sinks], 1)
    par2 = np.concatenate([by_feature(a[n + "_2"]) for n in
                           ("g_ffn1", "g_mix", "g_ffn2", "w_dw", "b_dw", "ln_g_conv", "ln_b_conv", "b_pw_conv",
                            "g_qnorm", "g_kvnorm", "b_fourier", "b_bgate", "g_final", "b_ada")], 1)
    c0, c1, c2, dft = constants()
    return {"xT": tokens(a["x"]), "ctxT": tokens(a["ctx_2"]), "w_stream": weight_stream(a),
            "w_ada": a["w_ada_2"].transpose(0, 2, 1).reshape(-1), "c": c, "par1": par1,
            "par2": par2, "cst0": c0, "cst1": c1, "cst2": c2, "dft": dft}


def kernel(**inputs):
    import numpy as _np
    import concourse.bacc as _bacc
    from concourse import mybir as _mybir
    from concourse.bass_utils import run_bass_kernel_spmd as _run

    arrays = {k: _np.ascontiguousarray(v) for k, v in layouts({k: _np.asarray(v) for k, v in inputs.items()}).items()}
    nc = _bacc.Bacc("TRN2", target_bir_lowering=False, num_devices=1)
    args = [nc.dram_tensor(f"in_{n}", v.shape, _mybir.dt.from_np(v.dtype), kind="ExternalInput").ap()
            for n, v in arrays.items()]
    args.append(nc.dram_tensor("outT", (P, DT * S), _mybir.dt.float32, kind="ExternalOutput").ap())
    program(nc, *args)
    r = _run(nc, [{f"in_{n}": v for n, v in arrays.items()}], core_ids=[0])
    got = r.results[0]["outT"]
    return _np.ascontiguousarray(got.reshape(P, DT, S).transpose(2, 1, 0)).reshape(1, S, D)
```

```python
from contextlib import ExitStack

import numpy as np

import concourse.bass as bass
from concourse import mybir

ALU = mybir.AluOpType
ACT = mybir.ActivationFunctionType
F32 = mybir.dt.float32
F32R = mybir.dt.float32r
AX_X = mybir.AxisListType.X

P = 128
L = 2
D = 1024
DT = D // P
S = 256
QT = S // P
HD = 64
H = 8
FF = 2816
FT = FF // P
CHUNKS = [8, 8, FT - 16]
ALPHA = (2 * L) ** 0.25
CONV_AT = 2
SCORES_AT = [8, 10, 12, 14, 16, 18, 20, 22]
LN_AT = [6, 8]
LN_EPS = 1e-5
EPS = 1e-6

SLOTS = 4
AHEAD = 3
SLOT = 8 * P

NADA = 9
CT = 3
TAPS = 31
PAD = TAPS // 2
ROPE = 32
QK = HD + ROPE
QLT, KVT = 3, 2
FG = 4

SLOPES = [2.0 ** (-8.0 * (i + 1.0) / (2 * H)) for i in range(2 * H)]


ADA_TILES = L * NADA * DT
BESIDE = {"up00": 1, "up01": 1, "up02": 1, "up10": 1, "up11": 1, "up12": 1, "fup100": 4, "fup101": 4, "fup102": 4,
          "fup200": 4, "fup201": 4, "fup202": 4, "fup110": 4, "fup111": 3, "fup112": 2}


def stages():
    out = []

    def swiglu(up, down):
        for c, n in enumerate(CHUNKS):
            out.append((f"{up}{c}", [8] * (2 * n)))
            out.append((f"{down}{c}", [n] * 8))

    for l in range(L):
        out.append((f"qkv{l}", [8] * 18))
        out.append((f"bbb{l}", [8] * 12))
        out.append((f"gate{l}", [8] * 24))
        out.append((f"merge{l}", [4] * 24))
        out.append((f"out{l}", [8] * 8))
        swiglu(f"up{l}", f"down{l}")
    for l in range(L):
        swiglu(f"fup1{l}", f"fdown1{l}")
        out.append((f"mix{l}", [8] * 16))
        out.append((f"kv{l}", [KVT] * 8))
        out.append((f"q{l}", [QLT] * H))
        out.append((f"bm{l}", [8, 4, 8, 4, 8, CT] * DT))
        out.append((f"bout{l}", [8] * 8))
        swiglu(f"fup2{l}", f"fdown2{l}")
    return out


class Plan:

    def __init__(self):
        self.start, self.count, self.kt, self.offset = {}, {}, [], []
        at = 0
        for name, units in stages():
            self.start[name], self.count[name] = len(self.kt), len(units)
            for kt in units:
                self.kt.append(kt)
                self.offset.append(at)
                at += P * kt * P
        self.units = len(self.kt)
        self.ada, at, loads = {}, 0, [0] * 4
        self.ada_end = []
        for name, n in BESIDE.items():
            iters = self.count[name] // SLOTS
            self.ada[name] = (at, n, tuple(loads), len(self.ada_end))
            self.ada_end += [at + n * (i + 1) for i in range(iters)]
            at += n * iters
            for s in range(n):
                loads[s] += iters
        assert at == ADA_TILES

    def ada_iterations(self, tiles):
        return sum(e < tiles for e in self.ada_end) + 1

    def freed(self, u):
        return u // SLOTS


class Tally:

    def __init__(self, eng, sem):
        self.eng, self.sem, self.n, self.per, self.it = eng, sem, 0, 0, 0

    def add(self, ins, k=1):
        ins.then_inc(self.sem, k)
        self.n += k
        return ins

    def wait(self, k=0):
        self.n += k
        self.eng.wait_ge(self.sem, self.n + self.per * self.it)

    def enter(self, it, per):
        self.it, self.per, self.at = it, per, self.n

    def leave(self, iters):
        assert self.n - self.at == self.per, (self.sem, self.n - self.at, self.per)
        self.n += self.per * (iters - 1)
        self.it = self.per = 0


def repeat(eng, iters, body, tallies):
    if iters <= 0:
        return
    if iters == 1:
        body(0)
        return
    with eng.Fori(0, iters) as i:
        for t, per in tallies:
            t.enter(i, per)
        body(i)
        for t, _ in tallies:
            t.leave(iters)


def columns(parts):
    out, at = {}, 0
    for name, n in parts:
        out[name] = (at, n)
        at += n
    return out, at


PAR1, NPAR1 = columns([("ln1_g", L * DT), ("ln1_b", L * DT), ("ln2_g", L * DT), ("ln2_b", L * DT),
                       ("conv_w", L * 3 * 4), ("sinks", L * H * QT)])
PAR2, NPAR2 = columns([("g_ffn1", L * DT), ("g_mix", L * DT), ("g_ffn2", L * DT), ("w_dw", L * TAPS * CT),
                       ("b_dw", L * CT), ("ln_g", L * CT), ("ln_b", L * CT), ("b_pw", L * DT),
                       ("g_qnorm", L * QLT), ("g_kvnorm", L * KVT), ("b_four", L * DT),
                       ("b_bgate", L * 3 * DT), ("g_final", DT), ("b_ada", L * NADA * DT)])
CST0, NCST0 = columns([("ident", P), ("ones", P), ("eps", 2)])
CST1, NCST1 = columns([("dist_a", QT * S), ("dist_c", QT * S)])
CST2, NCST2 = columns([("cos", S), ("sin", S)])
DFT, NDFT = columns([("chan", 2 * P), ("tok", QT * 2 * S)])


def program(nc, xT, ctxT, w_stream, w_ada, c_d, par1_d, par2_d, cst0_d, cst1_d, cst2_d, dft_d, out):
    plan = Plan()
    U = plan.start
    T2 = 2 * S

    with ExitStack() as ctx:
        def sem(name):
            return ctx.enter_context(nc.semaphore(name))

        def sb(where, name, shape, dt=F32):
            return where.enter_context(nc.sbuf_tensor(name, shape, dt))

        raw = sb(ctx, "raw", [P, SLOTS, SLOT])
        whi = sb(ctx, "whi", [P, SLOTS, SLOT], F32R)
        wlo = sb(ctx, "wlo", [P, SLOTS, SLOT], F32R)
        cst0 = sb(ctx, "cst0", [P, NCST0])
        cst2 = sb(ctx, "cst2", [P, NCST2])
        par2 = sb(ctx, "par2", [P, NPAR2])
        mod = sb(ctx, "mod", [P, L, NADA * DT, 2])
        h = sb(ctx, "h", [P, DT, T2])
        cs = sb(ctx, "cs", [P, 2, D])
        sums = sb(ctx, "ada_sums", [P, 8])
        tok = sb(ctx, "tok", [P, 2, 4])
        small = sb(ctx, "small", [P, 5, H * QT])
        smallc = sb(ctx, "smallc", [P, 3, H * QT])
        ident, ones = cst0[:, 0:P], cst0[:, P:2 * P]
        ln_eps, rms_eps = cst0[:, 2 * P:2 * P + 1], cst0[:, 2 * P + 1:2 * P + 2]

        one = ExitStack()
        gates = sb(one, "gates", [P, 24, S])
        qa = sb(one, "qa", [P, 4, S])
        ka = sb(one, "ka", [P, S])
        va = sb(one, "va", [P, QT, P])
        qc = sb(one, "qc", [P, 4, S])
        kc = sb(one, "kc", [P, 4, S])
        vc = sb(one, "vc", [P, QT, 4 * P])
        bbb = sb(one, "bbb", [P, 12, S])
        x1 = sb(one, "x1", [P, DT, S])
        x1hi = sb(one, "x1hi", [P, DT, S], F32R)
        x1lo = sb(one, "x1lo", [P, DT, S], F32R)
        y1hi = sb(one, "y1hi", [P, 12, S], F32R)
        y1lo = sb(one, "y1lo", [P, 12, S], F32R)
        lg = sb(one, "lg", [P, 2 * H, S])
        pt1 = sb(one, "pt1", [P, 2, QT * S])
        par1 = sb(one, "par1", [P, NPAR1])
        cst1 = sb(one, "cst1", [P, NCST1])
        one.close()
        with ExitStack() as place:
            sb(place, "lgc_ahead", [P, 24 * S + 4 * S + S + QT * P + 2 * 4 * S + QT * 4 * P + 12 * S + DT * S])
            lgc = sb(place, "lgc", [P, 2 * H, S])
        logits = {"a": lg, "c": lgc}

        two = ExitStack()
        uhi = sb(two, "uhi", [P, DT, T2], F32R)
        ulo = sb(two, "ulo", [P, DT, T2], F32R)
        yhi = sb(two, "yhi", [P, 9, T2], F32R)
        ylo = sb(two, "ylo", [P, 9, T2], F32R)
        big1 = sb(two, "big1", [P, DT, T2])
        big2 = sb(two, "big2", [P, DT, T2])
        vt = sb(two, "vt", [P, 4, T2])
        vpad = sb(two, "vpad", [P, CT, 2, S + 2 * PAD])
        acc = sb(two, "acc", [P, CT, T2])
        pp = sb(two, "pp", [P, 4, T2])
        scl = sb(two, "scl", [P, 3, DT, 2])
        hgt = sb(two, "hgt", [P, 2, DT, 2])
        two.close()
        def over(name, before, shape, dt):
            with ExitStack() as place:
                sb(place, name + "_ahead", [P, before * T2])
                return sb(place, name, shape, dt)

        YHI, YLO, BIG2, VCONV = 2 * DT, 2 * DT + 9, 3 * DT + 18, 4 * DT + 22
        ychi = over("ychi", VCONV, [P, CT, T2], F32R)
        csquares = over("csquares", VCONV, [P, CT, T2], F32)
        yclo = [ylo[:, 8, :], yhi[:, 8, :], over("yclo2", BIG2 + 7, [P, T2], F32R)[:, :]]
        spare = over("spare", YLO + 8, [P, T2], F32)
        swaps = [over("swapped_hi", YHI, [P, 2, T2], F32), over("swapped_lo", YLO, [P, 2, T2], F32)]
        swapped = [t[HD:QK, b, :] for t in swaps for b in range(2)]
        dft = pp[:, 0:3, :].rearrange("p a b -> p (a b)")
        xsum = pt1[:, 1, 0:S]
        rs1, rs2, rs3 = pt1[:, 0, 0:S], pp[:, 3, :], spare[:, :]
        cdev = spare[:, :]

        banks = [ctx.enter_context(nc.psum_tensor(f"bank{b}", [P, 512], F32)) for b in range(SLOTS)]
        aux = ctx.enter_context(nc.psum_tensor("aux", [P, 4, 512], F32))
        banks += [aux[:, b, :] for b in range(4)]

        def p1(name, l, n):
            at, _ = PAR1[name]
            return par1[:, at + l * n:at + (l + 1) * n]

        def p2(name, l, n):
            at, _ = PAR2[name]
            return par2[:, at + l * n:at + (l + 1) * n]

        def mods(l, n):
            return mod[:, l, n * DT:(n + 1) * DT, :]

        dist = {k: cst1[:, CST1[f"dist_{k}"][0]:CST1[f"dist_{k}"][0] + QT * S] for k in "ac"}
        cos, sin = cst2[HD:QK, 0:S], cst2[HD:QK, S:2 * S]

        s_land = [sem(f"unit_landed{s}") for s in range(SLOTS)]
        s_high = sem("unit_high_ready")
        s_low = sem("unit_low_ready")
        s_used = sem("unit_used")
        s_free = [sem(f"bank_read{s}") for s in range(SLOTS)]
        s_ada_land = [sem(f"ada_landed{s}") for s in range(4)]
        s_ada_sum = sem("ada_sums_ready")
        s_ada_mod = sem("ada_modulation_ready")
        s_x = sem("x_landed")
        s_const = sem("constants_landed")
        s_c = sem("c_landed")
        s_dft = sem("dft_landed")
        s_out = sem("out_landed")
        s_dve = sem("dve_step")
        s_val = sem("dve_value_ready")
        s_dop = sem("dve_operand_ready")
        s_split = sem("act_split_ready")
        s_sread = sem("scores_read")
        s_prob = sem("probs_ready")
        s_outv = sem("out_ready")
        s_aval = sem("act_value_ready")
        s_mid = sem("first_block_out")
        s_ahi = sem("act_high_ready")
        s_sq = sem("squares_ready")
        s_nsq = sem("norm_squares_ready")
        s_aop = sem("act_operand_ready")
        s_pt = sem("turned_probs_ready")
        s_stat = sem("sum_ready")
        s_mean = sem("token_value_ready")
        s_score = sem("scores_ready")
        s_turned = sem("probs_turned")
        s_head = sem("heads_ready")
        s_conv = sem("convolved")
        s_centred = sem("conv_centred")
        s_scaled = sem("conv_scaled")
        s_csq = sem("conv_squares_ready")
        s_cdev = sem("conv_deviation_ready")
        s_cmean = sem("conv_mean_ready")
        s_cvar = sem("conv_variance_ready")
        s_chigh = sem("conv_high_ready")
        s_clow = sem("conv_low_ready")
        score_bank = [banks[4], banks[5], banks[2]]
        ring1 = [gates[:, 4 * r:4 * r + 4, :] for r in range(2)]
        ring2 = [big2[:, 4:6, :], big2[:, 6:8, :], vt[:, 0:2, :], vt[:, 2:4, :]]
        waste1, waste2 = gates[:, 8:12, :], acc[:, 0:2, :]
        ring = lambda name: ring2 if name[0] == "f" else ring1
        block = ctx.enter_context(nc.Block())

        def after(u):
            return s_free[u % SLOTS], plan.freed(u) + 1

        def after_at(u0, j, i, per):
            u = u0 + j
            return s_free[u % SLOTS], plan.freed(u) + 1 + per // SLOTS * i

        @block.sync
        def _(sp):
            def load(u, it=0, per=0):
                if u >= SLOTS:
                    sp.wait_ge(s_low, u - SLOTS + 1 + per * it)
                n = plan.kt[u] * P
                if per:
                    src = w_stream[bass.ds((plan.offset[u + per] - plan.offset[u]) * it + plan.offset[u], P * n)]
                else:
                    src = w_stream[plan.offset[u]:plan.offset[u] + P * n]
                sp.dma_start(raw[:, u % SLOTS, 0:n], src.rearrange("(p n) -> p n", p=P)).then_inc(s_land[u % SLOTS], 16)

            def run(u0, n, per):
                iters = n // per
                if iters > 1:
                    with sp.Fori(0, iters - 1) as i:
                        for j in range(per):
                            load(u0 + j, i, per)
                for u in range(u0 + max(iters - 1, 0) * per, u0 + n):
                    load(u)

            load(0)
            load(1)
            sp.dma_start(x1[:, :, :], xT.rearrange("p (t s) -> p t s", t=DT)).then_inc(s_x, 16)
            for u in range(2, SLOTS):
                load(u)
            for name, n in plan.count.items():
                per = 12 if name.startswith("bm") else SLOTS
                first = SLOTS if U[name] == 0 else 0
                run(U[name] + first, n - first, per)
                if name == "qkv0":
                    sp.dma_start(par1[:, :], par1_d).then_inc(s_const, 16)
                    sp.dma_start(cst0[:, :], cst0_d).then_inc(s_const, 16)
                    sp.dma_start(cst1[:, :], cst1_d).then_inc(s_const, 16)
                    sp.dma_start(cst2[:, :], cst2_d).then_inc(s_const, 16)
                    sp.dma_start(par2[:, :], par2_d).then_inc(s_const, 16)
                    sp.dma_start(h[:, :, 0:S], ctxT.rearrange("p (t s) -> p t s", t=DT)).then_inc(s_const, 16)
                if name.startswith("mix"):
                    sp.wait_ge(s_used, U[name] + 1)
                    sp.dma_start(dft[:, 0:NDFT], dft_d).then_inc(s_dft, 16)
            for m in range(DT):
                sp.wait_ge(s_outv, m + 1)
                sp.dma_start(out[:, m * S:(m + 1) * S], big1[:, m, S:T2]).then_inc(s_out, 16)
            sp.wait_ge(s_out, 16 * DT)

        @block.gpsimd
        def _(pool):
            free = {"up00": ("merge0", 23), "up10": ("merge1", 23), "fup100": ("down12", 7),
                    "fup200": ("bout0", 0), "fup110": ("fdown202", 7)}
            pool.wait_ge(s_used, SLOTS)
            pool.dma_start(cs[:, :, :], c_d.rearrange("p (s d) -> p s d", s=2)).then_inc(s_c, 16)
            for name, (first, per, _, _) in plan.ada.items():
                if name in free:
                    stage, j = free[name]
                    pool.wait_ge(*after(U[stage] + j))
                if name == "fup100":
                    pool.wait_ge(s_mid, DT)

                def load(r, i):
                    n = P * D
                    at = (first + r) * n
                    src = w_ada[at:at + n] if i is None else w_ada[bass.ds(per * n * i + at, n)]
                    to = ring(name)[r]
                    pool.dma_start(to, src.rearrange("(p a b) -> p a b", p=P,
                                                     a=to.shape[1])).then_inc(s_ada_land[r], 16)

                if first:
                    pool.wait_ge(s_ada_sum, 2 * first)
                for r in range(per):
                    load(r, None)
                with pool.Fori(1, plan.count[name] // SLOTS) as i:
                    for r in range(per):
                        pool.wait_ge(s_ada_sum, 2 * per * i + 2 * (first + r + 1 - per))
                        load(r, i)

        @block.scalar
        def _(act):
            val, stat, turned, head = (Tally(act, s) for s in (s_val, s_stat, s_turned, s_head))
            sc = nc.scalar

            def high(u, it=0, per=0):
                if u >= plan.units:
                    return
                act.wait_ge(s_land[u % SLOTS], 16 * (u // SLOTS + 1) + 16 * (per // SLOTS) * it)
                if u >= SLOTS:
                    act.wait_ge(s_used, u - SLOTS + 1 + per * it)
                n = plan.kt[u] * P
                sc.copy(whi[:, u % SLOTS, 0:n], raw[:, u % SLOTS, 0:n]).then_inc(s_high, 1)

            def stream(u0, n, per, evac, tallies=()):
                iters = n // per

                def body(i):
                    for j in range(per):
                        evac(j, i)
                        high(u0 + j + AHEAD, i, per)

                repeat(act, iters - 1, body, tallies)
                for j in range(per):
                    evac(j, iters - 1)
                    high(u0 + n - per + j + AHEAD)

            def done(u0, j, i, per):
                act.wait_ge(s_used, u0 + j + per * i + 1)

            def bank(u0, j):
                return banks[(u0 + j) % SLOTS]

            def read(u0, j):
                return s_free[(u0 + j) % SLOTS]

            high(0)
            high(1)
            act.wait_ge(s_x, 16)
            for m in range(DT):
                sc.copy(x1hi[:, m, :], x1[:, m, :]).then_inc(s_ahi, 1)
            for u in range(2, AHEAD):
                high(u)

            def exp1(kind, h0):
                sm = small if kind == "a" else smallc
                lo = logits[kind]
                val.wait(1)
                for n in range(QT * h0, QT * (h0 + 4)):
                    sc.activation(lo[:, n, :], lo[:, n, :], ACT.Exp, bias=sm[:, 1, n:n + 1],
                                  scale=HD ** -0.5, accum_out=sm[:, 2, n:n + 1]).then_inc(s_aval, 1)
                if kind == "a" and h0:
                    sc.activation(small[:, 3, :], small[:, 4, :], ACT.Exp).then_inc(s_aval, 1)

            def outputs1(y0):
                for n in range(H + 1):
                    if n < H:
                        turned.wait(1)
                        b = banks[6 + n % 2]
                        sc.copy(pt1[:, n % 2, 0:S], b[:, 0:S])
                        sc.copy(pt1[:, n % 2, S + P:2 * S], b[:, S + P:2 * S]).then_inc(s_pt, 1)
                    if n >= 1 and n % 2 == 0:
                        head.wait(1)
                        sc.copy(y1hi[:, y0 + n // 2 - 1, :], banks[n // 2 - 1][:, 0:S]).then_inc(s_ahi, 1)

            def hidden(stage, c, c0, c1, sg, hid, ht):
                u0 = U[f"{stage}{c}"]
                sc.preload_act_table(ACT.Silu)

                def evac(j, i):
                    k = j // 2
                    if j % 2 == 0:
                        done(u0, j, i, 4)
                        sc.activation(sg(k)[:, c0:c1], bank(u0, j)[:, c0:c1], ACT.Silu).then_inc(read(u0, j), 1)
                    else:
                        act.wait_ge(*after_at(u0, j, i, 4))
                        sc.copy(ht[:, 2 * i + k, c0:c1], hid(k)[:, c0:c1]).then_inc(s_ahi, 1)

                stream(u0, plan.count[f"{stage}{c}"], 4, evac)

            def norm1(g, b, last):
                sc.preload_act_table(ACT.Sqrt)
                for m in range(0, DT, 2):
                    val.wait(1)
                    sc.activation(lg[:, m:m + 2, :], x1[:, m:m + 2, :], ACT.Square).then_inc(s_nsq, 1)
                stat.wait(1)
                sc.activation(tok[:, 1, 0:QT], aux[:, 0:QT, 0], ACT.Sqrt, bias=ln_eps, scale=1.0 / D).then_inc(s_aval, 1)
                for m in range(DT):
                    if m % 2 == 0:
                        val.wait(1)
                    gm, bm = g[:, m:m + 1], b[:, m:m + 1]
                    if last:
                        sc.activation(h[:, m, S:T2], lg[:, m, :], ACT.Identity, bias=bm, scale=gm).then_inc(s_mid, 1)
                    else:
                        sc.activation(x1hi[:, m, :], lg[:, m, :], ACT.Identity, bias=bm, scale=gm)
                        sc.activation(x1[:, m, :], lg[:, m, :], ACT.Identity, bias=bm, scale=gm).then_inc(s_ahi, 1)

            for l in range(L):
                u0 = U[f"qkv{l}"]
                dst = [qa[:, j, :] for j in range(4)] + [ka[:, :], None] + [qc[:, j, :] for j in range(4)] + \
                    [kc[:, j, :] for j in range(4)]
                for j in range(18):
                    high(u0 + j + AHEAD)
                    done(u0, j, 0, 0)
                    if j == 5:
                        sc.copy(va[:, :, :], bank(u0, j)[:, 0:S].rearrange("p (t c) -> p t c", t=QT)
                                ).then_inc(read(u0, j), 1)
                    elif j >= 14:
                        t, first = j % 2, j - j % 2
                        sc.copy(vc[:, t, (first - 14) * P:(first - 12) * P],
                                bank(u0, first)[:, t * S:(t + 1) * S]).then_inc(read(u0, first + 1 - t), 1)
                    else:
                        sc.copy(dst[j], bank(u0, j)[:, 0:S]).then_inc(read(u0, j), 1)

                u1 = U[f"bbb{l}"]

                def evac_b(j, i):
                    done(u1, j, i, 4)
                    sc.copy(bbb[:, 4 * i + j, :], bank(u1, j)[:, 0:S]).then_inc(read(u1, j), 1)
                stream(u1, 12, 4, evac_b)

                u2 = U[f"gate{l}"]
                if l == 0:
                    act.wait_ge(s_const, 6 * 16)
                    act.wait_ge(s_c, 16)
                    sc.activation(cs[:, :, :], cs[:, :, :], ACT.Silu).then_inc(s_aval, 1)
                for j in range(24):
                    high(u2 + j + AHEAD)
                    done(u2, j, 0, 0)
                    sc.activation(gates[:, j, :], bank(u2, j)[:, 0:S], ACT.Sigmoid).then_inc(read(u2, j), 1)
                    if j == CONV_AT + 10:
                        val.wait(1)
                        sc.copy(y1hi[:, 4:8, :], bbb[:, 8:12, :]).then_inc(s_ahi, 1)
                sc.preload_act_table(ACT.Exp)
                for kind in "ac":
                    exp1(kind, 0)
                    exp1(kind, 4)
                outputs1(0)
                outputs1(8)

                def evac_m(j, i):
                    if j % 3 == 2:
                        val.wait(1)
                        sc.copy(x1hi[:, 4 * i + j // 3, :], lg[:, 3 + (j // 3) % 2, :]).then_inc(s_ahi, 1)
                stream(U[f"merge{l}"], 24, 12, evac_m, [(val, 4)])
                stream(U[f"out{l}"], 8, 4, lambda j, i: None)
                norm1(p1("ln1_g", l, DT), p1("ln1_b", l, DT), False)
                for c, n in enumerate(CHUNKS):
                    hidden(f"up{l}", c, 0, S, lambda k: lg[:, k, :], lambda k: lg[:, 2 + k, :], y1hi)
                    stream(U[f"down{l}{c}"], 8, 4, lambda j, i: None)
                norm1(p1("ln2_g", l, DT), p1("ln2_b", l, DT), l == L - 1)

            act.wait_ge(s_mid, DT)

            def square(m, c0, u0):
                if u0:
                    act.wait_ge(*after(u0 + m))
                sc.activation(big1[:, m, c0:T2], h[:, m, c0:T2], ACT.Square).then_inc(s_nsq, 1)

            def update(u0, c0):
                def evac(j, i):
                    if 4 * i + j:
                        square(4 * i + j - 1, c0, u0)
                stream(u0, 8, 4, evac)

            def norm2(l, which, c0, ready):
                sc.preload_act_table(ACT.Sqrt)
                for m in range(DT - 1 if ready else 0, DT):
                    square(m, c0, ready)
                stat.wait(1)
                sc.activation(tok[:, 1, c0 // P:4], aux[:, c0 // P:4, 0], ACT.Sqrt, bias=rms_eps,
                              scale=1.0 / D).then_inc(s_aval, 1)
                if which is None:
                    return
                for m in range(DT):
                    val.wait(1)
                    for s in range(c0 // S, 2):
                        cols = slice(s * S, (s + 1) * S)
                        ins = sc.activation(uhi[:, m, cols], big1[:, m, cols], ACT.Identity,
                                            bias=mods(l, 3 * which)[:, m, s:s + 1])
                    ins.then_inc(s_ahi, 1)

            def ffn2(l, f, c0, c1):
                for c, n in enumerate(CHUNKS):
                    hidden(f"fup{f}{l}", c, c0, T2, lambda k: pp[:, k, :], lambda k: pp[:, 2 + k, :], yhi)
                    if c == len(CHUNKS) - 1:
                        update(U[f"fdown{f}{l}{c}"], c1)
                    else:
                        stream(U[f"fdown{f}{l}{c}"], 8, 4, lambda j, i: None)

            def attention2(l, s):
                c0 = S if l == L - 1 else 0
                nk = (s + 1) * S
                N = H * QT

                def exp(n):
                    val.wait(1)
                    sc.activation(pp[:, n % 2, 0:nk], score_bank[n % 3][:, 0:nk], ACT.Exp, bias=small[:, 1, n:n + 1],
                                  scale=QK ** -0.5, accum_out=small[:, 2, n:n + 1]).then_inc(s_aval, 1)
                exp(0)
                exp(1)
                for n in range(N + 1):
                    if n < N:
                        turned.wait(1)
                        sc.copy(pp[:, 2 + n % 2, 0:nk], banks[6 + n % 2][:, 0:nk]).then_inc(s_pt, 1)
                    if n + 2 < N:
                        exp(n + 2)
                    if n and n % 4 == 0:
                        head.wait(1)
                        j = n // 4 - 1
                        sc.copy(yhi[:, j, s * S:(s + 1) * S], banks[j % 2][:, 0:S]).then_inc(s_ahi, 1)
                    if s and n == LN_AT[l] + 1:
                        for m in range(CT):
                            act.wait_ge(s_centred, CT * l + m + 1)
                            sc.activation(csquares[:, m, c0:T2], acc[:, m, c0:T2], ACT.Square).then_inc(s_csq, 1)
                    if s and n == LN_AT[l] + 4:
                        act.wait_ge(s_cvar, l + 1)
                        sc.activation(cdev[:, c0:T2], banks[3][:, c0:T2], ACT.Sqrt, bias=rms_eps,
                                      scale=1.0 / (CT * P)).then_inc(s_cdev, 1)
                        sc.preload_act_table(ACT.Exp)
                    if s and n == LN_AT[l] + 8:
                        lng, lnb = p2("ln_g", l, CT), p2("ln_b", l, CT)
                        for m in range(CT):
                            act.wait_ge(s_scaled, CT * l + m + 1)
                            sc.activation(ychi[:, m, c0:T2], acc[:, m, c0:T2], ACT.Silu, bias=lnb[:, m:m + 1],
                                          scale=lng[:, m:m + 1])
                            sc.activation(acc[:, m, c0:T2], acc[:, m, c0:T2], ACT.Silu, bias=lnb[:, m:m + 1],
                                          scale=lng[:, m:m + 1]).then_inc(s_chigh, 1)

            for l in range(L):
                last = l == L - 1
                c0 = S if last else 0
                norm2(l, 0, 0, U[f"fdown2{l - 1}{len(CHUNKS) - 1}"] if l else 0)
                ffn2(l, "1", 0, 0)
                norm2(l, 1, 0, U[f"fdown1{l}{len(CHUNKS) - 1}"])

                u0 = U[f"mix{l}"]
                for j in range(16):
                    high(u0 + j + AHEAD)
                    done(u0, j, 0, 0)
                    cc = 0 if j < 3 else c0
                    src = bank(u0, j)[:, cc:T2]
                    if j == 2:
                        sc.copy(vt[HD:QK, 3, :], src[HD:QK, :])
                        sc.copy(big1[HD:QK, 2, 0:S], src[QK:P, S:T2]).then_inc(read(u0, j), 1)
                    elif 9 <= j < 12:
                        sc.activation(acc[:, j - 9, cc:T2], src, ACT.Sigmoid).then_inc(read(u0, j), 1)
                    else:
                        to = (big1[:, j, cc:T2] if j < 2 else vt[:, j - 3, cc:T2] if j < 6 else
                              big2[:, 4 + j - 6, cc:T2] if j < 9 else big2[:, j - 12, cc:T2])
                        sc.copy(to, src).then_inc(read(u0, j), 1)
                    if j == 5:
                        act.wait_ge(*after(u0 + 5))
                        for m in range(KVT):
                            sc.activation(big1[:, 4 + m, :], big1[:, m, :], ACT.Square).then_inc(s_sq, 1)
                        for m in range(QLT):
                            sc.activation(big1[:, (3, 6, 7)[m], c0:T2], vt[:, m, c0:T2], ACT.Square).then_inc(s_sq, 1)
                    if j == 8:
                        stat.wait(1)
                        sc.activation(rs2, banks[4][:, :], ACT.Sqrt, bias=rms_eps,
                                      scale=1.0 / (KVT * P)).then_inc(s_aval, 1)
                        stat.wait(1)
                        sc.activation(rs3[:, c0:T2], banks[5][:, c0:T2], ACT.Sqrt, bias=rms_eps,
                                      scale=1.0 / (QLT * P)).then_inc(s_aval, 1)
                    if j == 9:
                        val.wait(1)
                        for m in range(KVT):
                            val.wait(1)
                            sc.copy(yhi[:, m, :], big1[:, m, :]).then_inc(s_ahi, 1)
                    if j == 10:
                        for m in range(QLT):
                            val.wait(1)
                            sc.copy(yhi[:, (2, 3, 8)[m], c0:T2], vt[:, m, c0:T2]).then_inc(s_ahi, 1)

                N = FG * (2 - c0 // S)
                for n in range(N + 1):
                    if n < N:
                        stat.wait(1)
                        sc.copy(big1[:, 2 + n % 2, :], banks[4 + n % 2][:, :]).then_inc(s_aop, 1)
                    if n:
                        g, s = (n - 1) % FG, (n - 1) // FG + c0 // S
                        head.wait(1)
                        sc.copy(yhi[:, 4 + g, s * S:(s + 1) * S],
                                banks[6 + (n - 1) % 2][:, 0:S]).then_inc(s_ahi, 1)

                for hh in range(H):
                    ins = sc.copy(big2[HD:QK, hh, :], vt[HD:QK, 3, :])
                ins.then_inc(s_aop, 1)

                u0 = U[f"kv{l}"]
                for j in range(8):
                    high(u0 + j + AHEAD)
                    done(u0, j, 0, 0)
                    if j < 4:
                        sc.copy(big2[0:HD, 2 * j, :], bank(u0, j)[0:HD, :])
                        sc.copy(big2[0:HD, 2 * j + 1, :], bank(u0, j)[HD:P, :]).then_inc(read(u0, j), 1)
                    else:
                        t, at = 2 * (j % 2), (j - j % 2 - 4) * P
                        sc.copy(vt[:, t:t + 2, at:at + 2 * P],
                                bank(u0, j)[:, :].rearrange("p (t c) -> p t c", t=2)).then_inc(read(u0, j), 1)
                u0 = U[f"q{l}"]
                for j in range(H):
                    high(u0 + j + AHEAD)
                    done(u0, j, 0, 0)
                    sc.copy(big1[0:QK, j, c0:T2], bank(u0, j)[0:QK, c0:T2])
                    sc.copy(swapped[j // 2][:, j % 2 * S:(j % 2 + 1) * S],
                            bank(u0, j)[QK:P, S:T2]).then_inc(read(u0, j), 1)
                for s in range(c0 // S, 2):
                    attention2(l, s)

                u3 = U[f"bm{l}"]
                bg = p2("b_bgate", l, 3 * DT)
                sc.preload_act_table(ACT.Sigmoid)

                def evac_g2(j, i):
                    if j % 2 == 0:
                        br, m = (j % 6 // 2 + 1) % 3, 2 * i + j // 6
                        done(u3, j, i, 12)
                        sc.activation(pp[:, br, c0:T2], bank(u3, j)[:, c0:T2], ACT.Sigmoid,
                                      bias=bg[:, bass.ds(br * DT + m, 1)]).then_inc(read(u3, j), 1)
                stream(u3, 6 * DT, 12, evac_g2)
                for m in range(DT):
                    val.wait(1)
                    sc.copy(uhi[:, m, c0:T2], big1[:, m, c0:T2]).then_inc(s_ahi, 1)
                update(U[f"bout{l}"], c0)
                norm2(l, 2, c0, U[f"bout{l}"])
                ffn2(l, "2", c0, c0)
            norm2(L - 1, None, S, U[f"fdown2{L - 1}{len(CHUNKS) - 1}"])

        @block.vector
        def _(dve):
            ve = nc.vector
            step = Tally(dve, s_dve)
            aval, ahi, mean, score, nsq = (Tally(dve, s) for s in (s_aval, s_ahi, s_mean, s_score, s_nsq))

            def low(u, it=0, per=0):
                if u >= plan.units:
                    return
                dve.wait_ge(s_high, u + 1 + per * it)
                n = plan.kt[u] * P
                ve.tensor_tensor(wlo[:, u % SLOTS, 0:n], raw[:, u % SLOTS, 0:n],
                                 whi[:, u % SLOTS, 0:n].bitcast(F32), ALU.subtract).then_inc(s_low, 1)

            def stream(u0, n, per, evac, tallies=()):
                iters = n // per

                def body(i):
                    for j in range(per):
                        evac(j, i)
                        low(u0 + j + AHEAD, i, per)

                repeat(dve, iters - 1, body, tallies)
                for j in range(per):
                    evac(j, iters - 1)
                    low(u0 + n - per + j + AHEAD)

            def done(u0, j, i, per):
                dve.wait_ge(s_used, u0 + j + per * i + 1)

            def bank(u0, j):
                return banks[(u0 + j) % SLOTS]

            def read(u0, j):
                return s_free[(u0 + j) % SLOTS]

            def rest(dst, src, hi):
                ve.tensor_tensor(dst, src, hi.bitcast(F32), ALU.subtract).then_inc(s_split, 1)

            def chained(ins):
                step.add(ins)
                step.wait()

            nothing = lambda j, i: None
            low(0)
            low(1)
            for m in range(DT):
                ahi.wait(1)
                rest(x1lo[:, m, :], x1[:, m, :], x1hi[:, m, :])
            for u in range(2, AHEAD):
                low(u)

            def ada(name, j, i):
                first, per, loads, before = plan.ada[name]
                for o in range(2 * per):
                    if o * 4 // (2 * per) != j:
                        continue
                    r, s = o // 2, o % 2
                    if s == 0:
                        dve.wait_ge(s_ada_land[r], 16 * i + 16 * (loads[r] + 1))
                    if o == 0 and not (isinstance(i, int) and before + i == 0):
                        dve.wait_ge(s_ada_mod, i + before)
                    if not (isinstance(i, int) and first + o + i == 0):
                        dve.wait_ge(s_ada_sum, 2 * per * i + (2 * first + o))
                    out_ = waste2 if name[0] == "f" else waste1
                    ve.tensor_tensor_reduce(out_, ring(name)[r],
                                            cs[:, s, :].rearrange("p (a b) -> p a b", a=out_.shape[1]), 1.0, 0.0,
                                            ALU.mult, ALU.add, sums[:, o:o + 1]).then_inc(s_ada_sum, 1)
                if j == 3:
                    dve.wait_ge(s_ada_sum, 2 * per * i + 2 * (first + per))
                    ve.tensor_tensor(
                        mod[:, :, :, :].rearrange("p l t s -> p (l t) s")[:, bass.ds(per * i + first, per), :],
                        sums[:, 0:2 * per].rearrange("p (t s) -> p t s", s=2),
                        par2[:, bass.ds(per * i + (first + PAR2["b_ada"][0]), per)].unsqueeze(2)
                        .to_broadcast([P, per, 2]), ALU.add).then_inc(s_ada_mod, 1)

            def logits1(kind, hh):
                sm, lo = (small if kind == "a" else smallc), logits[kind]
                score.wait(1)
                slope = SLOPES[hh if kind == "a" else H + hh]
                chained(ve.scalar_tensor_tensor(
                    lo[:, 2 * hh:2 * hh + 2, :], dist[kind].rearrange("p (t s) -> p t s", t=2), -slope * HD ** 0.5,
                    banks[4 + hh % 2][:, :].rearrange("p (t s) -> p t s", t=2), ALU.mult, ALU.add))
                ve.tensor_reduce(sm[:, 0, 2 * hh:2 * hh + 2], lo[:, 2 * hh:2 * hh + 2, :], AX_X,
                                 ALU.max).then_inc(s_sread, 1)

            def biases1(kind, l, h0):
                sread[0] += 4
                dve.wait_ge(s_sread, sread[0])
                r = slice(QT * h0, QT * (h0 + 4))
                if kind == "a":
                    sinks = p1("sinks", l, H * QT)[:, r]
                    chained(ve.tensor_scalar(small[:, 3, r], sinks, HD ** 0.5, None, ALU.mult))
                    chained(ve.tensor_tensor(small[:, 0, r], small[:, 0, r], small[:, 3, r], ALU.max))
                    chained(ve.tensor_scalar(small[:, 1, r], small[:, 0, r], -HD ** -0.5, None, ALU.mult))
                    ve.tensor_tensor(small[:, 4, r], sinks, small[:, 1, r], ALU.add).then_inc(s_val, 1)
                else:
                    ve.tensor_scalar(smallc[:, 1, r], smallc[:, 0, r], -HD ** -0.5, None, ALU.mult).then_inc(s_val, 1)

            def scale1(kind):
                sm, lo = (small if kind == "a" else smallc), logits[kind]
                aval.wait(H * QT)
                if kind == "a":
                    aval.wait(1)
                    chained(ve.tensor_tensor(small[:, 2, :], small[:, 2, :], small[:, 3, :], ALU.add))
                chained(ve.reciprocal(sm[:, 2, :], sm[:, 2, :]))
                for hh in range(H):
                    for n in (2 * hh, 2 * hh + 1):
                        ins = ve.tensor_scalar(lo[:, n, :], lo[:, n, :], sm[:, 2, n:n + 1], None, ALU.mult)
                    ins.then_inc(s_prob, 1)

            def outputs1(y0):
                for j in range(H // 2):
                    ahi.wait(1)
                    rest(y1lo[:, y0 + j, :], banks[j][:, 0:S], y1hi[:, y0 + j, :])

            sread = [0]

            def short_conv(l, part):
                if part == 0:
                    dve.wait_ge(*after(U[f"bbb{l}"] + 11))
                    step.add(ve.tensor_tensor(bbb[:, 0:4, :], bbb[:, 0:4, :], bbb[:, 8:12, :], ALU.mult))
                elif part < 4:
                    w = p1("conv_w", l, 12)
                    step.wait()
                    k, d = 3 - part, part - 1
                    for j in range(4):
                        wk = w[:, 4 * k + j:4 * k + j + 1]
                        if d == 0:
                            ins = ve.tensor_scalar(bbb[:, 8 + j, :], bbb[:, j, :], wk, None, ALU.mult)
                        else:
                            ins = ve.scalar_tensor_tensor(bbb[:, 8 + j, d:S], bbb[:, j, 0:S - d], wk,
                                                          bbb[:, 8 + j, d:S], ALU.mult, ALU.add)
                        step.add(ins)
                elif part == 4:
                    step.wait()
                    ve.tensor_tensor(bbb[:, 8:12, :], bbb[:, 8:12, :], bbb[:, 4:8, :], ALU.mult).then_inc(s_val, 1)
                else:
                    ahi.wait(1)
                    rest(y1lo[:, 4:8, :], bbb[:, 8:12, :], y1hi[:, 4:8, :])

            def hidden(stage, c, c0, c1, sg, hid, hi, lo):
                name = f"{stage}{c}"
                u0 = U[name]

                def evac(j, i):
                    k = j // 2
                    if j % 2:
                        dve.wait_ge(*after_at(u0, j - 1, i, 4))
                        done(u0, j, i, 4)
                        ve.tensor_tensor(hid(k)[:, c0:c1], sg(k)[:, c0:c1], bank(u0, j)[:, c0:c1],
                                         ALU.mult).then_inc(read(u0, j), 1)
                        ahi.wait(1)
                        rest(lo[:, 2 * i + k, c0:c1], hid(k)[:, c0:c1], hi[:, 2 * i + k, c0:c1])
                    if name in plan.ada:
                        ada(name, j, i)
                stream(u0, plan.count[name], 4, evac, [(ahi, 2)])

            def diagonal(dst, value, n):
                ve.tensor_tensor(dst.rearrange("p (t c) -> p t c", t=n), ident.unsqueeze(1).to_broadcast([P, n, P]),
                                 value.unsqueeze(2).to_broadcast([P, n, P]), ALU.mult).then_inc(s_dop, 1)

            def norm1(last):
                mean.wait(1)
                for m in range(0, DT, 2):
                    ve.scalar_tensor_tensor(x1[:, m:m + 2, :], banks[6][:, 0:S].unsqueeze(1).to_broadcast([P, 2, S]),
                                            -1.0 / D, x1[:, m:m + 2, :], ALU.mult, ALU.add).then_inc(s_val, 1)
                nsq.wait(1)
                for m in range(2, DT, 2):
                    nsq.wait(1)
                    chained(ve.tensor_tensor(lg[:, 0:2, :], lg[:, 0:2, :], lg[:, m:m + 2, :], ALU.add))
                ve.tensor_tensor(lg[:, 0, :], lg[:, 0, :], lg[:, 1, :], ALU.add).then_inc(s_dop, 1)
                aval.wait(1)
                chained(ve.reciprocal(tok[:, 1, 0:QT], tok[:, 1, 0:QT]))
                diagonal(rs1, tok[:, 1, 0:QT], QT)
                mean.wait(1)
                for m in range(0, DT, 2):
                    ve.tensor_tensor(lg[:, m:m + 2, :], x1[:, m:m + 2, :],
                                     banks[7][:, 0:S].unsqueeze(1).to_broadcast([P, 2, S]), ALU.mult).then_inc(s_val, 1)
                if last:
                    return
                for m in range(DT):
                    ahi.wait(1)
                    rest(x1lo[:, m, :], x1[:, m, :], x1hi[:, m, :])

            def residual1(u0, first, last=True):
                def evac(j, i):
                    done(u0, j, i, 4)
                    m = 4 * i + j
                    if first:
                        ins = ve.scalar_tensor_tensor(x1[:, m, :], x1[:, m, :], ALPHA, bank(u0, j)[:, 0:S],
                                                      ALU.mult, ALU.add)
                    else:
                        ins = ve.tensor_tensor(x1[:, m, :], x1[:, m, :], bank(u0, j)[:, 0:S], ALU.add)
                    ins.then_inc(read(u0, j), 1)
                    if last and m:
                        dve.wait_ge(*after(u0 + m))
                        if m > 1:
                            step.wait()
                        ins = ve.tensor_tensor(xsum, x1[:, 0, :] if m == 1 else xsum, x1[:, m, :], ALU.add)
                        if m < DT - 1:
                            step.add(ins)
                        else:
                            ins.then_inc(s_dop, 1)
                stream(u0, 8, 4, evac)

            for l in range(L):
                for u in range(U[f"qkv{l}"], U[f"qkv{l}"] + 18):
                    low(u + AHEAD)
                stream(U[f"bbb{l}"], 12, 4, nothing)
                if l == 0:
                    dve.wait_ge(s_const, 6 * 16)
                    aval.wait(1)
                for j in range(24):
                    low(U[f"gate{l}"] + j + AHEAD)
                    if j in range(CONV_AT, CONV_AT + 10, 2):
                        short_conv(l, (j - CONV_AT) // 2)
                    if j == CONV_AT + 11:
                        short_conv(l, 5)
                    if j in SCORES_AT:
                        logits1("a", SCORES_AT.index(j))
                biases1("a", l, 0)
                biases1("a", l, 4)
                for h0 in (0, 4):
                    for hh in range(h0, h0 + 4):
                        logits1("c", hh)
                    biases1("c", l, h0)
                scale1("a")
                scale1("c")
                outputs1(0)
                outputs1(8)
                u0 = U[f"merge{l}"]

                def evac_m(j, i):
                    br, m = j % 3, 4 * i + j // 3
                    done(u0, j, i, 12)
                    ve.tensor_tensor(lg[:, br, :], gates[:, br * DT + m, :], bank(u0, j)[:, 0:S],
                                     ALU.mult).then_inc(read(u0, j), 1)
                    if br == 2:
                        dve.wait_ge(*after_at(u0, j, i, 12))
                        mg = lg[:, 3 + (j // 3) % 2, :]
                        chained(ve.tensor_tensor(lg[:, 0, :], lg[:, 0, :], lg[:, 1, :], ALU.add))
                        ve.tensor_tensor(mg, lg[:, 0, :], lg[:, 2, :], ALU.add).then_inc(s_val, 1)
                        ahi.wait(1)
                        rest(x1lo[:, m, :], mg, x1hi[:, m, :])
                stream(u0, 24, 12, evac_m, [(ahi, 4), (step, 4)])
                residual1(U[f"out{l}"], True)
                norm1(False)
                for c, n in enumerate(CHUNKS):
                    hidden(f"up{l}", c, 0, S, lambda k: lg[:, k, :], lambda k: lg[:, 2 + k, :], y1hi, y1lo)
                    residual1(U[f"down{l}{c}"], c == 0, c == len(CHUNKS) - 1)
                norm1(l == L - 1)
            dve.wait_ge(s_mid, DT)

            def norm2(l, which, c0):
                for m in range(0 if l == which == 0 else DT - 1, DT):
                    add_square(m, c0)
                if which is not None:
                    w = 3 * which
                    dve.wait_ge(s_ada_mod, plan.ada_iterations(DT * (NADA * l + w + 2)))
                    gn = p2(("g_ffn1", "g_mix", "g_ffn2")[which], l, DT)
                    chained(ve.scalar_tensor_tensor(scl[:, which, :, :], mods(l, w + 1), 1.0,
                                                    gn.unsqueeze(2).to_broadcast([P, DT, 2]), ALU.add, ALU.mult))
                aval.wait(1)
                t0 = c0 // P
                chained(ve.reciprocal(tok[:, 1, t0:4], tok[:, 1, t0:4]))
                diagonal(rs2[:, c0:T2], tok[:, 1, t0:4], 4 - t0)
                mean.wait(1)
                rms = banks[4][:, c0:T2]
                if which is None:
                    for m in range(DT):
                        ve.scalar_tensor_tensor(big1[:, m, c0:T2], h[:, m, c0:T2], p2("g_final", 0, DT)[:, m:m + 1],
                                                rms, ALU.mult, ALU.mult).then_inc(s_outv, 1)
                    return
                halves = [(s, slice(s * S, (s + 1) * S)) for s in range(c0 // S, 2)]
                for m in range(DT + 2):
                    if m < DT:
                        for s, cols in halves:
                            ins = ve.scalar_tensor_tensor(big1[:, m, cols], h[:, m, cols], scl[:, which, m, s:s + 1],
                                                          banks[4][:, cols], ALU.mult, ALU.mult)
                        ins.then_inc(s_val, 1)
                    if m >= 2:
                        ahi.wait(1)
                        for s, cols in halves:
                            ins = ve.scalar_tensor_tensor(ulo[:, m - 2, cols], big1[:, m - 2, cols],
                                                          mods(l, 3 * which)[:, m - 2, s:s + 1],
                                                          uhi[:, m - 2, cols].bitcast(F32), ALU.add, ALU.subtract)
                        ins.then_inc(s_split, 1)

            def add_square(m, c0):
                if m:
                    dve.wait_ge(s_dve, step.n)
                nsq.wait(1)
                if m:
                    ins = ve.tensor_tensor(big1[:, 0, c0:T2], big1[:, 0, c0:T2], big1[:, m, c0:T2], ALU.add)
                    if m < DT - 1:
                        step.add(ins)
                    else:
                        ins.then_inc(s_dop, 1)

            def update(u0, c0, gate, c1=None):
                def evac(j, i):
                    done(u0, j, i, 4)
                    m = 4 * i + j
                    for s in range(c0 // S, 2):
                        cols = slice(s * S, (s + 1) * S)
                        ins = ve.scalar_tensor_tensor(h[:, m, cols], bank(u0, j)[:, cols], gate(m, s), h[:, m, cols],
                                                      ALU.mult, ALU.add)
                    ins.then_inc(read(u0, j), 1)
                    if c1 is not None and m:
                        add_square(m - 1, c1)
                stream(u0, 8, 4, evac)

            def ffn2(l, f, c0):
                for c, n in enumerate(CHUNKS):
                    hidden(f"fup{f}{l}", c, c0, T2, lambda k: pp[:, k, :], lambda k: pp[:, 2 + k, :], yhi, ylo)
                    if c == 0:
                        part = {"1": 2, "2": 8}[f]
                        dve.wait_ge(s_ada_mod, plan.ada_iterations(DT * (NADA * l + part + 1)))
                        chained(ve.tensor_scalar(hgt[:, int(f) - 1, :, :], mods(l, part), 0.5, None, ALU.mult))
                    update(U[f"fdown{f}{l}{c}"], c0,
                           lambda m, s: hgt[:, int(f) - 1, :, :].rearrange("p t s -> p (t s)")[:, bass.ds(2 * m + s, 1)],
                           c0 if c == len(CHUNKS) - 1 else None)

            class Convolution:

                def __init__(self, l, c0):
                    self.l, self.c0, self.at, self.last = l, c0, 0, [0] * CT

                def taps(self, n):
                    w, b = p2("w_dw", self.l, TAPS * CT), p2("b_dw", self.l, CT)
                    for _ in range(min(n, TAPS * CT - self.at)):
                        k, m = self.at // CT, self.at % CT
                        a = acc[:, m, self.c0:T2].rearrange("p (s t) -> p s t", t=S)
                        v = vpad[:, m, self.c0 // S:2, k:k + S]
                        wk = w[:, k * CT + m:k * CT + m + 1]
                        dve.wait_ge(s_dve, self.last[m])
                        if k == 0:
                            ins = ve.tensor_scalar(a, v, wk, b[:, m:m + 1], ALU.mult, ALU.add)
                        else:
                            ins = ve.scalar_tensor_tensor(a, v, wk, a, ALU.mult, ALU.add)
                        if k < TAPS - 1:
                            step.add(ins)
                            self.last[m] = step.n
                        else:
                            ins.then_inc(s_conv, 1)
                        self.at += 1

            def attention2(l, s, conv):
                c0 = S if l == L - 1 else 0
                nk = (s + 1) * S
                N = H * QT

                def bias(n):
                    score.wait(1)
                    chained(ve.tensor_reduce(small[:, 0, n:n + 1], score_bank[n % 3][:, 0:nk], AX_X, ALU.max))
                    ve.tensor_scalar(small[:, 1, n:n + 1], small[:, 0, n:n + 1], -QK ** -0.5, None,
                                     ALU.mult).then_inc(s_val, 1)

                def scale(n):
                    aval.wait(1)
                    chained(ve.reciprocal(small[:, 3, n:n + 1], small[:, 2, n:n + 1]))
                    ve.tensor_scalar(pp[:, n % 2, 0:nk], pp[:, n % 2, 0:nk], small[:, 3, n:n + 1], None,
                                     ALU.mult).then_inc(s_prob, 1)
                bias(0)
                bias(1)
                bias(2)
                scale(0)
                for n in range(N + 1):
                    if n + 1 < N:
                        scale(n + 1)
                    if n + 3 < N:
                        bias(n + 3)
                    if n and n % 4 == 0:
                        ahi.wait(1)
                        j = n // 4 - 1
                        rest(ylo[:, j, s * S:(s + 1) * S], banks[j % 2][:, 0:S], yhi[:, j, s * S:(s + 1) * S])
                    if not s:
                        conv.taps(1)
                        continue
                    if n < LN_AT[l]:
                        conv.taps(-(-(TAPS * CT - conv.at) // (LN_AT[l] - n)))
                    if n == LN_AT[l] + 1:
                        dve.wait_ge(s_cmean, l + 1)
                        for m in range(CT):
                            ve.scalar_tensor_tensor(acc[:, m, c0:T2], banks[3][:, c0:T2], -1.0 / (CT * P),
                                                    acc[:, m, c0:T2], ALU.mult, ALU.add).then_inc(s_centred, 1)
                    if n == LN_AT[l] + 5:
                        dve.wait_ge(s_cdev, l + 1)
                        chained(ve.reciprocal(cdev[:, c0:T2], cdev[:, c0:T2]))
                    if n == LN_AT[l] + 6:
                        for m in range(CT):
                            ve.tensor_tensor(acc[:, m, c0:T2], acc[:, m, c0:T2], cdev[:, c0:T2],
                                             ALU.mult).then_inc(s_scaled, 1)
                    if n == LN_AT[l] + 8:
                        dve.wait_ge(s_scaled, CT * (l + 1))
                        for m in range(CT):
                            dve.wait_ge(s_chigh, CT * l + m + 1)
                            ve.tensor_tensor(yclo[m][:, c0:T2], acc[:, m, c0:T2], ychi[:, m, c0:T2].bitcast(F32),
                                             ALU.subtract).then_inc(s_clow, 1)

            for l in range(L):
                last = l == L - 1
                c0 = S if last else 0
                norm2(l, 0, 0)
                ffn2(l, "1", 0)
                norm2(l, 1, 0)
                u0 = U[f"mix{l}"]
                conv = Convolution(l, c0)
                dve.wait_ge(s_used, u0 + 1)
                step.add(ve.memset(vpad[:, :, :, :], 0.0))
                s0 = c0 // S
                for j in range(16):
                    low(u0 + j + AHEAD)
                    if j == 6:
                        dve.wait_ge(*after(u0 + 2))
                        step.add(ve.tensor_tensor(vt[HD:QK, 3, S:T2], vt[HD:QK, 3, S:T2], cos, ALU.mult))
                        chained(ve.tensor_tensor(big1[HD:QK, 2, 0:S], big1[HD:QK, 2, 0:S], sin, ALU.mult))
                        ve.tensor_tensor(vt[HD:QK, 3, S:T2], vt[HD:QK, 3, S:T2], big1[HD:QK, 2, 0:S],
                                         ALU.add).then_inc(s_val, 1)
                    if 9 <= j < 12:
                        m = j - 9
                        dve.wait_ge(*after(u0 + j))
                        step.add(ve.tensor_tensor(
                            vpad[:, m, s0:2, PAD:PAD + S],
                            big2[:, 4 + m, c0:T2].rearrange("p (s t) -> p s t", t=S),
                            acc[:, m, c0:T2].rearrange("p (s t) -> p s t", t=S), ALU.mult))
                        conv.last[m] = step.n
                    if j == 8:
                        aval.wait(1)
                        chained(ve.reciprocal(rs2, rs2))
                        for m in range(KVT):
                            ve.scalar_tensor_tensor(big1[:, m, :], big1[:, m, :], p2("g_kvnorm", l, KVT)[:, m:m + 1],
                                                    rs2, ALU.mult, ALU.mult).then_inc(s_val, 1)
                    if j == 9:
                        aval.wait(1)
                        chained(ve.reciprocal(rs3[:, c0:T2], rs3[:, c0:T2]))
                        for m in range(QLT):
                            ve.scalar_tensor_tensor(vt[:, m, c0:T2], vt[:, m, c0:T2],
                                                    p2("g_qnorm", l, QLT)[:, m:m + 1], rs3[:, c0:T2],
                                                    ALU.mult, ALU.mult).then_inc(s_val, 1)
                    if j == 10:
                        for m in range(KVT):
                            ahi.wait(1)
                            rest(ylo[:, m, :], big1[:, m, :], yhi[:, m, :])
                    if j == 11:
                        for m in range(QLT):
                            ahi.wait(1)
                            t = (2, 3, 8)[m]
                            rest(ylo[:, t, c0:T2], vt[:, m, c0:T2], yhi[:, t, c0:T2])
                    if j >= 12:
                        conv.taps(4 if last else 6)
                for n in range(FG * (2 - c0 // S)):
                    g, s = n % FG, n // FG + c0 // S
                    conv.taps(6 if last else 3)
                    ahi.wait(1)
                    rest(ylo[:, 4 + g, s * S:(s + 1) * S], banks[6 + n % 2][:, 0:S],
                         yhi[:, 4 + g, s * S:(s + 1) * S])
                u0 = U[f"kv{l}"]
                for j in range(8):
                    low(u0 + j + AHEAD)
                    conv.taps(2)
                u0 = U[f"q{l}"]
                bcast = lambda t: t.unsqueeze(1).to_broadcast([ROPE, 2, S])
                for j in range(H):
                    low(u0 + j + AHEAD)
                    if j % 2:
                        dve.wait_ge(*after(u0 + j))
                        qx = big1[HD:QK, j - 1:j + 1, S:T2]
                        sw = swapped[j // 2].rearrange("p (a t) -> p a t", a=2)
                        step.add(ve.tensor_tensor(qx, qx, bcast(cos), ALU.mult))
                        chained(ve.tensor_tensor(sw, sw, bcast(sin), ALU.mult))
                        ve.tensor_tensor(qx, qx, sw, ALU.add).then_inc(s_dop, 1)
                for s in range(c0 // S, 2):
                    attention2(l, s, conv)

                u3 = U[f"bm{l}"]
                by = {0: p2("b_pw", l, DT), 2: p2("b_four", l, DT)}

                def evac_m2(j, i):
                    if j % 2 == 0:
                        return
                    br, m = (j % 6 // 2 + 1) % 3, 2 * i + j // 6
                    dve.wait_ge(*after_at(u3, j - 1, i, 12))
                    done(u3, j, i, 12)
                    bias = by[br][:, bass.ds(m, 1)] if br in by else 0.0
                    t = 3 * (j // 6)
                    ve.scalar_tensor_tensor(big2[:, t + br, c0:T2], bank(u3, j)[:, c0:T2], bias, pp[:, br, c0:T2],
                                            ALU.add, ALU.mult).then_inc(read(u3, j), 1)
                    if j % 6 == 5:
                        dve.wait_ge(*after_at(u3, j, i, 12))
                        chained(ve.tensor_tensor(big2[:, t, c0:T2], big2[:, t, c0:T2], big2[:, t + 1, c0:T2], ALU.add))
                        ve.tensor_tensor(big1[:, m, c0:T2], big2[:, t, c0:T2], big2[:, t + 2, c0:T2],
                                         ALU.add).then_inc(s_val, 1)
                stream(u3, 6 * DT, 12, evac_m2, [(step, 2)])
                for m in range(DT):
                    ahi.wait(1)
                    rest(ulo[:, m, c0:T2], big1[:, m, c0:T2], uhi[:, m, c0:T2])
                update(U[f"bout{l}"], c0,
                       lambda m, s: mod[:, l, :, :].rearrange("p t s -> p (t s)")[:, bass.ds(2 * (5 * DT + m) + s, 1)],
                       c0)
                norm2(l, 2, c0)
                ffn2(l, "2", c0)
            norm2(L - 1, None, S)

        @block.tensor
        def _(pe):
            te = nc.tensor
            split, sq, dop, aop, prob, pt = (Tally(pe, s) for s in (s_split, s_sq, s_dop, s_aop, s_prob, s_pt))

            def two_units(u, hi, lo, c0, c1, late=8):
                n = plan.kt[u]

                def start(v):
                    pe.wait_ge(s_low, v + 1)
                    if plan.freed(v):
                        pe.wait_ge(s_free[v % SLOTS], plan.freed(v))

                def products(v, k):
                    w, s, out_ = slice(k * P, (k + 1) * P), v % SLOTS, banks[v % SLOTS][:, c0:c1]
                    te.matmul(out_, whi[:, s, w], hi(k)[:, c0:c1], start=k == 0, stop=False)
                    te.matmul(out_, whi[:, s, w], lo(k)[:, c0:c1], start=False, stop=False)
                    ins = te.matmul(out_, wlo[:, s, w], hi(k)[:, c0:c1], start=False, stop=k == n - 1)
                    if k == n - 1:
                        ins.then_inc(s_used, 1)

                start(u)
                for k in range(n - late):
                    split.wait(1)
                    products(u, k)
                start(u + 1)
                for k in range(n - late):
                    products(u + 1, k)
                for k in range(max(n - late, 0), n):
                    split.wait(1)
                    products(u, k)
                    products(u + 1, k)

            def by_token(src, t0, t1):
                dop.wait(1)
                for t in range(t0, t1):
                    ins = te.matmul(banks[4 + t][:, 0:1], src[:, t * P:(t + 1) * P], ones[:, 0:1],
                                    start=True, stop=True)
                ins.then_inc(s_stat, 1)

            def spread(bank_, diagonal):
                dop.wait(1)
                te.matmul(bank_, ones, diagonal, start=True, stop=True).then_inc(s_mean, 1)

            def unit(u0, j, i, per, hi, lo, c0, c1):
                u = u0 + j
                pe.wait_ge(s_low, u + 1 + per * i)
                if plan.freed(u):
                    pe.wait_ge(s_free[u % SLOTS], plan.freed(u) + per // SLOTS * i)
                out_ = banks[u % SLOTS][:, c0:c1]
                for k in range(plan.kt[u]):
                    w = slice(k * P, (k + 1) * P)
                    te.matmul(out_, whi[:, u % SLOTS, w], hi(k)[:, c0:c1], start=k == 0, stop=False)
                    te.matmul(out_, whi[:, u % SLOTS, w], lo(k)[:, c0:c1], start=False, stop=False)
                    ins = te.matmul(out_, wlo[:, u % SLOTS, w], hi(k)[:, c0:c1], start=False,
                                    stop=k == plan.kt[u] - 1)
                ins.then_inc(s_used, 1)

            def units_v(u, n, hi, lo, tt):
                for v in range(u, u + n):
                    pe.wait_ge(s_low, v + 1)
                    pe.wait_ge(s_free[v % SLOTS], plan.freed(v))
                s = slice(u % SLOTS, u % SLOTS + n)
                assert s.stop <= SLOTS
                for t in range(tt):
                    at = t * n * P
                    out_ = banks[(u + at // 512) % SLOTS][:, at % 512:at % 512 + n * P]
                    rows_ = slice(t * P, (t + 1) * P)
                    for k in range(plan.kt[u]):
                        w = slice(k * P, (k + 1) * P)
                        te.matmul(out_, hi(k)[:, rows_], whi[:, s, w], start=k == 0, stop=False)
                        te.matmul(out_, lo(k)[:, rows_], whi[:, s, w], start=False, stop=False)
                        ins = te.matmul(out_, hi(k)[:, rows_], wlo[:, s, w], start=False,
                                        stop=k == plan.kt[u] - 1)
                ins.then_inc(s_used, n)

            def stream(u0, n, per, hi, lo, c0, c1, ready=False, late=8):
                iters = n // per
                first = 0
                if ready:
                    two_units(u0, lambda k: hi(0, k), lambda k: lo(0, k), c0, c1, late)
                    for j in range(2, per):
                        unit(u0, j, 0, 0, lambda k: hi(j, k), lambda k: lo(j, k), c0, c1)
                    first = 1

                def body(i):
                    for j in range(per):
                        unit(u0 + first * per, j, i, per, lambda k: hi(j, k), lambda k: lo(j, k), c0, c1)
                repeat(pe, iters - first, body, [])

            tile = lambda t: (lambda j, k: t[:, k, :])

            x1h, x1l = tile(x1hi), tile(x1lo)

            def scores1(kind, heads, before):
                for hh in heads:
                    if before + hh >= 2:
                        pe.wait_ge(s_sread, before + hh - 1)
                    g, j = (hh // 4, hh % 4) if kind == "a" else (hh % 2, hh // 2)
                    q, k = (qa, ka[:, :]) if kind == "a" else (qc, kc[:, hh // 2, :])
                    r = slice(HD * g, HD * g + HD)
                    for qt in range(QT):
                        ins = te.matmul(banks[4 + hh % 2][:, qt * S:(qt + 1) * S], q[r, j, qt * P:(qt + 1) * P],
                                        k[r, :], start=True, stop=True)
                    ins.then_inc(s_score, 1)

            def outputs1(kind, v):
                lo = logits[kind]

                def turn_(hh):
                    prob.wait(1)
                    b = banks[6 + hh % 2]
                    te.transpose(b[:, 0:P], lo[:, 2 * hh, 0:P], ident)
                    te.transpose(b[:, P:S], lo[:, 2 * hh + 1, 0:P], ident)
                    te.transpose(b[:, S + P:2 * S], lo[:, 2 * hh + 1, P:S], ident).then_inc(s_turned, 1)

                def outputs(hh):
                    pt.wait(1)
                    if kind == "c" and hh % 2 == 0:
                        split.wait(1)
                    c = hh // 4 if kind == "a" else hh
                    r = slice(HD * (hh % 2), HD * (hh % 2) + HD)
                    b = banks[hh // 2]
                    te.matmul(b[r, 0:S], v[:, 0, c * HD:(c + 1) * HD], pt1[:, hh % 2, 0:S], start=True, stop=False)
                    ins = te.matmul(b[r, P:S], v[:, 1, c * HD:(c + 1) * HD], pt1[:, hh % 2, S + P:2 * S],
                                    start=False, stop=True)
                    if hh % 2:
                        ins.then_inc(s_head, 1)

                for hh in range(H + 1):
                    if hh < H:
                        turn_(hh)
                    if hh:
                        outputs(hh - 1)

            def norm1():
                spread(banks[6][:, 0:S], xsum)
                by_token(lg[:, 0, :], 0, QT)
                spread(banks[7][:, 0:S], rs1)

            for l in range(L):
                u0 = U[f"qkv{l}"]
                hi_, lo_ = (lambda k: x1hi[:, k, :]), (lambda k: x1lo[:, k, :])
                two_units(u0, hi_, lo_, 0, S)
                for j in range(2, 18):
                    if j == 5:
                        units_v(u0 + j, 1, hi_, lo_, QT)
                    elif j >= 14:
                        if j % 2 == 0:
                            units_v(u0 + j, 2, hi_, lo_, QT)
                    else:
                        unit(u0, j, 0, 0, hi_, lo_, 0, S)
                stream(U[f"bbb{l}"], 12, 4, x1h, x1l, 0, S)
                for j in range(24):
                    unit(U[f"gate{l}"], j, 0, 0, hi_, lo_, 0, S)
                    if j + 1 in SCORES_AT:
                        pe.wait_ge(*after(U[f"qkv{l}"] + 17))
                        scores1("a", [SCORES_AT.index(j + 1)], 2 * H * l)
                pe.wait_ge(*after(U[f"gate{l}"] + 23))
                pe.wait_ge(s_const, 6 * 16)
                scores1("c", range(H), 2 * H * l + H)
                split.wait(1)
                outputs1("a", va)
                outputs1("c", vc)
                split.wait(4)
                stream(U[f"merge{l}"], 24, 12, lambda j, k: y1hi[:, 4 * (j % 3) + k, :],
                       lambda j, k: y1lo[:, 4 * (j % 3) + k, :], 0, S)
                stream(U[f"out{l}"], 8, 4, x1h, x1l, 0, S, ready=True, late=1)
                norm1()
                for c, n in enumerate(CHUNKS):
                    stream(U[f"up{l}{c}"], 2 * n, 4, x1h, x1l, 0, S, ready=c == 0)
                    stream(U[f"down{l}{c}"], 8, 4, tile(y1hi), tile(y1lo), 0, S, ready=True, late=1)
                norm1()

            u2h, u2l = tile(uhi), tile(ulo)

            def add_up(bank_, n, c0, src):
                for m in range(n):
                    sq.wait(1)
                    ins = te.matmul(bank_[:, c0:T2], ones, src(m)[:, c0:T2], start=m == 0, stop=m == n - 1)
                ins.then_inc(s_stat, 1)

            def ffn2(l, f, c0):
                for c, n in enumerate(CHUNKS):
                    stream(U[f"fup{f}{l}{c}"], 2 * n, 4, u2h, u2l, c0, T2, ready=c == 0)
                    stream(U[f"fdown{f}{l}{c}"], 8, 4, tile(yhi), tile(ylo), c0, T2, ready=True, late=1)

            def attention2(l, s):
                c0 = S if l == L - 1 else 0
                nk = (s + 1) * S
                N = H * QT

                def scores(n):
                    hh, qt = n // QT, n % QT
                    q0 = s * S + qt * P
                    if s and n % (2 * QT) == 0:
                        dop.wait(1)
                    te.matmul(score_bank[n % 3][:, 0:nk], big1[0:QK, hh, q0:q0 + P], big2[0:QK, hh, 0:nk],
                              start=True, stop=True).then_inc(s_score, 1)

                def turn_(n):
                    prob.wait(1)
                    for k in range(nk // P):
                        ins = te.transpose(banks[6 + n % 2][:, k * P:(k + 1) * P], pp[:, n % 2, k * P:(k + 1) * P], ident)
                    ins.then_inc(s_turned, 1)

                def outputs(n):
                    pt.wait(1)
                    hh, qt = n // QT, n % QT
                    if n % 4 == 0 and n >= 8:
                        split.wait(1)
                    r = slice(HD * (hh % 2), HD * (hh % 2) + HD)
                    for k in range(nk // P):
                        ins = te.matmul(banks[hh // 2 % 2][r, qt * P:(qt + 1) * P], vt[:, k, hh * HD:(hh + 1) * HD],
                                        pp[:, 2 + n % 2, k * P:(k + 1) * P], start=k == 0, stop=k == nk // P - 1)
                    if n % 4 == 3:
                        ins.then_inc(s_head, 1)
                for n in range(3):
                    scores(n)
                for n in range(N + 1):
                    if n < N:
                        turn_(n)
                    if n:
                        outputs(n - 1)
                    if n + 3 < N:
                        scores(n + 3)
                    if s and n == LN_AT[l]:
                        for m in range(CT):
                            pe.wait_ge(s_conv, CT * l + m + 1)
                            ins = te.matmul(banks[3][:, c0:T2], ones, acc[:, m, c0:T2], start=m == 0, stop=m == CT - 1)
                        ins.then_inc(s_cmean, 1)
                    if s and n == LN_AT[l] + 3:
                        for m in range(CT):
                            pe.wait_ge(s_csq, CT * l + m + 1)
                            ins = te.matmul(banks[3][:, c0:T2], ones, csquares[:, m, c0:T2],
                                            start=m == 0, stop=m == CT - 1)
                        ins.then_inc(s_cvar, 1)
                split.wait(2)

            def norm2(c0):
                by_token(big1[:, 0, :], c0 // P, T2 // P)
                spread(banks[4][:, c0:T2], rs2[:, c0:T2])

            for l in range(L):
                last = l == L - 1
                c0 = S if last else 0
                norm2(0)
                ffn2(l, "1", 0)
                norm2(0)
                u0 = U[f"mix{l}"]
                two_units(u0, lambda k: uhi[:, k, :], lambda k: ulo[:, k, :], 0, T2)
                for j in range(2, 16):
                    unit(u0, j, 0, 0, lambda k: uhi[:, k, :], lambda k: ulo[:, k, :], 0 if j < 3 else c0, T2)
                    if j == 7:
                        add_up(banks[4], KVT, 0, lambda m: big1[:, 4 + m, :])
                        add_up(banks[5], QLT, c0, lambda m: big1[:, (3, 6, 7)[m], :])
                pe.wait_ge(s_dft, 16 * (l + 1))
                split.wait(KVT + QLT)
                pe.wait_ge(*after(u0 + 15))
                N = FG * (2 - c0 // S)
                for n in range(N + 1):
                    if n < N:
                        g, s = n % FG, n // FG + c0 // S
                        for t in range(QT):
                            q0 = s * S + t * P
                            ins = te.matmul(banks[4 + n % 2][:, t * S:(t + 1) * S], big2[:, g, q0:q0 + P],
                                            dft[:, 0:2 * P], start=True, stop=True)
                        ins.then_inc(s_stat, 1)
                    if n:
                        aop.wait(1)
                        if n > 2:
                            split.wait(1)
                        b = (n - 1) % 2
                        for t in range(QT):
                            for part in range(2):
                                at = 2 * P + (2 * t + part) * S
                                ins = te.matmul(banks[6 + b][:, 0:S],
                                                big1[:, 2 + b, t * S + part * P:t * S + (part + 1) * P],
                                                dft[:, at:at + S], start=t + part == 0, stop=t + part == 2)
                        ins.then_inc(s_head, 1)
                split.wait(2)
                u0 = U[f"kv{l}"]
                kvh, kvl = (lambda k: yhi[:, k, :]), (lambda k: ylo[:, k, :])
                for j in range(8):
                    if j < 4:
                        unit(u0, j, 0, 0, kvh, kvl, 0, T2)
                    elif j % 2 == 0:
                        units_v(u0 + j, 2, kvh, kvl, 4)
                u0 = U[f"q{l}"]
                qt_ = [2, 3, 8]
                for j in range(H):
                    unit(u0, j, 0, 0, lambda k: yhi[:, qt_[k], :], lambda k: ylo[:, qt_[k], :], c0, T2)
                pe.wait_ge(*after(u0 + H - 1))
                aop.wait(1)
                for s in range(c0 // S, 2):
                    attention2(l, s)
                rows_of = {1: (yhi, ylo, 0), 3: (yhi, ylo, 4)}

                def rows(part):
                    def at(j, k):
                        if j % 6 == 5:
                            if part == 0 and k == 0:
                                pe.wait_ge(s_clow, CT * (l + 1))
                            return (ychi[:, k, :], yclo[k])[part]
                        *t, first = rows_of.get(j % 6, (uhi, ulo, 0))
                        return t[part][:, first + k, :]
                    return at
                stream(U[f"bm{l}"], 6 * DT, 12, rows(0), rows(1), c0, T2)
                stream(U[f"bout{l}"], 8, 4, u2h, u2l, c0, T2, ready=True)
                norm2(c0)
                ffn2(l, "2", c0)
            norm2(S)


def tiles(w, cols=P):
    k, n = w.shape
    return np.ascontiguousarray(w.reshape(k // P, P, n // cols, cols).transpose(2, 1, 0, 3)).reshape(n // cols, -1)


def by_feature(v):
    return np.moveaxis(v.reshape(v.shape[:-1] + (v.shape[-1] // P, P)), -1, 0).reshape(P, -1)


SWAP = np.arange(ROPE) ^ (ROPE // 4)


def weight_stream(a):
    out = []
    for l in range(L):
        w = a["w_in"][l]
        q = w[:, 0:512].reshape(D, 2, 4, HD).transpose(0, 2, 1, 3).reshape(D, 512)
        out += [tiles(q), tiles(w[:, 512:768]), tiles(w[:, 2304:3840]), tiles(w[:, 768:2304]), tiles(w[:, 3840:])]
        br = [tiles(a[f"w_branch_{x}"][l]) for x in "abc"]
        out += [b[m] for m in range(DT) for b in br]
        out.append(tiles(a["w_out"][l]))
        out += swiglu_units(a["w_ffn_gate"][l], a["w_ffn_up"][l], a["w_ffn_down"][l])
    for l in range(L):
        for f in "12":
            if f == "2":
                w = a["w_in_2"][l]
                kr = w[:, 1408:1440]
                out += [tiles(w[:, 1152:1408]), tiles(np.concatenate([kr, kr, kr, kr[:, SWAP]], 1)),
                        tiles(w[:, 768:1152]), tiles(w[:, 0:768]), tiles(w[:, 1440:1952])]
                kv = a["w_ukv_2"][l].reshape(-1, H, 2, HD)
                out += [tiles(kv[:, :, 0].reshape(-1, H * HD)), tiles(kv[:, :, 1].reshape(-1, H * HD))]
                q = a["w_uq_2"][l].reshape(-1, H, QK)
                out.append(tiles(np.concatenate([q, q[:, :, HD + SWAP]], 2).reshape(-1, H * P)))
                g = tiles(a["w_bgate_2"][l])
                br = [tiles(a[x][l]) for x in ("w_pw_conv_2", "w_o_mla_2", "w_fourier_2")]
                out += [y for m in range(DT) for b in (1, 2, 0) for y in (g[b * DT + m], br[b][m])]
                out.append(tiles(a["w_out_2"][l]))
            out += swiglu_units(a[f"w1_ffn{f}_2"][l], a[f"w3_ffn{f}_2"][l], a[f"w2_ffn{f}_2"][l])
    return np.concatenate([np.ascontiguousarray(o).reshape(-1) for o in out])


def swiglu_units(gate, up, down):
    own = np.stack([tiles(gate), tiles(up)], 1).reshape(2 * FT, -1)
    out, t = [], 0
    for n in CHUNKS:
        out += [own[2 * t:2 * (t + n)], tiles(down[t * P:(t + n) * P])]
        t += n
    return out


def constants():
    c0 = np.zeros((P, NCST0), np.float32)
    c0[:, 0:P] = np.eye(P)
    c0[:, P:2 * P] = 1.0
    c0[:, 2 * P], c0[:, 2 * P + 1] = LN_EPS, EPS
    q = (np.arange(QT)[None, :, None] * P + np.arange(P)[:, None, None])
    d = (q - np.arange(S)[None, None, :]).astype(np.float64)
    far = 1e30
    da = np.where((d >= 0) & (d < 128), d, far).reshape(P, -1)
    dc = np.where(d >= 0, d, far).reshape(P, -1)
    c1 = np.concatenate([da, dc], 1).astype(np.float32)
    ax = ROPE // 2
    t = np.arange(S)
    inv = 1.0 / (10000.0 ** (np.arange(ax // 2) * 2.0 / ax))
    ar, ac = (t // 64)[:, None] * inv, (t % 64)[:, None] * inv
    ang = np.concatenate([ar, ar, ac, ac], 1).T
    sign = np.where(np.arange(ROPE) % ax < ax // 2, -1.0, 1.0)[:, None]
    c2 = np.zeros((P, NCST2), np.float32)
    c2[HD:QK, :] = np.concatenate([np.cos(ang), np.sin(ang) * sign], 1)
    a = 2 * np.pi * np.outer(np.arange(P), np.arange(P)) / P
    b = 2 * np.pi * np.outer(np.arange(S), np.arange(S)) / S
    tok = np.stack([np.cos(b), -np.sin(b)], 1) / np.sqrt(S)
    tok = tok.reshape(QT, P, 2, S).transpose(1, 0, 2, 3).reshape(P, -1)
    dft = np.concatenate([np.cos(a) / np.sqrt(P), np.sin(a) / np.sqrt(P), tok], 1)
    return c0, c1, c2, dft.astype(np.float32)


def layouts(a):
    def tokens(x):
        return np.ascontiguousarray(x.reshape(S, DT, P).transpose(2, 1, 0)).reshape(P, -1)

    c = np.broadcast_to(np.concatenate([a["c_ctx_2"].reshape(-1), a["c_2"].reshape(-1)]), (P, 2 * D))
    sinks = np.broadcast_to(a["attn_sinks"].reshape(1, L, H, 1), (P, L, H, QT)).reshape(P, -1)
    par1 = np.concatenate([by_feature(a[n]) for n in ("ln1_g", "ln1_b", "ln2_g", "ln2_b", "conv_w")] +
                          [sinks], 1)
    par2 = np.concatenate([by_feature(a[n + "_2"]) for n in
                           ("g_ffn1", "g_mix", "g_ffn2", "w_dw", "b_dw", "ln_g_conv", "ln_b_conv", "b_pw_conv",
                            "g_qnorm", "g_kvnorm", "b_fourier", "b_bgate", "g_final", "b_ada")], 1)
    c0, c1, c2, dft = constants()
    return {"xT": tokens(a["x"]), "ctxT": tokens(a["ctx_2"]), "w_stream": weight_stream(a),
            "w_ada": a["w_ada_2"].transpose(0, 2, 1).reshape(-1), "c": c, "par1": par1,
            "par2": par2, "cst0": c0, "cst1": c1, "cst2": c2, "dft": dft}


def kernel(**inputs):
    import numpy as _np
    import concourse.bacc as _bacc
    from concourse import mybir as _mybir
    from concourse.bass_utils import run_bass_kernel_spmd as _run

    arrays = {k: _np.ascontiguousarray(v) for k, v in layouts({k: _np.asarray(v) for k, v in inputs.items()}).items()}
    nc = _bacc.Bacc("TRN2", target_bir_lowering=False, num_devices=1)
    args = [nc.dram_tensor(f"in_{n}", v.shape, _mybir.dt.from_np(v.dtype), kind="ExternalInput").ap()
            for n, v in arrays.items()]
    args.append(nc.dram_tensor("outT", (P, DT * S), _mybir.dt.float32, kind="ExternalOutput").ap())
    program(nc, *args)
    r = _run(nc, [{f"in_{n}": v for n, v in arrays.items()}], core_ids=[0])
    got = r.results[0]["outT"]
    return _np.ascontiguousarray(got.reshape(P, DT, S).transpose(2, 1, 0)).reshape(1, S, D)
```
